# Optimizing a Trainium2 kernel written in Bass

```python
import math
import jax, jax.numpy as jnp
from jax import lax
import numpy as np

D_MODEL = 1024
BATCH = 1
SEQ = 256
DEPTH = 1

GDN_HEADS = 8
GDN_DK = 64
GDN_DV = 64
GDN_CONV = 4
GDN_CHUNK = 64
NSA_HEADS = 8
NSA_KV_GROUPS = 2
NSA_HPG = NSA_HEADS // NSA_KV_GROUPS
NSA_DH = 64
NSA_BRANCHES = 3
CMP_BLOCK = 32
CMP_STRIDE = 16
SEL_BLOCK = 64
N_SELECT = 16
WINDOW = 512
NSA_QBLOCK = 64
FORCE_BONUS = 1e4
REL_BUCKETS = 32
REL_MAX_DIST = 128
PEER_HEADS = 8
PEER_NKEYS = 128
PEER_N_EXPERTS = PEER_NKEYS * PEER_NKEYS
PEER_TOPK = 16
PEER_DQ = 256
PEER_DQH = PEER_DQ // 2
PEER_TOKBLOCK = 128
GDN_QKV_W = 2 * GDN_HEADS * GDN_DK + GDN_HEADS * GDN_DV
GDN_Z_W = GDN_HEADS * GDN_DV
GDN_BETA_W = GDN_HEADS
GDN_DECAY_W = GDN_HEADS
NSA_Q_W = NSA_HEADS * NSA_DH
NSA_KV_W = NSA_BRANCHES * 2 * NSA_KV_GROUPS * NSA_DH
NSA_GATE_W = NSA_HEADS * NSA_BRANCHES
MERGE_W = 2 * D_MODEL
N_IN = GDN_QKV_W + GDN_Z_W + GDN_BETA_W + GDN_DECAY_W + NSA_Q_W + NSA_KV_W + NSA_GATE_W + MERGE_W
RMS_EPS = 1e-6
NEG = -1e30

kernel_name = 'hybrid_gdn_nsa_peer_block'

def rms_norm(x, w):
    xf = x.astype(jnp.float32)
    y = xf * lax.rsqrt(jnp.mean(xf * xf, axis=-1, keepdims=True) + RMS_EPS)
    return (y * w.astype(jnp.float32)).astype(x.dtype)

def l2_normalize(x):
    xf = x.astype(jnp.float32)
    return xf * lax.rsqrt(jnp.sum(xf * xf, axis=-1, keepdims=True) + 1e-6)

def t5_bucket(dist):
    dist = jnp.maximum(dist, 0)
    max_exact = REL_BUCKETS // 2
    d = jnp.maximum(dist, 1).astype(jnp.float32)
    large = max_exact + (jnp.log(d / max_exact) / math.log(REL_MAX_DIST / max_exact)
                         * (REL_BUCKETS - max_exact)).astype(jnp.int32)
    large = jnp.minimum(large, REL_BUCKETS - 1)
    return jnp.where(dist < max_exact, dist, large)

def masked_softmax(s, mask):
    s = jnp.where(mask, s.astype(jnp.float32), NEG)
    p = jax.nn.softmax(s, axis=-1)
    return jnp.where(mask, p, 0.0)

def causal_depthwise_conv(x, w):
    k = w.shape[0]
    return lax.conv_general_dilated(x, w[:, None, :].astype(x.dtype), (1,), ((k - 1, 0),),
                                    dimension_numbers=('NWC', 'WIO', 'NWC'),
                                    feature_group_count=x.shape[-1])

def gated_delta_rule_chunked(q, k, v, g, beta):
    b, h, s, dk = q.shape
    dv = v.shape[-1]
    c = GDN_CHUNK
    n = s // c
    q = (q * dk ** -0.5).reshape(b, h, n, c, dk)
    k = k.reshape(b, h, n, c, dk)
    v = v.reshape(b, h, n, c, dv)
    beta = beta.reshape(b, h, n, c)
    g = jnp.cumsum(g.reshape(b, h, n, c), axis=-1)
    lower = jnp.tril(jnp.ones((c, c), bool))
    strict = jnp.tril(jnp.ones((c, c), bool), -1)
    decay = jnp.where(lower, jnp.exp(jnp.where(lower, g[..., :, None] - g[..., None, :], 0.0)), 0.0)
    k_beta = k * beta[..., None]
    a_mat = jnp.where(strict, jnp.einsum('bhnid,bhnjd->bhnij', k_beta, k) * decay, 0.0)
    tri = a_mat + jnp.eye(c, dtype=a_mat.dtype)
    u = lax.linalg.triangular_solve(tri, v * beta[..., None], left_side=True, lower=True, unit_diagonal=True)
    w = lax.linalg.triangular_solve(tri, k_beta * jnp.exp(g)[..., None], left_side=True, lower=True,
                                    unit_diagonal=True)
    attn = jnp.einsum('bhnid,bhnjd->bhnij', q, k) * decay
    q_dec = q * jnp.exp(g)[..., None]
    k_dec = k * jnp.exp(g[..., -1:] - g)[..., None]
    g_last = jnp.exp(g[..., -1])

    def step(state, inp):
        u_i, w_i, q_i, a_i, k_i, gl_i = inp
        v_new = u_i - jnp.einsum('bhcd,bhde->bhce', w_i, state)
        o_i = jnp.einsum('bhcd,bhde->bhce', q_i, state) + jnp.einsum('bhij,bhje->bhie', a_i, v_new)
        state = state * gl_i[..., None, None] + jnp.einsum('bhcd,bhce->bhde', k_i, v_new)
        return state, o_i

    xs = (jnp.moveaxis(u, 2, 0), jnp.moveaxis(w, 2, 0), jnp.moveaxis(q_dec, 2, 0),
          jnp.moveaxis(attn, 2, 0), jnp.moveaxis(k_dec, 2, 0), jnp.moveaxis(g_last, 2, 0))
    state0 = jnp.zeros((b, h, dk, dv), jnp.float32)
    _, o = lax.scan(step, state0, xs)
    return jnp.moveaxis(o, 0, 2).reshape(b, h, s, dv)

def nsa_attention(q, kv, gates, cmp_pe_k, cmp_pe_v, cmp_w_k, cmp_w_v, rel_bias):
    b, s = q.shape[0], q.shape[1]
    G, HPG, DH, QB = NSA_KV_GROUPS, NSA_HPG, NSA_DH, NSA_QBLOCK
    scale = DH ** -0.5
    k_c, v_c = kv[:, :, 0, 0], kv[:, :, 0, 1]
    k_s, v_s = kv[:, :, 1, 0], kv[:, :, 1, 1]
    k_w, v_w = kv[:, :, 2, 0], kv[:, :, 2, 1]
    n_cmp = (s - CMP_BLOCK) // CMP_STRIDE + 1
    blk_idx = jnp.arange(n_cmp)[:, None] * CMP_STRIDE + jnp.arange(CMP_BLOCK)[None, :]
    k_cmp = jnp.einsum('bnlgd,lde->bnge', k_c[:, blk_idx] + cmp_pe_k[:, None, :], cmp_w_k)
    v_cmp = jnp.einsum('bnlgd,lde->bnge', v_c[:, blk_idx] + cmp_pe_v[:, None, :], cmp_w_v)
    cmp_start = jnp.arange(n_cmp) * CMP_STRIDE
    cmp_end = cmp_start + CMP_BLOCK - 1
    n_sel = s // SEL_BLOCK
    top_n = min(N_SELECT, n_sel)
    sel_start = jnp.arange(n_sel) * SEL_BLOCK
    overlap = jnp.clip(jnp.minimum(cmp_end[:, None] + 1, sel_start[None, :] + SEL_BLOCK)
                       - jnp.maximum(cmp_start[:, None], sel_start[None, :]), 0, None).astype(jnp.float32) / CMP_BLOCK
    k_s_g = k_s.transpose(0, 2, 1, 3)
    v_s_g = v_s.transpose(0, 2, 1, 3)
    pad = ((0, 0), (WINDOW, 0), (0, 0), (0, 0))
    k_w_pad = jnp.pad(k_w, pad)
    v_w_pad = jnp.pad(v_w, pad)
    tbl_g = rel_bias.reshape(REL_BUCKETS, G, HPG).transpose(1, 0, 2)
    b_ix = jnp.arange(b)[:, None, None, None, None]
    g_ix = jnp.arange(G)[None, :, None, None, None]

    def head_bias(dist):
        bb = rel_bias[t5_bucket(dist)]
        return bb.reshape(dist.shape + (G, HPG)).transpose(2, 3, 0, 1)

    def block(args):
        qi, q_blk, g_blk = args
        t = qi * QB + jnp.arange(QB)
        s_c = jnp.einsum('bqghd,bngd->bghqn', q_blk, k_cmp) * scale + head_bias(t[:, None] - cmp_end[None, :])
        p_c = masked_softmax(s_c, cmp_end[None, :] <= t[:, None])
        o_c = jnp.einsum('bghqn,bngd->bqghd', p_c.astype(v_cmp.dtype), v_cmp)
        imp = jnp.einsum('bghqn,nm->bgqm', p_c, overlap)
        blk = jnp.arange(n_sel)[None, :]
        cur = (t // SEL_BLOCK)[:, None]
        valid_blk = sel_start[None, :] <= t[:, None]
        forced = (blk == 0) | (blk == cur) | (blk == cur - 1)
        imp = jnp.where(valid_blk, imp + jnp.where(forced, FORCE_BONUS, 0.0), -1.0)
        top_val, top_idx = lax.top_k(imp, top_n)
        pos = top_idx[..., None] * SEL_BLOCK + jnp.arange(SEL_BLOCK)
        m_s = ((top_val >= 0.0)[..., None] & (pos <= t[None, None, :, None, None])).reshape(b, G, QB, -1)
        k_sel = k_s_g[b_ix, g_ix, pos].reshape(b, G, QB, -1, DH)
        v_sel = v_s_g[b_ix, g_ix, pos].reshape(b, G, QB, -1, DH)
        pos = pos.reshape(b, G, QB, -1)
        bias_s = tbl_g[g_ix[..., 0], t5_bucket(t[None, None, :, None] - pos)]
        s_s = jnp.einsum('bqghd,bgqld->bghql', q_blk, k_sel) * scale + bias_s.transpose(0, 1, 4, 2, 3)
        p_s = masked_softmax(s_s, m_s[:, :, None])
        o_s = jnp.einsum('bghql,bgqld->bqghd', p_s.astype(v_sel.dtype), v_sel)
        start = qi * QB
        k_win = lax.dynamic_slice_in_dim(k_w_pad, start, WINDOW + QB, axis=1)
        v_win = lax.dynamic_slice_in_dim(v_w_pad, start, WINDOW + QB, axis=1)
        kpos = start - WINDOW + jnp.arange(WINDOW + QB)
        dist = t[:, None] - kpos[None, :]
        m_w = (kpos[None, :] >= 0) & (dist >= 0) & (dist < WINDOW)
        s_w = jnp.einsum('bqghd,bkgd->bghqk', q_blk, k_win) * scale + head_bias(dist)
        p_w = masked_softmax(s_w, m_w)
        o_w = jnp.einsum('bghqk,bkgd->bqghd', p_w.astype(v_win.dtype), v_win)
        gate = jax.nn.sigmoid(g_blk.astype(jnp.float32))
        return gate[..., 0:1] * o_c + gate[..., 1:2] * o_s + gate[..., 2:3] * o_w

    nq = s // QB
    q_blocks = q.reshape(b, nq, QB, G, HPG, DH).swapaxes(0, 1)
    g_blocks = gates.reshape(b, nq, QB, G, HPG, NSA_BRANCHES).swapaxes(0, 1)
    out = lax.map(block, (jnp.arange(nq, dtype=jnp.int32), q_blocks, g_blocks))
    return out.swapaxes(0, 1).reshape(b, s, NSA_HEADS * DH).astype(q.dtype)

def peer_ffn(h, w_query, sub_keys, expert_u, expert_v):
    b, s, d = h.shape
    tok = h.reshape(-1, PEER_TOKBLOCK, d)
    kk = PEER_TOPK

    def block(h_blk):
        tb = h_blk.shape[0]
        qry = (h_blk @ w_query).reshape(tb, PEER_HEADS, 2, PEER_DQH)
        sc = jnp.einsum('thpd,hpkd->thpk', qry, sub_keys).astype(jnp.float32)
        s1, i1 = lax.top_k(sc[:, :, 0], kk)
        s2, i2 = lax.top_k(sc[:, :, 1], kk)
        cand = (s1[..., :, None] + s2[..., None, :]).reshape(tb, PEER_HEADS, kk * kk)
        cidx = (i1[..., :, None] * PEER_NKEYS + i2[..., None, :]).reshape(tb, PEER_HEADS, kk * kk)
        top, sel = lax.top_k(cand, kk)
        eidx = jnp.take_along_axis(cidx, sel, axis=-1)
        gate = jax.nn.softmax(top, axis=-1)
        u = expert_u[eidx]
        v = expert_v[eidx]
        act = jax.nn.gelu(jnp.einsum('td,thkd->thk', h_blk, u).astype(jnp.float32))
        return jnp.einsum('thk,thkd->td', (gate * act).astype(v.dtype), v)

    out = lax.map(block, tok)
    return out.reshape(b, s, d).astype(h.dtype)

def _split_points():
    widths = (GDN_QKV_W, GDN_Z_W, GDN_BETA_W, GDN_DECAY_W, NSA_Q_W, NSA_KV_W, NSA_GATE_W)
    pts = []
    acc = 0
    for wd in widths:
        acc += wd
        pts.append(acc)
    return pts

def hybrid_layer(x, rel_bias, norm_mix, w_in, conv_w, a_log, dt_bias, gdn_norm, cmp_pe_k, cmp_pe_v,
                 cmp_w_k, cmp_w_v, w_branch_a, w_branch_b, w_out, norm_ffn, w_query, sub_keys,
                 expert_u, expert_v):
    b, s, _ = x.shape
    h = rms_norm(x, norm_mix)
    proj = h @ w_in
    qkv, z, beta_in, a_in, q_n, kv_n, gate_n, merge = jnp.split(proj, _split_points(), axis=-1)
    qkv = jax.nn.silu(causal_depthwise_conv(qkv, conv_w))
    qa, ka, va = jnp.split(qkv, [GDN_HEADS * GDN_DK, 2 * GDN_HEADS * GDN_DK], axis=-1)
    qa = l2_normalize(qa.reshape(b, s, GDN_HEADS, GDN_DK).transpose(0, 2, 1, 3))
    ka = l2_normalize(ka.reshape(b, s, GDN_HEADS, GDN_DK).transpose(0, 2, 1, 3))
    va = va.reshape(b, s, GDN_HEADS, GDN_DV).transpose(0, 2, 1, 3).astype(jnp.float32)
    beta = jax.nn.sigmoid(beta_in.astype(jnp.float32)).transpose(0, 2, 1)
    g = (-jnp.exp(a_log.astype(jnp.float32))
         * jax.nn.softplus(a_in.astype(jnp.float32) + dt_bias.astype(jnp.float32))).transpose(0, 2, 1)
    oa = gated_delta_rule_chunked(qa, ka, va, g, beta).transpose(0, 2, 1, 3)
    oa = rms_norm(oa, gdn_norm) * jax.nn.silu(z.reshape(b, s, GDN_HEADS, GDN_DV).astype(jnp.float32))
    ya = oa.reshape(b, s, -1).astype(x.dtype) @ w_branch_a
    qb = q_n.reshape(b, s, NSA_KV_GROUPS, NSA_HPG, NSA_DH)
    kvb = kv_n.reshape(b, s, NSA_BRANCHES, 2, NSA_KV_GROUPS, NSA_DH)
    gb = gate_n.reshape(b, s, NSA_KV_GROUPS, NSA_HPG, NSA_BRANCHES)
    ob = nsa_attention(qb, kvb, gb, cmp_pe_k, cmp_pe_v, cmp_w_k, cmp_w_v, rel_bias)
    yb = ob @ w_branch_b
    gate_a, gate_b = jnp.split(merge, 2, axis=-1)
    mixed = (jax.nn.sigmoid(gate_a) * ya + jax.nn.sigmoid(gate_b) * yb).astype(x.dtype)
    x = x + mixed @ w_out
    x = x + peer_ffn(rms_norm(x, norm_ffn), w_query, sub_keys, expert_u, expert_v)
    return x

def setup_inputs(seed: int = 0) -> dict:
    key = jax.random.key(seed)
    ks = jax.random.split(key, 24)
    f32 = jnp.float32

    def nrm(k, shape, sc):
        return jax.random.normal(k, shape, f32) * sc

    L = DEPTH
    dt = jnp.exp(jax.random.uniform(ks[5], (L, GDN_HEADS), f32, math.log(1e-3), math.log(1e-1)))
    return {
        'x': nrm(ks[0], (BATCH, SEQ, D_MODEL), 1.0),
        'rel_bias': nrm(ks[1], (REL_BUCKETS, NSA_HEADS), 0.5),
        'norm_final': 1.0 + nrm(ks[2], (D_MODEL,), 0.1),
        'norm_mix': 1.0 + nrm(ks[3], (L, D_MODEL), 0.1),
        'w_in': nrm(ks[4], (L, D_MODEL, N_IN), D_MODEL ** -0.5),
        'conv_w': nrm(ks[6], (L, GDN_CONV, GDN_QKV_W), GDN_CONV ** -0.5),
        'a_log': jnp.log(jax.random.uniform(ks[7], (L, GDN_HEADS), f32, 1.0, 16.0)),
        'dt_bias': dt + jnp.log(-jnp.expm1(-dt)),
        'gdn_norm': 1.0 + nrm(ks[8], (L, GDN_DV), 0.1),
        'cmp_pe_k': nrm(ks[9], (L, CMP_BLOCK, NSA_DH), 0.5),
        'cmp_pe_v': nrm(ks[10], (L, CMP_BLOCK, NSA_DH), 0.5),
        'cmp_w_k': nrm(ks[11], (L, CMP_BLOCK, NSA_DH, NSA_DH), (CMP_BLOCK * NSA_DH) ** -0.5),
        'cmp_w_v': nrm(ks[12], (L, CMP_BLOCK, NSA_DH, NSA_DH), (CMP_BLOCK * NSA_DH) ** -0.5),
        'w_branch_a': nrm(ks[13], (L, GDN_HEADS * GDN_DV, D_MODEL), (GDN_HEADS * GDN_DV) ** -0.5),
        'w_branch_b': nrm(ks[14], (L, NSA_HEADS * NSA_DH, D_MODEL), (NSA_HEADS * NSA_DH) ** -0.5),
        'w_out': nrm(ks[15], (L, D_MODEL, D_MODEL), D_MODEL ** -0.5),
        'norm_ffn': 1.0 + nrm(ks[16], (L, D_MODEL), 0.1),
        'w_query': nrm(ks[17], (L, D_MODEL, PEER_HEADS * PEER_DQ), D_MODEL ** -0.5),
        'sub_keys': nrm(ks[18], (L, PEER_HEADS, 2, PEER_NKEYS, PEER_DQH), PEER_DQH ** -0.5),
        'expert_u': nrm(ks[19], (L, PEER_N_EXPERTS, D_MODEL), D_MODEL ** -0.5),
        'expert_v': nrm(ks[20], (L, PEER_N_EXPERTS, D_MODEL), 0.5),
    }

def reference(x, rel_bias, norm_final, norm_mix, w_in, conv_w, a_log, dt_bias, gdn_norm, cmp_pe_k,
              cmp_pe_v, cmp_w_k, cmp_w_v, w_branch_a, w_branch_b, w_out, norm_ffn, w_query, sub_keys,
              expert_u, expert_v):
    for layer in range(DEPTH):
        x = hybrid_layer(x, rel_bias, norm_mix[layer], w_in[layer], conv_w[layer], a_log[layer],
                         dt_bias[layer], gdn_norm[layer], cmp_pe_k[layer], cmp_pe_v[layer],
                         cmp_w_k[layer], cmp_w_v[layer], w_branch_a[layer], w_branch_b[layer],
                         w_out[layer], norm_ffn[layer], w_query[layer], sub_keys[layer],
                         expert_u[layer], expert_v[layer])
    return rms_norm(x, norm_final)


_drawn_inputs = setup_inputs


def setup_inputs(seed=0):
    import zlib

    import numpy as np

    out = dict(_drawn_inputs(seed))
    spreads = {}
    factors = {}
    for name, (base, spread) in spreads.items():
        noise = np.random.default_rng([zlib.crc32(name.encode()), seed]).standard_normal(out[name].shape)
        drawn = base * np.exp(spread * noise) if base else spread * noise
        out[name] = __import__('jax').numpy.asarray(drawn.astype(out[name].dtype))
    for name, factor in factors.items():
        out[name] = (out[name] * factor).astype(out[name].dtype)
    return out
```

```python
from contextlib import ExitStack

import concourse.bass as bass
from concourse import mybir

P = 128
T = 256
TT_ = T // P
D = 1024
KT = D // P
H = 8
HP = H // 2
DH = 64
CH = 64
NSLOT = 8
NKEYS = 128
TOPK = 16
NCMP = (T - 32) // 16 + 1
EPS = 1e-6
NEG = -1e30

N_GDN, N_TOK, N_NSA, N_MERGE, N_CMP, N_AB, N_OUT, N_WQ, N_SK = 12, 8, 8, 16, 4, 8, 8, 16, 2
T_GDN = 0
T_TOK = T_GDN + N_GDN
T_NSA = T_TOK + N_TOK
T_MERGE = T_NSA + N_NSA
T_CMP = T_MERGE + N_MERGE
T_AB = T_CMP + N_CMP
T_OUT = T_AB + N_AB
T_WQ = T_OUT + N_OUT
T_SK = T_WQ + N_WQ
T_U = T_SK + N_SK
T_V = T_U + NKEYS
N_TILES = T_V + NKEYS

C_ID, C_TRI, C_SAME, C_ONES, C_IOTA, C_LEV = 0, 128, 256, 384, 512, 640
N_LEV = 6
C_CMASK = C_LEV + N_LEV * 128
C_FLIP = C_CMASK + 32
N_CONST = C_FLIP + 128
R_NM, R_NF, R_CW, R_PE, R_ALOG, R_DT, R_GN = 0, 8, 16, 64, 128, 136, 144
N_PAR = 208
N_E1, N_E2 = 384, 511

F32 = mybir.dt.float32
U32 = mybir.dt.uint32
ALU = mybir.AluOpType
ACT = mybir.ActivationFunctionType
AX = mybir.AxisListType


def build(nc, x, stream, consts, params, onehot, relb, nfinal, bias_scratch, out, debug=None):
    ctx = ExitStack()
    with ctx:
        def sb(name, shape, dt=F32):
            return ctx.enter_context(nc.sbuf_tensor(name, shape, dt))

        semaphores = {}

        def sem(name):
            if name not in semaphores:
                semaphores[name] = ctx.enter_context(nc.semaphore(name))
            return semaphores[name]

        ring = sb("ring", [P, NSLOT, 1024])
        xr = sb("xr", [P, TT_, D])
        cst = sb("cst", [P, N_CONST])
        par = sb("par", [P, N_PAR])
        small = sb("small", [P, 640])
        arena = sb("arena", [P, 40208])
        ps = ctx.enter_context(nc.psum_tensor("ps", [P, 8, 512], F32))

        def at(off, n):
            return arena[:, off:off + n]

        ident = cst[:, C_ID:C_ID + P]
        tri = cst[:, C_TRI:C_TRI + P]
        same = cst[:, C_SAME:C_SAME + P]
        ones = cst[:, C_ONES:C_ONES + P]
        iota = cst[:, C_IOTA:C_IOTA + P]
        level = cst[:, C_LEV:C_LEV + N_LEV * P].rearrange("p (l j) -> p l j", l=N_LEV)
        flip = cst[:, C_FLIP:C_FLIP + P]
        cmask = cst[:, C_CMASK:C_CMASK + 32].rearrange("p (i n) -> p i n", i=TT_)

        hT = at(0, 2048).rearrange("p (k t) -> p k t", k=KT)
        Yb = at(0, 2048).rearrange("p (g h j) -> p g h j", g=4, h=HP)
        pad = at(2048, 12 * 259).rearrange("p (n t) -> p n t", n=12)
        conv = at(5160, 3072).rearrange("p (n t) -> p n t", n=12)
        kn, kb, qn, qd, kbg, vb = [
            at(2048 + 1024 * n, 1024).rearrange("p (i h d) -> p i h d", i=TT_, h=H) for n in range(6)]
        qkvt = at(8448, 3072).rearrange("p (i c) -> p i c", i=TT_)
        Tm = at(8448, 2048).rearrange("p (g h j) -> p g h j", g=4, h=HP)
        vn = at(8448, 512)
        S = at(8960, 512).rearrange("p (q e) -> p q e", q=HP)
        oaT = at(9472, 1024).rearrange("p (k t) -> p k t", k=HP)
        nsaf = at(11520, 2048).rearrange("p (n t) -> p n t", n=8)
        mg = at(13568, 4096).rearrange("p (n t) -> p n t", n=16)
        zs = at(17664, 1024).rearrange("p (i c) -> p i c", i=TT_)
        tk = at(18688, 592).rearrange("p (i c) -> p i c", i=TT_)
        BT = at(19328, 2048).rearrange("p (h j) -> p h j", h=H)
        BTrev = at(0, 2048).rearrange("p (h j) -> p h j", h=H)
        XT = at(21376, 4096).rearrange("p (x i q t) -> p x i q t", x=4, i=TT_, q=HP)
        onsa = at(21376, 1024).rearrange("p (i c) -> p i c", i=TT_)
        obT = at(22400, 1024).rearrange("p (k t) -> p k t", k=HP)
        oa = at(23424, 1024).rearrange("p (i c) -> p i c", i=TT_)
        qdT = XT[:, 3]
        DT = at(25472, 2048).rearrange("p (i h t) -> p i h t", i=TT_, h=H)
        nwT = at(25472, 1024).rearrange("p (i q t) -> p i q t", i=TT_, q=HP)
        AT = at(27520, 2048).rearrange("p (i h t) -> p i h t", i=TT_, h=H)
        mixT = at(27520, 2048).rearrange("p (k t) -> p k t", k=KT)
        attnT = at(29568, 2048).rearrange("p (i h t) -> p i h t", i=TT_, h=H)
        TT = at(31616, 2048).rearrange("p (g h j) -> p g h j", g=4, h=HP)
        AbT = at(33664, 2048).rearrange("p (g h j) -> p g h j", g=4, h=HP)
        grhs = at(33664, 2048).rearrange("p (i h t) -> p i h t", i=TT_, h=H)
        kd = at(35712, 1024).rearrange("p (i h d) -> p i h d", i=TT_, h=H)
        kd_f = at(35712, 1024).rearrange("p (i c) -> p i c", i=TT_)
        Sb = at(36736, 1024).rearrange("p (b j) -> p b j", b=2)
        PT = at(37760, 1024).rearrange("p (b j) -> p b j", b=2)
        vcbd = at(38784, 512)
        kcmpT = at(39296, 16)
        vcs = at(39312, 128)
        bcmp = at(39440, 256).rearrange("p (i h n) -> p i h n", i=TT_, h=H)
        pc = at(39696, 256).rearrange("p (i h n) -> p i h n", i=TT_, h=H)
        pc_f = at(39696, 256).rearrange("p (i c) -> p i c", i=TT_)
        pcT = at(39952, 256).rearrange("p (i t) -> p i t", i=TT_)
        rrs = at(36736, 384)
        E = at(33664, N_E1 + N_E2)
        kcpe = at(31616, 960).rearrange("p (s l n) -> p s l n", s=2, l=32)
        junk = at(27520, 2048).rearrange("p (i c) -> p i c", i=TT_)
        sq = at(29568, 2048).rearrange("p (i c) -> p i c", i=TT_)

        act_w = at(0, NKEYS * T).rearrange("p (e t) -> p e t", e=NKEYS)
        qT = at(16384, 4096).rearrange("p (n t) -> p n t", n=16)
        sc = at(20480, 4096).rearrange("p (i n k) -> p i n k", i=TT_, n=16)
        oh = at(24576, 2048).rearrange("p (m a) -> p m a", a=TOPK)
        tkv = at(26624, 512).rearrange("p (i n k) -> p i n k", i=TT_, n=16)
        tki = at(27136, 512).rearrange("p (i n k) -> p i n k", i=TT_, n=16)
        tki_u = at(27648, 512).bitcast(U32).rearrange("p (i n k) -> p i n k", i=TT_, n=16)
        rep = at(28160, 128)
        cand = at(28288, 256)
        cand2 = at(28544, 256)
        topv = at(28800, 256).rearrange("p (i h k) -> p i h k", i=TT_, h=H)
        topi_u = at(29056, 256).bitcast(U32).rearrange("p (i h k) -> p i h k", i=TT_, h=H)
        ab_u = at(29312, 512).bitcast(U32).rearrange("p (s i c) -> p s i c", s=2, i=TT_)
        ab_f = at(29824, 512).rearrange("p (s i c) -> p s i c", s=2, i=TT_)
        e_f = at(37632, 512).rearrange("p (s i c) -> p s i c", s=2, i=TT_)
        gate = at(38144, 256).rearrange("p (i h k) -> p i h k", i=TT_, h=H)
        gate_f = at(38144, 256).rearrange("p (i c) -> p i c", i=TT_)
        h2T = at(32768, 2048).rearrange("p (k t) -> p k t", k=KT)
        egT = at(34816, 768).rearrange("p (s t) -> p s t", s=3)
        ohA = at(35584, 2048).rearrange("p (t j) -> p t j", t=16)
        ohB = at(37632, 2048).rearrange("p (t j) -> p t j", t=16)
        nfin = at(32768, 1024)
        peerT = at(0, 2048).rearrange("p (k t) -> p k t", k=KT)

        def sm(off, n):
            return small[:, off:off + n]

        rms = sm(0, 8)
        sg = sm(8, 64).rearrange("p (i c) -> p i c", i=TT_)
        ga_ = sm(72, 16).rearrange("p (i h) -> p i h", i=TT_)
        gm = sm(88, 16).rearrange("p (i h) -> p i h", i=TT_)
        ge = sm(104, 16).rearrange("p (i h) -> p i h", i=TT_)
        gz = sm(120, 16).rearrange("p (i h) -> p i h", i=TT_)
        gt = sm(136, 16).rearrange("p (i h) -> p i h", i=TT_)
        gp = sm(152, 16).rearrange("p (i h) -> p i h", i=TT_)
        gg = sm(168, 16).rearrange("p (i h) -> p i h", i=TT_)
        ea = sm(184, 8)
        gcl = sm(192, 32).rearrange("p (i c) -> p i c", i=TT_)
        ngc = sm(224, 16).rearrange("p (i h) -> p i h", i=TT_)
        eg = sm(240, 16).rearrange("p (i h) -> p i h", i=TT_)
        neg_eg = sm(256, 16).rearrange("p (i h) -> p i h", i=TT_)
        ekd = sm(272, 16).rearrange("p (i h) -> p i h", i=TT_)
        egl = sm(288, 16).rearrange("p (i q c) -> p i q c", i=TT_, q=HP)
        ssq = sm(304, 32).rearrange("p (i c) -> p i c", i=TT_)
        rq = sm(336, 32).rearrange("p (i c) -> p i c", i=TT_)
        mx = sm(368, 32).rearrange("p (n b) -> p n b", n=16)
        sums = sm(400, 48).rearrange("p (i h b) -> p i h b", i=TT_, h=H)
        coef = sm(448, 48).rearrange("p (i h b) -> p i h b", i=TT_, h=H)
        cmx = sm(496, 16).rearrange("p (i h) -> p i h", i=TT_)
        gs = sm(512, 16).rearrange("p (i h) -> p i h", i=TT_)
        gr = sm(528, 16).rearrange("p (i h) -> p i h", i=TT_)
        oss = sm(544, 16).rearrange("p (i h) -> p i h", i=TT_)
        osr = sm(560, 16).rearrange("p (i h) -> p i h", i=TT_)
        rel = sm(576, 8)
        k2s = sm(584, 16)

        def par_cols(off, n):
            return par[:, off:off + n]

        def bank(b, a=0, n=512):
            return ps[:, b, a:a + n]

        def slot(n):
            return ring[:, n % NSLOT, :]

        def each(ap, n):
            return ap.unsqueeze(2).broadcast_to([ap.shape[0], ap.shape[1], n])

        def over(ap, n):
            return ap.unsqueeze(1).broadcast_to([ap.shape[0], n, ap.shape[1]])

        block = ctx.enter_context(nc.Block())

        @block.sync
        def _(sp):
            sp.dma_start(xr[:, :, :], x.rearrange("(i p) d -> p i d", p=P)).then_inc(sem("x_in"), 16)
            sp.dma_start(cst[:, :], consts).then_inc(sem("consts_in"), 16)
            sp.dma_start(par[:, :], params).then_inc(sem("params_in"), 16)
            sp.dma_start(E[0:33, :], onehot).then_inc(sem("onehot_in"), 16)
            sp.dma_start(rel[0:33, :], relb).then_inc(sem("onehot_in"), 16)
            for s in range(NSLOT):
                sp.dma_start(slot(s), stream[s]).then_inc(sem(f"slot{s}_in"), 16)

            def refill(group, s):
                sp.wait_ge(sem("tiles_used"), group * NSLOT + (s - NSLOT + 1))
                sp.dma_start(slot(s), stream[group * NSLOT + s]).then_inc(sem(f"slot{s}_in"), 16)

            with sp.Fori(1, N_TILES // NSLOT, 1) as group:
                for s in range(NSLOT):
                    refill(group, s)
            for s in range(N_TILES % NSLOT):
                refill(N_TILES // NSLOT, s)
            sp.wait_ge(sem("out_ready"), TT_)
            sp.dma_start(out.rearrange("(i p) d -> p i d", p=P), xr[:, :, :]).then_inc(sem("stored"), 16)
            sp.wait_ge(sem("stored"), 16)

        @block.tensor
        def _(pe):
            def mm(o, lhsT, rhs, start=True, stop=True):
                return pe.matmul(o, lhsT, rhs, start=start, stop=stop, skip_group_check=True)

            def arrived(n):
                pe.wait_ge(sem(f"slot{n % NSLOT}_in"), 16 * (n // NSLOT + 1))

            pe.wait_ge(sem("onehot_in"), 32)
            mm(bank(0, 0, N_E1)[0:H], rel[0:33, :], E[0:33, 0:N_E1]).then_inc(sem("bias_row_done"), 1)
            for i in range(TT_):
                for n in range(NCMP):
                    k = N_E1 + 224 - 16 * n + P * i
                    m = mm(bank(1, (i * NCMP + n) * H, H), E[0:33, k:k + P], rel[0:33, :],
                           start=(i == 0 and n == 0))
            m.then_inc(sem("bias_cmp_done"), 1)

            pe.wait_ge(sem("consts_in"), 16)
            for i in range(TT_):
                pe.wait_ge(sem("xn_ready"), i + 1)
                for half in range(2):
                    for j in range(4):
                        k = half * 4 + j
                        m = pe.transpose(bank(4 + 2 * i + half, j * P, P), junk[:, i, k * P:(k + 1) * P], ident)
                    m.then_inc(sem("hT_done"), 1)

            def project(n, tile):
                arrived(tile)
                if n >= 4:
                    pe.wait_ge(sem("proj_evac"), n - 3)
                w = slot(tile).rearrange("p (k m) -> p k m", k=KT)
                for k in range(KT):
                    m = mm(bank(n % 4, 0, T), w[:, k, :], hT[:, k, :], start=(k == 0), stop=(k == KT - 1))
                m.then_inc(sem("tiles_used"), 1)

            pe.wait_ge(sem("hT_ready"), 4)
            pe.wait_ge(sem("bias_read"), 3)
            for n in range(N_GDN):
                project(n, T_GDN + n)
            for k in range(N_TOK):
                arrived(T_TOK + k)
                w = slot(T_TOK + k)
                for i in range(TT_):
                    h_t = hT[:, k, i * P:(i + 1) * P]
                    mm(bank(4 + 2 * i), h_t, w[:, 0:512], start=(k == 0), stop=(k == KT - 1))
                    m = mm(bank(5 + 2 * i, 0, 296), h_t, w[:, 512:808], start=(k == 0), stop=(k == KT - 1))
                m.then_inc(sem("tiles_used"), 1)
            for n in range(N_NSA):
                project(N_GDN + n, T_NSA + n)

            for f in range(6):
                part, i = f // 2, f % 2
                pe.wait_ge(sem("silu_done"), 4 * (part + 1))
                pe.wait_ge(*[(sem("z_evac"), 1), (sem("tok_evac"), 1), (sem("z_evac"), 2), (sem("tok_evac"), 2),
                             (sem("tt_evac"), 1), (sem("tt_evac"), 2)][f])
                for j in range(4):
                    m = pe.transpose(bank(4 + f % 4, j * P, P), conv[:, part * 4 + j, i * P:(i + 1) * P], ident)
                m.then_inc(sem("tt_done"), 1)

            for n in range(N_MERGE):
                project(N_GDN + N_NSA + n, T_MERGE + n)

            pe.wait_ge(sem("g_ready"), 1)
            pe.wait_ge(sem("tt_evac"), 5)
            for i in range(TT_):
                mm(bank(4, 16 * i, 8), tri, gg[:, i, :], start=(i == 0))
                m = mm(bank(4, 16 * i + 8, 8), same, gg[:, i, :], start=False)
            m.then_inc(sem("gcl_done"), 1)
            pe.wait_ge(sem("tt_evac"), 6)
            for i in range(TT_):
                pe.wait_ge(sem("grhs_ready"), i + 1)
                for half in range(2):
                    if i == 1 and half == 1:
                        pe.wait_ge(sem("gcl_evac"), 1)
                    m = mm(bank(4 + (1 + 2 * i + half) % 4), ones, grhs[:, i, 4 * half:4 * half + 4, :])
                m.then_inc(sem("gbc_done"), 1)

            pe.wait_ge(sem("proj_evac"), N_GDN + N_NSA + N_MERGE)
            for f in range(8):
                which, i = f // 2, f % 2
                pe.wait_ge(sem("gdn_rows_ready"), f + 1)
                if f >= 4:
                    pe.wait_ge(sem("fT_evac"), f - 3)
                src = at(2048 + 1024 * which, 1024).rearrange("p (i c) -> p i c", i=TT_)
                for q in range(HP):
                    m = pe.transpose(bank(f % 4, q * P, P), src[:, i, q * P:(q + 1) * P], ident)
                m.then_inc(sem("fT_done"), 1)

            pe.wait_ge(sem("gbc_read"), 2)
            pe.wait_ge(sem("DT_in"), 2)
            pe.wait_ge(sem("fT_evac"), 8)
            for r in range(8):
                which, i, p = r // 4, (r // 2) % 2, r % 2
                if r >= 4:
                    pe.wait_ge(sem("am_evac"), r - 3)
                rows = slice(DH * p, DH * p + DH)
                for q in range(HP):
                    m = mm(bank(4 + r % 4, q * P, P), XT[rows, 0, i, q, :], XT[rows, 1 + which, i, q, :],
                           start=(q == 0))
                m.then_inc(sem("am_done"), 1)

            pe.wait_ge(sem("kcpe_ready"), 4)
            for s in range(2):
                for half in range(2):
                    tile = T_CMP + 2 * s + half
                    arrived(tile)
                    w = slot(tile).rearrange("p (l e) -> p l e", l=16)
                    for g in range(2):
                        rows = slice(DH * g, DH * g + DH)
                        for l in range(16):
                            ll = half * 16 + l
                            if s == 0:
                                m = mm(ps[rows, g, 0:NCMP], w[rows, l, :], kcpe[rows, 0, ll, :],
                                       start=(ll == 0), stop=(ll == 31))
                            else:
                                m = mm(ps[0:NCMP, 2 + g, 0:DH], kcpe[rows, 1, ll, :], w[rows, l, :],
                                       start=(ll == 0), stop=(ll == 31))
                    m.then_inc(sem("tiles_used"), 1)

            pe.wait_ge(sem("kvcmp_evac"), 4)
            pe.wait_ge(sem("am_evac"), 8)
            for i in range(TT_):
                for g in range(2):
                    rows = slice(DH * g, DH * g + DH)
                    for q in range(4):
                        m = mm(bank(4 + 2 * i + g, q * 16, NCMP), nsaf[rows, q, i * P:(i + 1) * P],
                               kcmpT[rows, 0:NCMP], start=(q == 0))
                    m.then_inc(sem("sc_done"), 1)
            pe.wait_ge(sem("BTrev_in"), 16)
            for b in range(4):
                mm(bank(b), flip, BTrev[:, 2 * b:2 * b + 2, :]).then_inc(sem("BT_done"), 1)
            pe.wait_ge(sem("BT_in"), 4)
            pe.wait_ge(sem("vcbd_in"), 16 * H)
            for i in range(TT_):
                pe.wait_ge(sem("pc_ready"), i + 1)
                pe.transpose(bank(i, 0, P), pc_f[:, i, :], ident).then_inc(sem("pcT_done"), 1)
            for i in range(TT_):
                pe.wait_ge(sem("pcT_evac"), i + 1)
                mm(bank(2 + i), pcT[:, i, :], vcbd).then_inc(sem("oc_done"), 1)

            def nsa_scores(n):
                i, h = n // H, n % H
                nk = P * (i + 1)
                if n < 2:
                    pe.wait_ge(sem("pcT_evac"), n + 1)
                else:
                    pe.wait_ge(sem("s_evac"), n - 1)
                rows = slice(DH * (h // 4), DH * (h // 4) + DH)
                for b in range(2):
                    m = mm(bank(n % 2, b * nk, nk), nsaf[rows, h % 4, i * P:(i + 1) * P],
                           nsaf[rows, 5 + b, 0:nk], start=(b == 0))
                m.then_inc(sem("s_done"), 1)

            def nsa_transpose(n):
                i = n // H
                pe.wait_ge(sem("p_ready"), n + 1)
                if n < 2:
                    pe.wait_ge(sem("oc_evac"), n + 1)
                else:
                    pe.wait_ge(sem("pT_evac"), n - 1)
                for j in range(2 * (i + 1)):
                    m = pe.transpose(bank(2 + n % 2, j * P, P), Sb[:, n % 2, j * P:(j + 1) * P], ident)
                m.then_inc(sem("pT_done"), 1)

            def nsa_values(n):
                i, h = n // H, n % H
                g = h // 4
                pe.wait_ge(sem("pT_evac"), n + 1)
                for b in range(2):
                    for j in range(i + 1):
                        m = mm(bank(4 + 2 * i + b, h * DH, DH), PT[:, n % 2, (b * (i + 1) + j) * P:][:, 0:P],
                               tk[:, j, 40 + 128 * b + DH * g:][:, 0:DH], start=(h == 0 and j == 0), stop=(j == i))
                m.then_inc(sem("pv_done"), 1)

            for n in range(TT_ * H + 2):
                if n < TT_ * H:
                    nsa_scores(n)
                if 1 <= n <= TT_ * H:
                    nsa_transpose(n - 1)
                if n >= 2:
                    nsa_values(n - 2)

            for g in range(4):
                pe.wait_ge(sem("TT0_ready"), g + 1)
                if g == 0:
                    pe.wait_ge(sem("pT_evac"), TT_ * H)
                for q in range(HP):
                    m = pe.transpose(bank(g, q * P, P), TT[:, g, q, :], ident)
                m.then_inc(sem("T0_done"), 1)
            pe.wait_ge(sem("onsa_ready"), TT_)
            for lv in range(1, N_LEV):
                for g in range(4):
                    pe.wait_ge(sem("AbT_ready"), (lv - 1) * 4 + g + 1)
                    pe.wait_ge(sem("T_ready"), (lv - 1) * 4 + g + 1)
                    for q in range(HP):
                        m = mm(bank(g, q * P, P), AbT[:, g, q, :], Tm[:, g, q, :], start=(q == 0))
                    m.then_inc(sem("Y_done"), 1)
                for g in range(4):
                    n = (lv - 1) * 4 + g
                    pe.wait_ge(sem("Y_evac"), n + 1)
                    if n >= 2:
                        pe.wait_ge(sem("TT_ready"), n - 1)
                    b0 = 4 + 2 * (g % 2)
                    if lv < N_LEV - 1:
                        for q in range(HP):
                            mm(bank(b0, q * P, P), TT[:, g, q, :], Yb[:, g, q, :], start=(q == 0))
                    for q in range(HP):
                        m = mm(bank(b0 + 1, q * P, P), Yb[:, g, q, :], TT[:, g, q, :], start=(q == 0))
                    m.then_inc(sem("TY_done"), 1)

            for i in range(TT_):
                for p in range(2):
                    pe.wait_ge(sem("TT_ready"), 4 * (N_LEV - 2) + 2 * i + p + 1)
                    for q in range(HP):
                        m = mm(ps[DH * p:DH * p + DH, i, q * P:(q + 1) * P], kbg[:, i, 2 * q + p, :],
                               TT[:, 2 * i + p, q, :], start=(q == 0))
                m.then_inc(sem("nwT_done"), 1)

            pe.wait_ge(sem("TT_ready"), 4 * (N_LEV - 1))
            pe.wait_ge(sem("scan_zero"), 2)
            for c in range(T // CH):
                i, r0 = c // 2, CH * (c % 2)
                rows = slice(r0, r0 + CH)
                if c == 0:
                    pe.wait_ge(sem("nwT_evac"), TT_)
                for h in range(H):
                    m = mm(ps[rows, 2, h * DH:(h + 1) * DH], TT[:, 2 * i + h % 2, h // 2, rows],
                           vb[:, i, h, :], start=(h == 0), stop=(c == 0))
                if c >= 1:
                    pe.wait_ge(sem("S_ready"), c)
                    for q in range(HP):
                        m = mm(ps[rows, 2, q * P:(q + 1) * P], nwT[:, i, q, rows], S[:, q, :], start=False)
                m.then_inc(sem("vn_done"), 1)
                if c >= 1:
                    pe.wait_ge(sem("o_evac"), c)
                    for q in range(HP):
                        mm(ps[rows, 3, q * P:(q + 1) * P], qdT[:, i, q, rows], S[:, q, :], start=(q == 0), stop=False)
                pe.wait_ge(sem("vn_evac"), c + 1)
                if c < T // CH - 1:
                    for q in range(HP):
                        m = mm(bank(4, q * P, P), kd_f[rows, i, q * P:(q + 1) * P], vn[rows, q * P:(q + 1) * P],
                               start=(q == 0))
                    m.then_inc(sem("dS_done"), 1)
                for h in range(H):
                    m = mm(ps[rows, 3, h * DH:(h + 1) * DH], attnT[:, i, h, rows], vn[:, h * DH:(h + 1) * DH],
                           start=(c == 0 and h == 0))
                m.then_inc(sem("o_done"), 1)

            for i in range(TT_):
                pe.wait_ge(sem("onsa_ready"), TT_)
                for k in range(HP):
                    m = pe.transpose(bank(i, k * P, P), onsa[:, i, k * P:(k + 1) * P], ident)
                m.then_inc(sem("obT_done"), 1)
            for i in range(TT_):
                pe.wait_ge(sem("oa_ready"), TT_)
                for k in range(HP):
                    m = pe.transpose(bank(5 + i, k * P, P), oa[:, i, k * P:(k + 1) * P], ident)
                m.then_inc(sem("oaT_done"), 1)

            pe.wait_ge(sem("oaT_evac"), TT_)
            pe.wait_ge(sem("obT_evac"), TT_)
            for j in range(N_AB):
                arrived(T_AB + j)
                if j >= 4:
                    pe.wait_ge(sem("mix_ready"), j - 3)
                w = slot(T_AB + j).rearrange("p (k m) -> p k m", k=2 * HP)
                for s, src in ((0, oaT), (1, obT)):
                    for k in range(HP):
                        m = mm(bank(j % 4, s * T, T), w[:, s * HP + k, :], src[:, k, :],
                               start=(s == 0 and k == 0), stop=(k == HP - 1))
                m.then_inc(sem("tiles_used"), 1)
            for k in range(N_OUT):
                arrived(T_OUT + k)
                pe.wait_ge(sem("mix_ready"), k + 1)
                for i in range(TT_):
                    for half in range(2):
                        m = mm(bank(4 + 2 * i + half), mixT[:, k, i * P:(i + 1) * P],
                               slot(T_OUT + k)[:, half * 512:(half + 1) * 512], start=(k == 0), stop=(k == KT - 1))
                m.then_inc(sem("tiles_used"), 1)

            pe.wait_ge(sem("mix_ready"), N_AB)
            for i in range(TT_):
                pe.wait_ge(sem("xn2_ready"), i + 1)
                for half in range(2):
                    for j in range(4):
                        k = half * 4 + j
                        m = pe.transpose(bank(2 * i + half, j * P, P), junk[:, i, k * P:(k + 1) * P], ident)
                    m.then_inc(sem("h2T_done"), 1)

            pe.wait_ge(sem("h2T_ready"), 4)
            for n in range(N_WQ):
                arrived(T_WQ + n)
                if n >= 4:
                    pe.wait_ge(sem("q_evac"), n - 3)
                w = slot(T_WQ + n).rearrange("p (k m) -> p k m", k=KT)
                for k in range(KT):
                    m = mm(bank(n % 4, 0, T), w[:, k, :], h2T[:, k, :], start=(k == 0), stop=(k == KT - 1))
                m.then_inc(sem("tiles_used"), 1)
            for s in range(N_SK):
                arrived(T_SK + s)
                w = slot(T_SK + s).rearrange("p (n k) -> p n k", n=8)
                pe.wait_ge(sem("q_evac"), 8 * s + 8)
                for i in range(TT_):
                    for half in range(2):
                        f = s * 4 + i * 2 + half
                        if f >= 4:
                            pe.wait_ge(sem("key_sc_evac"), f - 3)
                        for j in range(4):
                            n = half * 4 + j
                            m = mm(bank(4 + f % 4, j * P, P), qT[:, s * 8 + n, i * P:(i + 1) * P], w[:, n, :],
                                   start=(j == 0))
                        m.then_inc(sem("tiles_used" if f % 4 == 3 else "key_sc_done"), 1)

            def expert_in(group, s):
                n = T_U + s
                pe.wait_ge(sem(f"slot{n % NSLOT}_in"), group * 16 + 16 * (n // NSLOT + 1))
                pe.wait_ge(sem("u_evac"), group * NSLOT + (s + 1))
                w = slot(n).rearrange("p (k m) -> p k m", k=KT)
                for k in range(KT):
                    m = mm(bank(s % 4, 0, T), w[:, k, :], h2T[:, k, :], start=(k == 0), stop=(k == KT - 1))
                m.then_inc(sem("tiles_used"), 1)

            with pe.Fori(0, NKEYS // NSLOT, 1) as group:
                for s in range(NSLOT):
                    expert_in(group, s)

            pe.wait_ge(sem("choice_ready"), 1)
            for s in range(3):
                for i in range(TT_):
                    src = gate_f[:, i, :] if s == 2 else e_f[:, s, i, :]
                    m = pe.transpose(bank(4 + s, i * P, P), src, ident)
            m.then_inc(sem("egT_done"), 1)

            pe.wait_ge(sem("u_evac"), NKEYS + 4)
            pe.sem_inc(sem("G_done"), 4)
            with pe.Fori(0, T // 16, 1) as group:
                for q in range(4):
                    pe.wait_ge(sem("ohA_ready"), group * 4 + (q + 1))
                    pe.wait_ge(sem("ohB_ready"), group * 2 + (q // 2 + 1))
                    pe.wait_ge(sem("weighed"), group * 4 + (q + 1))
                    for j in range(4):
                        t = 4 * q + j
                        m = mm(bank(q, j * P, P), ohA[:, t, :], ohB[:, t, :], start=(j == 0))
                    m.then_inc(sem("G_done"), 1)

            pe.wait_ge(sem("egT_read"), 1)
            pe.wait_ge(sem("weighed"), T // 4 + 4)

            def expert_out(group, s, first):
                n = T_V + s
                pe.wait_ge(sem(f"slot{n % NSLOT}_in"), group * 16 + 16 * (n // NSLOT + 1))
                for c in range(KT):
                    m = mm(bank(4 + c // 2, (c % 2) * T, T), slot(n)[:, c * P:(c + 1) * P],
                           act_w[:, group * NSLOT + s, :], start=(first and s == 0 and c % 2 == 0), stop=False)
                m.then_inc(sem("tiles_used"), 1)

            for s in range(NSLOT):
                expert_out(0, s, True)
            with pe.Fori(1, NKEYS // NSLOT, 1) as group:
                for s in range(NSLOT):
                    expert_out(group, s, False)

            pe.wait_ge(sem("peerT_ready"), 4)
            for i in range(TT_):
                for half in range(2):
                    for j in range(4):
                        k = half * 4 + j
                        m = pe.transpose(bank(2 * i + half, j * P, P), peerT[:, k, i * P:(i + 1) * P], ident)
                    m.then_inc(sem("peer_done"), 1)

        @block.scalar
        def _(act):
            def tile_done(n):
                act.wait_ge(sem("tiles_used"), n + 1)

            act.wait_ge(sem("rms_mean"), 1)
            act.activation(rms[:, 4:6], rms[:, 2:4], ACT.Sqrt).then_inc(sem("rms_root"), 1)
            act.wait_ge(sem("pad_zero"), 1)
            for n in range(N_GDN + 2):
                if n < N_GDN:
                    tile_done(T_GDN + n)
                    act.activation(pad[:, n, 3:259], bank(n % 4, 0, T), ACT.Copy).then_inc(sem("proj_evac"), 1)
                if n >= 2:
                    act.wait_ge(sem("conv_done"), n - 1)
                    act.activation(conv[:, n - 2, :], conv[:, n - 2, :], ACT.Silu).then_inc(sem("silu_done"), 1)
            tile_done(T_TOK + N_TOK - 1)
            for i in range(TT_):
                act.activation(zs[:, i, :], bank(4 + 2 * i), ACT.Silu).then_inc(sem("z_evac"), 1)
            for n in range(N_NSA):
                tile_done(T_NSA + n)
                act.activation(nsaf[:, n, :], bank((N_GDN + n) % 4, 0, T), ACT.Copy).then_inc(sem("proj_evac"), 1)
            for f in range(6):
                act.wait_ge(sem("tt_done"), f + 1)
                act.activation(qkvt[:, f % 2, 512 * (f // 2):][:, 0:512], bank(4 + f % 4), ACT.Copy)\
                   .then_inc(sem("tt_evac"), 1)
            act.wait_ge(sem("tok_evac"), TT_)
            act.activation(sg, tk[:, :, 0:32], ACT.Sigmoid).then_inc(sem("sg_ready"), 1)
            for n in range(N_MERGE):
                tile_done(T_MERGE + n)
                act.activation(mg[:, n, :], bank((N_GDN + N_NSA + n) % 4, 0, T), ACT.Sigmoid)\
                   .then_inc(sem("proj_evac"), 1)
                if n == 3:
                    act.wait_ge(sem("ge_in"), 1)
                    act.activation(ge, ge, ACT.Exp).then_inc(sem("ge_out"), 1)
                    act.activation(ea, par_cols(R_ALOG, 8), ACT.Exp).then_inc(sem("ge_out"), 1)
                    act.wait_ge(sem("ssq_ready"), 1)
                    act.activation(rq, ssq, ACT.Sqrt).then_inc(sem("rq_root"), 1)
            act.wait_ge(sem("gcl_evac"), 1)
            act.activation(eg, gcl[:, :, 0:8], ACT.Exp).then_inc(sem("eg_ready"), 1)
            act.wait_ge(sem("ekd_in"), 1)
            act.activation(ekd, ekd, ACT.Exp).then_inc(sem("ekd_ready"), 1)
            for i in range(TT_):
                act.wait_ge(sem("DT_in"), i + 1)
                for p in range(2):
                    rows = slice(DH * p, DH * p + DH)
                    for half in range(2):
                        b = 4 + (1 + 2 * i + half) % 4
                        src = ps[rows, b, :].rearrange("p (q z c t) -> p q z c t", q=2, z=2, c=2)[:, :, p, :, CH - 1]
                        m = act.activation(egl[rows, i, 2 * half:2 * half + 2, :], src, ACT.Exp)
                m.then_inc(sem("gbc_read"), 1)
                act.activation(DT[:, i], DT[:, i], ACT.Exp).then_inc(sem("DT_exp"), 1)
            for f in range(8):
                act.wait_ge(sem("fT_done"), f + 1)
                act.activation(XT[:, f // 2, f % 2], bank(f % 4), ACT.Copy).then_inc(sem("fT_evac"), 1)
            for i in range(TT_):
                act.wait_ge(sem("pc_in"), i + 1)
                act.activation(pc[:, i], pc[:, i], ACT.Exp).then_inc(sem("pc_exp"), 1)
            for b in range(4):
                act.wait_ge(sem("BT_done"), b + 1)
                act.activation(BT[:, 2 * b:2 * b + 2, :], bank(b), ACT.Copy).then_inc(sem("BT_in"), 1)
            for i in range(TT_):
                act.wait_ge(sem("pcT_done"), i + 1)
                act.activation(pcT[:, i, :], bank(i, 0, P), ACT.Copy).then_inc(sem("pcT_evac"), 1)
            for n in range(TT_ * H + 1):
                if n < TT_ * H:
                    i, h = n // H, n % H
                    nk = P * (i + 1)
                    act.wait_ge(sem("s_ready"), n + 1)
                    for b in range(2):
                        m = act.activation(Sb[:, n % 2, b * nk:(b + 1) * nk], Sb[:, n % 2, b * nk:(b + 1) * nk], ACT.Exp,
                                           bias=mx[:, n, b:b + 1], accum_out=sums[:, i, h, 1 + b:2 + b])
                    m.then_inc(sem("p_ready"), 1)
                if n >= 1:
                    w = 2 * P * ((n - 1) // H + 1)
                    act.wait_ge(sem("pT_done"), n)
                    if n >= 3:
                        act.wait_ge(sem("pv_done"), n - 2)
                    act.activation(PT[:, (n - 1) % 2, 0:w], bank(2 + (n - 1) % 2, 0, w), ACT.Copy)\
                       .then_inc(sem("pT_evac"), 1)
            for g in range(4):
                act.wait_ge(sem("T0_done"), g + 1)
                act.activation(Tm[:, g], bank(g), ACT.Copy).then_inc(sem("T_ready"), 1)
            for n in range(4 * (N_LEV - 1)):
                act.wait_ge(sem("Y_done"), n + 1)
                if n >= 4:
                    act.wait_ge(sem("TY_done"), n - 3)
                act.activation(Yb[:, n % 4], bank(n % 4), ACT.Copy).then_inc(sem("Y_evac"), 1)
            for i in range(TT_):
                act.wait_ge(sem("nwT_done"), i + 1)
                act.activation(nwT[:, i], bank(i), ACT.Copy).then_inc(sem("nwT_evac"), 1)
            for c in range(T // CH):
                rows = slice(CH * (c % 2), CH * (c % 2) + CH)
                act.wait_ge(sem("o_done"), c + 1)
                act.activation(oa[rows, c // 2, :], ps[rows, 3, :], ACT.Copy).then_inc(sem("o_evac"), 1)
            act.wait_ge(sem("oss_ready"), 1)
            act.activation(osr, oss, ACT.Sqrt).then_inc(sem("osr_root"), 1)
            for i in range(TT_):
                act.wait_ge(sem("obT_done"), i + 1)
                act.activation(obT[:, :, i * P:(i + 1) * P], bank(i), ACT.Copy).then_inc(sem("obT_evac"), 1)
            for i in range(TT_):
                act.wait_ge(sem("oaT_done"), i + 1)
                act.activation(oaT[:, :, i * P:(i + 1) * P], bank(5 + i), ACT.Copy).then_inc(sem("oaT_evac"), 1)
            act.wait_ge(sem("rms_mean"), 2)
            act.activation(rms[:, 4:6], rms[:, 2:4], ACT.Sqrt).then_inc(sem("rms_root"), 1)
            for n in range(N_WQ):
                tile_done(T_WQ + n)
                act.activation(qT[:, n, :], bank(n % 4, 0, T), ACT.Copy).then_inc(sem("q_evac"), 1)
            for f in range(8):
                s, i, half = f // 4, (f // 2) % 2, f % 2
                if f % 4 == 3:
                    tile_done(T_SK + s)
                else:
                    act.wait_ge(sem("key_sc_done"), 3 * s + f % 4 + 1)
                act.activation(sc[:, i, 8 * s + 4 * half:8 * s + 4 * half + 4, :], bank(4 + f % 4), ACT.Copy)\
                   .then_inc(sem("key_sc_evac"), 1)
            act.wait_ge(sem("q_evac"), N_WQ)
            act.sem_inc(sem("u_evac"), 4)
            act.preload_act_table(ACT.Gelu_apprx_tanh)

            def gelu(group, s):
                act.wait_ge(sem("tiles_used"), group * NSLOT + (T_U + s + 1))
                act.activation(act_w[:, group * NSLOT + s, :], bank(s % 4, 0, T), ACT.Gelu_apprx_tanh)\
                   .then_inc(sem("u_evac"), 1)

            with act.Fori(0, NKEYS // NSLOT // 2, 1) as group:
                for s in range(NSLOT):
                    gelu(group, s)
            act.wait_ge(sem("gate_in"), TT_)
            for i in range(TT_):
                act.activation(gate[:, i], gate[:, i], ACT.Exp).then_inc(sem("gate_exp"), 1)
            act.preload_act_table(ACT.Gelu_apprx_tanh)
            with act.Fori(NKEYS // NSLOT // 2, NKEYS // NSLOT, 1) as group:
                for s in range(NSLOT):
                    gelu(group, s)
            act.wait_ge(sem("egT_done"), 1)
            m = act.activation(egT[:, :, :], ps[:, 4:7, 0:T], ACT.Copy)
            m.then_inc(sem("egT_read"), 1)
            act.wait_ge(sem("tiles_used"), N_TILES)
            for b in range(4):
                act.activation(peerT[:, 2 * b:2 * b + 2, :], bank(4 + b), ACT.Copy).then_inc(sem("peerT_ready"), 1)
            act.wait_ge(sem("rms_mean"), 3)
            act.activation(rms[:, 4:6], rms[:, 2:4], ACT.Sqrt).then_inc(sem("rms_root"), 1)

        @block.vector
        def _(dve):
            chain = [0]

            def link(m):
                chain[0] += 1
                m.then_inc(sem("dve_chain"), 1)
                dve.wait_ge(sem("dve_chain"), chain[0])

            tt, ts, stt = dve.tensor_tensor, dve.tensor_scalar, dve.scalar_tensor_tensor

            def tile_done(n):
                dve.wait_ge(sem("tiles_used"), n + 1)

            def rms_scale(turn):
                for i in range(TT_):
                    link(dve.tensor_tensor_reduce(sq[:, i, :], xr[:, i, :], xr[:, i, :], 1.0, 0.0, ALU.mult,
                                                  ALU.add, rms[:, i:i + 1]))
                ts(rms[:, 2:4], rms[:, 0:2], 1.0 / D, EPS, ALU.mult, ALU.add).then_inc(sem("rms_mean"), 1)
                dve.wait_ge(sem("rms_root"), turn)
                link(dve.reciprocal(rms[:, 6:8], rms[:, 4:6]))

            dve.wait_ge(sem("bias_row_done"), 1)
            dve.tensor_copy(rrs[0:H, :], bank(0, 0, N_E1)[0:H]).then_inc(sem("bias_read"), 1)
            dve.wait_ge(sem("bias_cmp_done"), 1)
            for i in range(TT_):
                src = bank(1, i * NCMP * H, NCMP * H).rearrange("p (n h) -> p h n", h=H)
                dve.tensor_copy(bcmp[:, i, :, 0:NCMP], src).then_inc(sem("bias_read"), 1)

            dve.wait_ge(sem("x_in"), 16)
            rms_scale(1)
            for i in range(TT_):
                ts(junk[:, i, :], xr[:, i, :], rms[:, 6 + i:7 + i], None, ALU.mult).then_inc(sem("xn_ready"), 1)
            dve.wait_ge(sem("params_in"), 16)
            for f in range(4):
                i, half = f // 2, f % 2
                dve.wait_ge(sem("hT_done"), f + 1)
                tt(hT[:, 4 * half:4 * half + 4, i * P:(i + 1) * P], bank(4 + f).rearrange("p (k t) -> p k t", k=4),
                   each(par_cols(R_NM + 4 * half, 4), P), ALU.mult).then_inc(sem("hT_ready"), 1)

            for n in range(N_GDN):
                dve.wait_ge(sem("proj_evac"), n + 1)
                c0 = R_CW + 4 * n
                link(ts(conv[:, n, :], pad[:, n, 0:T], par[:, c0:c0 + 1], None, ALU.mult))
                for j in range(1, 4):
                    m = stt(out=conv[:, n, :], in0=pad[:, n, j:j + T], scalar=par[:, c0 + j:c0 + j + 1],
                            in1=conv[:, n, :], op0=ALU.mult, op1=ALU.add)
                    if j < 3:
                        link(m)
                m.then_inc(sem("conv_done"), 1)

            tile_done(T_TOK + N_TOK - 1)
            for i in range(TT_):
                dve.tensor_copy(tk[:, i, :], bank(5 + 2 * i, 0, 296)).then_inc(sem("tok_evac"), 1)
            dve.wait_ge(sem("tok_evac"), TT_)
            link(tt(gs, tk[:, :, 32:40], over(par_cols(R_DT, 8), TT_), ALU.add))
            link(ts(gm, gs, 0.0, None, ALU.max))
            stt(out=ge, in0=gs, scalar=-1.0, in1=gs, op0=ALU.mult, op1=ALU.min).then_inc(sem("ge_in"), 1)

            for s in range(2):
                dve.wait_ge(sem("proj_evac"), N_GDN + (8 if s else 5))
                src = nsaf[:, 7 if s else 4, :].rearrange("p (m b) -> p b m", b=16)
                for a in range(2):
                    tt(kcpe[:, s, 16 * a:16 * a + 16, :], src[:, :, a:a + NCMP],
                       each(par_cols(R_PE + 32 * s + 16 * a, 16), NCMP), ALU.add).then_inc(sem("kcpe_ready"), 1)

            dve.wait_ge(sem("tt_evac"), 4)
            for i in range(TT_):
                link(tt(sq[:, i, :], qkvt[:, i, 0:1024], qkvt[:, i, 0:1024], ALU.mult))
                link(dve.tensor_reduce(ssq[:, i, :], sq[:, i, :].rearrange("p (h d) -> p h d", d=DH), AX.X, ALU.add))
            ts(ssq, ssq, EPS, None, ALU.add).then_inc(sem("ssq_ready"), 1)

            dve.wait_ge(sem("ge_out"), 2)
            link(ts(gz, ge, 2.0, None, ALU.add))
            link(dve.reciprocal(gr, gz))
            link(tt(gz, ge, gr, ALU.mult))
            link(tt(gt, gz, gz, ALU.mult))
            link(ts(gp, gt, 1.0 / 17, None, ALU.mult))
            for k in range(15, 1, -2):
                link(stt(out=gp, in0=gp, scalar=1.0 / k, in1=gt, op0=ALU.add, op1=ALU.mult))
            link(stt(out=gp, in0=gp, scalar=1.0, in1=gz, op0=ALU.add, op1=ALU.mult))
            link(stt(out=gp, in0=gp, scalar=2.0, in1=gm, op0=ALU.mult, op1=ALU.add))
            stt(out=gg, in0=gp, scalar=-1.0, in1=over(ea, TT_), op0=ALU.mult, op1=ALU.mult).then_inc(sem("g_ready"), 1)

            dve.wait_ge(sem("rq_root"), 1)
            link(dve.reciprocal(rq, rq))
            link(ts(rq[:, :, 0:8], rq[:, :, 0:8], DH ** -0.5, None, ALU.mult))
            dve.wait_ge(sem("tt_done"), 6)
            dve.wait_ge(sem("sg_ready"), 1)

            def heads(i, part):
                return qkvt[:, i, 512 * part:512 * part + 512].rearrange("p (h d) -> p h d", h=H)

            for i in range(TT_):
                tt(kn[:, i], heads(i, 1), each(rq[:, i, 8:16], DH), ALU.mult).then_inc(sem("gdn_rows_ready"), 1)
            dve.wait_ge(sem("gdn_rows_ready"), 2)
            for i in range(TT_):
                tt(kb[:, i], kn[:, i], each(sg[:, i, 0:8], DH), ALU.mult).then_inc(sem("gdn_rows_ready"), 1)
            for i in range(TT_):
                tt(qn[:, i], heads(i, 0), each(rq[:, i, 0:8], DH), ALU.mult).then_inc(sem("gdn_rows_ready"), 1)
            dve.wait_ge(sem("tt_evac"), 6)
            for i in range(TT_):
                link(tt(vb[:, i], heads(i, 2), each(sg[:, i, 0:8], DH), ALU.mult))
            for i in range(TT_):
                z = zs[:, i, :].rearrange("p (h d) -> p h d", h=H)
                dve.wait_ge(sem("z_evac"), i + 1)
                link(tt(z, z, over(par_cols(R_GN, DH), H), ALU.mult))

            dve.wait_ge(sem("gcl_done"), 1)
            dve.tensor_copy(gcl, bank(4, 0, 32).rearrange("p (i c) -> p i c", i=TT_)).then_inc(sem("gcl_evac"), 1)
            dve.wait_ge(sem("gcl_evac"), 1)
            tt(ekd, gcl[:, :, 8:16], gcl[:, :, 0:8], ALU.subtract).then_inc(sem("ekd_in"), 1)
            link(ts(ngc, gcl[:, :, 0:8], -1.0, None, ALU.mult))
            dve.wait_ge(sem("eg_ready"), 1)
            dve.wait_ge(sem("gdn_rows_ready"), 6)
            for i in range(TT_):
                tt(qd[:, i], qn[:, i], each(eg[:, i, :], DH), ALU.mult).then_inc(sem("gdn_rows_ready"), 1)
            for i in range(TT_):
                dve.wait_ge(sem("gbc_done"), i + 1)
                for h in range(H):
                    m = stt(out=DT[:, i, h, :], in0=bank(4 + (1 + 2 * i + h // 4) % 4, (h % 4) * P, P),
                            scalar=ngc[:, i, h:h + 1], in1=tri, op0=ALU.add, op1=ALU.mult)
                m.then_inc(sem("DT_in"), 1)
            link(ts(neg_eg, eg, -1.0, None, ALU.mult))
            dve.wait_ge(sem("ekd_ready"), 1)
            for i in range(TT_):
                tt(kbg[:, i], kb[:, i], each(neg_eg[:, i, :], DH), ALU.mult)
                link(tt(kd[:, i], kn[:, i], each(ekd[:, i, :], DH), ALU.mult))
            for i in range(TT_):
                dve.wait_ge(sem("DT_exp"), i + 1)
                link(tt(DT[:, i], DT[:, i], over(tri, H), ALU.mult))
            for r in range(8):
                which, i, p = r // 4, (r // 2) % 2, r % 2
                dve.wait_ge(sem("am_done"), r + 1)
                dst = attnT if which else AT
                tt(dst[:, i, p:H:2, :], bank(4 + r % 4).rearrange("p (q t) -> p q t", q=HP), DT[:, i, p:H:2, :],
                   ALU.mult).then_inc(sem("am_evac"), 1)

            for g in range(2):
                rows = slice(DH * g, DH * g + DH)
                tile_done(T_CMP + 1)
                dve.tensor_copy(kcmpT[rows, 0:NCMP], ps[rows, g, 0:NCMP]).then_inc(sem("kvcmp_evac"), 1)
            for g in range(2):
                tile_done(T_CMP + 3)
                dve.tensor_copy(vcs[0:NCMP, g * DH:(g + 1) * DH], ps[0:NCMP, 2 + g, 0:DH]).then_inc(sem("kvcmp_evac"), 1)
            dve.wait_ge(sem("nsa_zero"), 2)
            for i in range(TT_):
                for g in range(2):
                    dve.wait_ge(sem("sc_done"), 2 * i + g + 1)
                    link(stt(out=pc[:, i, 4 * g:4 * g + 4, 0:NCMP],
                             in0=bank(4 + 2 * i + g, 0, 64).rearrange("p (q n) -> p q n", q=4)[:, :, 0:NCMP],
                             scalar=DH ** -0.5, in1=bcmp[:, i, 4 * g:4 * g + 4, 0:NCMP], op0=ALU.mult, op1=ALU.add))
                link(dve.tensor_reduce(cmx[:, i, :], pc[:, i, :, 0:NCMP], AX.X, ALU.max))
                tt(pc[:, i, :, 0:NCMP], pc[:, i, :, 0:NCMP], each(cmx[:, i, :], NCMP), ALU.subtract)\
                    .then_inc(sem("pc_in"), 1)
            for i in range(TT_):
                dve.wait_ge(sem("pc_exp"), i + 1)
                link(dve.tensor_reduce(sums[:, i, :, 0], pc[:, i, :, 0:NCMP], AX.X, ALU.add))
                tt(pc[:, i], pc[:, i], over(cmask[:, i, :], H), ALU.mult).then_inc(sem("pc_ready"), 1)

            def branch_gates(i, b0, b1):
                gates = sg[:, i, 8:32].rearrange("p (h b) -> p h b", h=H)
                link(dve.reciprocal(coef[:, i, :, b0:b1], sums[:, i, :, b0:b1]))
                link(tt(coef[:, i, :, b0:b1], coef[:, i, :, b0:b1], gates[:, :, b0:b1], ALU.mult))

            for i in range(TT_):
                branch_gates(i, 0, 1)
                dve.wait_ge(sem("oc_done"), i + 1)
                tt(onsa[:, i, :].rearrange("p (h d) -> p h d", h=H), bank(2 + i).rearrange("p (h d) -> p h d", h=H),
                   each(coef[:, i, :, 0], DH), ALU.mult).then_inc(sem("oc_evac"), 1)

            dve.wait_ge(sem("BT_in"), 4)
            for n in range(TT_ * H):
                i, h = n // H, n % H
                nk = P * (i + 1)
                dve.wait_ge(sem("s_done"), n + 1)
                if n >= 2:
                    dve.wait_ge(sem("pT_done"), n - 1)
                s = Sb[:, n % 2, 0:2 * nk].rearrange("p (b j) -> p b j", b=2)
                stt(out=s, in0=bank(n % 2, 0, 2 * nk).rearrange("p (b j) -> p b j", b=2), scalar=DH ** -0.5,
                    in1=over(BT[:, h, T - nk:T], 2), op0=ALU.mult, op1=ALU.add).then_inc(sem("s_evac"), 1)
                dve.wait_ge(sem("s_evac"), n + 1)
                dve.tensor_reduce(mx[:, n, :], s, AX.X, ALU.max, negate=True).then_inc(sem("s_ready"), 1)
            dve.wait_ge(sem("pT_done"), TT_ * H)
            dve.wait_ge(sem("pv_done"), TT_ * H)
            for i in range(TT_):
                branch_gates(i, 1, 3)
                for b in range(2):
                    link(tt(Sb[:, b, :].rearrange("p (h d) -> p h d", h=H),
                            bank(4 + 2 * i + b).rearrange("p (h d) -> p h d", h=H),
                            each(coef[:, i, :, 1 + b], DH), ALU.mult))
                link(tt(onsa[:, i, :], onsa[:, i, :], Sb[:, 0, :], ALU.add))
                tt(onsa[:, i, :], onsa[:, i, :], Sb[:, 1, :], ALU.add).then_inc(sem("onsa_ready"), 1)

            for n in range(4 * (N_LEV - 1)):
                g = n % 4
                b0 = 4 + 2 * (g % 2)
                dve.wait_ge(sem("TY_done"), n + 1)
                for b, M, s in ((b0, Tm, "T_ready"), (b0 + 1, TT, "TT_ready")):
                    if s == "T_ready" and n >= 4 * (N_LEV - 2):
                        continue
                    tt(M[:, g], M[:, g], bank(b).rearrange("p (q j) -> p q j", q=HP), ALU.subtract)\
                        .then_inc(sem(s), 1)

            dve.wait_ge(sem("scan_zero"), 2)
            for c in range(T // CH):
                rows = slice(CH * (c % 2), CH * (c % 2) + CH)
                dve.wait_ge(sem("vn_done"), c + 1)
                dve.tensor_copy(vn[rows, :], ps[rows, 2, :]).then_inc(sem("vn_evac"), 1)
                if c == T // CH - 1:
                    continue
                dve.wait_ge(sem("dS_done"), c + 1)
                for p in range(2):
                    hr = slice(DH * p, DH * p + DH)
                    dS = ps[hr, 4, :].rearrange("p (q e) -> p q e", q=HP)[:, :, DH * p:DH * p + DH]
                    Sp = S[hr, :, DH * p:DH * p + DH]
                    link(tt(Sp, Sp, each(egl[hr, c // 2, :, c % 2], DH), ALU.mult))
                    m = tt(Sp, Sp, dS, ALU.add)
                    if p == 0:
                        link(m)
                m.then_inc(sem("S_ready"), 1)

            dve.wait_ge(sem("o_evac"), T // CH)
            dve.wait_ge(sem("TY_done"), 4 * (N_LEV - 1))
            osq = at(0, 1024).rearrange("p (i c) -> p i c", i=TT_)
            link(tt(osq, oa, oa, ALU.mult))
            for i in range(TT_):
                link(dve.tensor_reduce(oss[:, i, :], osq[:, i, :].rearrange("p (h d) -> p h d", h=H), AX.X, ALU.add))
            ts(oss, oss, 1.0 / DH, EPS, ALU.mult, ALU.add).then_inc(sem("oss_ready"), 1)
            dve.wait_ge(sem("osr_root"), 1)
            link(dve.reciprocal(osr, osr))
            for i in range(TT_):
                o3 = oa[:, i, :].rearrange("p (h d) -> p h d", h=H)
                link(tt(o3, o3, each(osr[:, i, :], DH), ALU.mult))
                tt(oa[:, i, :], oa[:, i, :], zs[:, i, :], ALU.mult).then_inc(sem("oa_ready"), 1)

            both = at(0, 512).rearrange("p (s t) -> p s t", s=2)
            for j in range(N_AB):
                tile_done(T_AB + j)
                link(tt(both, bank(j % 4).rearrange("p (s t) -> p s t", s=2), mg[:, j:16:8, :], ALU.mult))
                tt(mixT[:, j, :], both[:, 0, :], both[:, 1, :], ALU.add).then_inc(sem("mix_ready"), 1)
                dve.wait_ge(sem("mix_ready"), j + 1)
            tile_done(T_OUT + N_OUT - 1)
            for i in range(TT_):
                for half in range(2):
                    xh = xr[:, i, 512 * half:512 * half + 512]
                    link(tt(xh, xh, bank(4 + 2 * i + half), ALU.add))
            rms_scale(2)
            for i in range(TT_):
                ts(junk[:, i, :], xr[:, i, :], rms[:, 6 + i:7 + i], None, ALU.mult).then_inc(sem("xn2_ready"), 1)
            for f in range(4):
                i, half = f // 2, f % 2
                dve.wait_ge(sem("h2T_done"), f + 1)
                tt(h2T[:, 4 * half:4 * half + 4, i * P:(i + 1) * P], bank(f).rearrange("p (k t) -> p k t", k=4),
                   each(par_cols(R_NF + 4 * half, 4), P), ALU.mult).then_inc(sem("h2T_ready"), 1)

            def best16(val, idx, src, left):
                link(dve.max(val[:, 0:8], src))
                dve.max_index(idx[:, 0:8], val[:, 0:8], src)
                link(dve.match_replace(left, val[:, 0:8], src, -3e38))
                link(dve.max(val[:, 8:16], left))
                link(dve.max_index(idx[:, 8:16], val[:, 8:16], left))

            dve.wait_ge(sem("key_sc_evac"), 8)
            for i in range(TT_):
                for n in range(2 * H):
                    best16(tkv[:, i, n, :], tki_u[:, i, n, :], sc[:, i, n, :], rep)
            link(dve.tensor_copy(tki, tki_u))
            for i in range(TT_):
                for h in range(H):
                    link(tt(cand.rearrange("p (a b) -> p a b", a=TOPK), each(tkv[:, i, 2 * h, :], TOPK),
                            over(tkv[:, i, 2 * h + 1, :], TOPK), ALU.add))
                    best16(topv[:, i, h, :], topi_u[:, i, h, :], cand, cand2)
            topi_c = topi_u.rearrange("p i h k -> p i (h k)")
            link(ts(ab_u[:, 0], topi_c, 4, None, ALU.logical_shift_right))
            link(ts(ab_u[:, 1], topi_c, 15, None, ALU.bitwise_and))
            link(dve.tensor_copy(ab_f, ab_u))
            for s in range(2):
                for i in range(TT_):
                    link(tt(oh, each(ab_f[:, s, i, :], TOPK), over(iota[:, 0:TOPK], P), ALU.is_equal))
                    oh4 = oh.rearrange("p (h k) a -> p h k a", h=H)
                    keys = tki[:, i, s:2 * H:2, :].unsqueeze(2).broadcast_to([P, H, TOPK, TOPK])
                    link(tt(oh4, oh4, keys, ALU.mult))
                    link(dve.tensor_reduce(e_f[:, s, i, :], oh, AX.X, ALU.add))
            for i in range(TT_):
                tt(gate[:, i], topv[:, i], each(topv[:, i, :, 0], TOPK), ALU.subtract).then_inc(sem("gate_in"), 1)
            dve.wait_ge(sem("gate_exp"), TT_)
            gsum = gs
            link(dve.tensor_reduce(gsum, gate, AX.X, ALU.add))
            link(dve.reciprocal(gr, gsum))
            link(tt(gate[:, 0], gate[:, 0], each(gr[:, 0, :], TOPK), ALU.mult))
            tt(gate[:, 1], gate[:, 1], each(gr[:, 1, :], TOPK), ALU.mult).then_inc(sem("choice_ready"), 1)

            dve.wait_ge(sem("egT_read"), 1)
            dve.wait_ge(sem("u_evac"), NKEYS + 4)
            dve.sem_inc(sem("weighed"), 4)
            with dve.Fori(0, T // 16, 1) as group:
                for q in range(4):
                    dve.wait_ge(sem("G_done"), group * 4 + (q + 1))
                    for j in range(4):
                        t = 4 * q + j
                        m = ts(ohA[:, t, :], iota, egT[:, 0, bass.ds(group * 16 + t, 1)],
                               egT[:, 2, bass.ds(group * 16 + t, 1)], ALU.is_equal, ALU.mult)
                    m.then_inc(sem("ohA_ready"), 1)
                for q in range(4):
                    dve.wait_ge(sem("G_done"), group * 4 + (q + 5))
                    aw = act_w[:, :, bass.ds(group * 16 + 4 * q, 4)]
                    tt(aw, aw, bank(q).rearrange("p (t e) -> p e t", t=4), ALU.mult).then_inc(sem("weighed"), 1)

            for i in range(TT_):
                for half in range(2):
                    dve.wait_ge(sem("peer_done"), 2 * i + half + 1)
                    xh = xr[:, i, 512 * half:512 * half + 512]
                    link(tt(xh, xh, bank(2 * i + half), ALU.add))
            rms_scale(3)
            dve.wait_ge(sem("nfinal_in"), 16)
            for i in range(TT_):
                stt(out=xr[:, i, :], in0=xr[:, i, :], scalar=rms[:, 6 + i:7 + i], in1=nfin, op0=ALU.mult,
                    op1=ALU.mult).then_inc(sem("out_ready"), 1)

        @block.gpsimd
        def _(pool):
            pool.memset(pad[:, :, 0:3], 0.0).then_inc(sem("pad_zero"), 1)
            pool.memset(pc, 0.0).then_inc(sem("nsa_zero"), 1)
            pool.memset(vcbd, 0.0).then_inc(sem("nsa_zero"), 1)
            pool.wait_ge(sem("bias_read"), 1)
            pool.dma_start(bias_scratch, rrs[0:H, :]).then_inc(sem("bias_row_out"), 16)
            pool.wait_ge(sem("consts_in"), 16)
            pool.wait_ge(sem("bias_cmp_done"), 1)
            pool.wait_ge(sem("g_ready"), 1)
            for i in range(TT_):
                for h in range(H):
                    m = pool.tensor_scalar(grhs[:, i, h, :], tri, gg[:, i, h:h + 1], None, ALU.mult)
                m.then_inc(sem("grhs_ready"), 1)
            pool.wait_ge(sem("bias_row_out"), 16)
            pool.wait_ge(sem("tiles_used"), T_CMP)
            pool.dma_start(BTrev, bass.AP(bias_scratch.tensor, 0, [[1, P], [N_E1, H], [1, T]]))\
                .then_inc(sem("BTrev_in"), 16)
            pool.wait_ge(sem("kvcmp_evac"), 4)
            pool.wait_ge(sem("nsa_zero"), 2)
            for h in range(H):
                g = h // 4
                pool.dma_start(vcbd[16 * h:16 * h + NCMP, h * DH:(h + 1) * DH], vcs[0:NCMP, g * DH:(g + 1) * DH])\
                    .then_inc(sem("vcbd_in"), 16)
            pool.wait_ge(sem("am_evac"), 4)
            for g in range(4):
                i, p = g // 2, g % 2
                pool.tensor_tensor(TT[:, g], AT[:, i, p:H:2, :], over(level[:, 0, :], HP), ALU.mult)\
                    .then_inc(sem("TT0_part"), 1)
                pool.wait_ge(sem("TT0_part"), g + 1)
                pool.tensor_tensor(TT[:, g], over(ident, HP), TT[:, g], ALU.subtract).then_inc(sem("TT0_ready"), 1)
            pool.wait_ge(sem("gbc_done"), TT_)
            for lv in range(1, N_LEV):
                for g in range(4):
                    i, p = g // 2, g % 2
                    if lv >= 2:
                        pool.wait_ge(sem("Y_done"), (lv - 2) * 4 + g + 1)
                    pool.tensor_tensor(AbT[:, g], AT[:, i, p:H:2, :], over(level[:, lv, :], HP), ALU.mult)\
                        .then_inc(sem("AbT_ready"), 1)
            pool.wait_ge(sem("Y_done"), 4 * (N_LEV - 1))
            pool.memset(vn, 0.0).then_inc(sem("scan_zero"), 1)
            pool.memset(S, 0.0).then_inc(sem("scan_zero"), 1)
            pool.wait_ge(sem("u_evac"), NKEYS + 4)
            pool.dma_start(nfin, nfinal.partition_broadcast(P)).then_inc(sem("nfinal_in"), 16)
            pool.wait_ge(sem("egT_read"), 1)
            with pool.Fori(0, T // 16, 1) as group:
                pool.tensor_copy(k2s, egT[:, 1, bass.ds(group * 16, 16)]).then_inc(sem("k2_here"), 1)
                pool.wait_ge(sem("k2_here"), group + 1)
                for hb in range(2):
                    pool.wait_ge(sem("G_done"), group * 4 + (2 * hb + 2))
                    pool.sem_inc(sem("ohB_free"), 1)
                    for t in range(8 * hb, 8 * hb + 8):
                        m = pool.tensor_scalar(ohB[:, t, :], iota, k2s[:, t:t + 1], None, ALU.is_equal)
                    m.then_inc(sem("ohB_ready"), 1)
                pool.wait_ge(sem("ohB_ready"), group * 2 + 2)
                pool.sem_inc(sem("k2_free"), 1)


def _constants():
    import math
    import numpy as np
    k = np.arange(P)[:, None]
    i = np.arange(P)[None, :]
    chunk = (k // CH) == (i // CH)
    c = np.zeros((P, N_CONST), np.float32)
    c[:, C_ID:C_ID + P] = np.eye(P)
    c[:, C_TRI:C_TRI + P] = chunk & (k <= i)
    c[:, C_SAME:C_SAME + P] = chunk
    c[:, C_ONES:C_ONES + P] = 1.0
    c[:, C_IOTA:C_IOTA + P] = i
    c[:, C_FLIP:C_FLIP + P] = (k + i) == P - 1
    for lv in range(N_LEV):
        b = 1 << lv
        c[:, C_LEV + lv * P:C_LEV + (lv + 1) * P] = (k // (2 * b) == i // (2 * b)) & ((i // b) % 2 == 1) & ((k // b) % 2 == 0)
    for t in range(TT_):
        for n in range(NCMP):
            c[:, C_CMASK + 16 * t + n] = (16 * n + 31) <= (np.arange(P) + P * t)

    def bucket(d):
        far = 16 + int(np.float32(np.log(np.float32(max(d, 1) / 16))) / np.float32(math.log(8.0)) * np.float32(16))
        return d if d < 16 else min(far, 31)

    e = np.zeros((33, N_E1 + N_E2), np.float32)
    for m in range(N_E1):
        d = T - 1 - m
        e[bucket(d) if d >= 0 else 32, m] = 1.0
    for m in range(N_E2):
        d = m - (T - 1)
        e[bucket(d) if d >= 0 else 32, N_E1 + m] = 1.0
    return c, e


def _layout(a):
    import numpy as np
    w_in = a["w_in"][0]
    stream = np.zeros((N_TILES, P, 1024), np.float32)

    def by_columns(w, cols, first):
        n = len(cols) // P
        t = w[:, cols].reshape(KT, P, n, P)
        stream[first:first + n] = t.transpose(2, 1, 0, 3).reshape(n, P, 1024)

    z0, b0, d0, q0, kv0, g0, m0 = 1536, 2048, 2056, 2064, 2576, 3344, 3368
    ar = np.arange
    by_columns(w_in, ar(0, 1536), T_GDN)
    v_cols = [ar(kv0 + ((b * 2 + 1) * 2) * DH, kv0 + ((b * 2 + 1) * 2) * DH + P) for b in (1, 2)]
    tok = np.concatenate([ar(z0, z0 + 512), ar(b0, b0 + 8), ar(g0, g0 + 24), ar(d0, d0 + 8)] + v_cols)
    stream[T_TOK:T_TOK + KT, :, 0:len(tok)] = w_in[:, tok].reshape(KT, P, len(tok))
    q_cols = [ar(q0 + h * DH, q0 + (h + 1) * DH) for m in range(4) for h in (m, m + 4)]
    k_cols = [ar(kv0 + (b * 2 * 2) * DH, kv0 + (b * 2 * 2) * DH + P) for b in range(3)]
    by_columns(w_in, np.concatenate(q_cols + k_cols + [ar(kv0 + 2 * DH, kv0 + 4 * DH)]), T_NSA)
    by_columns(w_in, ar(m0, m0 + 2048), T_MERGE)
    for s, name in enumerate(("cmp_w_k", "cmp_w_v")):
        w = a[name][0].transpose(1, 0, 2).reshape(DH, 2, 1024).transpose(1, 0, 2)
        stream[T_CMP + 2 * s:T_CMP + 2 * s + 2] = np.concatenate([w, w], axis=1)
    for s, name in enumerate(("w_branch_a", "w_branch_b")):
        w = a[name][0].reshape(HP, P, N_AB, P).transpose(2, 1, 0, 3).reshape(N_AB, P, 512)
        stream[T_AB:T_AB + N_AB, :, 512 * s:512 * s + 512] = w
    stream[T_OUT:T_OUT + N_OUT] = a["w_out"][0].reshape(N_OUT, P, D)
    by_columns(a["w_query"][0], ar(2048), T_WQ)
    sk = a["sub_keys"][0].reshape(N_SK, 8, P, P).transpose(0, 3, 1, 2).reshape(N_SK, P, 1024)
    stream[T_SK:T_SK + N_SK] = sk
    u = a["expert_u"][0].reshape(NKEYS, NKEYS, KT, P)
    stream[T_U:T_U + NKEYS] = u.transpose(1, 3, 2, 0).reshape(NKEYS, P, 1024)
    stream[T_V:T_V + NKEYS] = a["expert_v"][0].reshape(NKEYS, NKEYS, D).transpose(1, 0, 2)

    par = np.zeros((P, N_PAR), np.float32)
    par[:, R_NM:R_NM + 8] = a["norm_mix"][0].reshape(8, P).T
    par[:, R_NF:R_NF + 8] = a["norm_ffn"][0].reshape(8, P).T
    par[:, R_CW:R_CW + 48] = a["conv_w"][0].reshape(4, 12, P).transpose(2, 1, 0).reshape(P, 48)
    for s, name in enumerate(("cmp_pe_k", "cmp_pe_v")):
        pe = a[name][0].T
        par[:, R_PE + 32 * s:R_PE + 32 * s + 32] = np.concatenate([pe, pe], axis=0)
    par[:, R_ALOG:R_ALOG + 8] = a["a_log"][0][None, :]
    par[:, R_DT:R_DT + 8] = a["dt_bias"][0][None, :]
    par[:, R_GN:R_GN + DH] = a["gdn_norm"][0][None, :]
    relb = np.concatenate([a["rel_bias"], np.full((1, H), NEG, np.float32)], axis=0)
    consts, onehot = _constants()
    return {"x": a["x"][0], "stream": stream, "consts": consts, "params": par, "onehot": onehot,
            "relb": relb, "nfinal": a["norm_final"]}


def kernel(**inputs):
    import numpy as np
    import concourse.bacc as bacc
    from concourse.bass_utils import run_bass_kernel_spmd
    arrays = _layout({k: np.asarray(v) for k, v in inputs.items()})
    nc = bacc.Bacc("TRN2", target_bir_lowering=False, num_devices=1)
    aps = {k: nc.dram_tensor("in_" + k, v.shape, F32, kind="ExternalInput").ap() for k, v in arrays.items()}
    out = nc.dram_tensor("out", (T, D), F32, kind="ExternalOutput").ap()
    scratch = nc.dram_tensor("bias_scratch", (H, N_E1), F32, kind="Internal").ap()
    build(nc, bias_scratch=scratch, out=out, **aps)
    r = run_bass_kernel_spmd(nc, [{"in_" + k: np.ascontiguousarray(v) for k, v in arrays.items()}], core_ids=[0])
    return r.results[0]["out"].reshape(1, T, D)
```

```python
from contextlib import ExitStack

import concourse.bass as bass
from concourse import mybir

P = 128
T = 256
TT_ = T // P
D = 1024
KT = D // P
H = 8
HP = H // 2
DH = 64
CH = 64
NSLOT = 4
NKEYS = 128
TOPK = 16
NCMP = (T - 32) // 16 + 1
EPS = 1e-6
NEG = -1e30

N_GDN, N_TOK, N_NSA, N_MERGE, N_CMP, N_AB, N_OUT, N_WQ, N_SK = 12, 8, 8, 16, 4, 8, 8, 16, 2
T_GDN = 0
T_TOK = T_GDN + N_GDN
T_NSA = T_TOK + N_TOK
T_MERGE = T_NSA + N_NSA
T_CMP = T_MERGE + N_MERGE
T_AB = T_CMP + N_CMP
T_OUT = T_AB + N_AB
T_WQ = T_OUT + N_OUT
T_SK = T_WQ + N_WQ
T_U = T_SK + N_SK
T_V = T_U + NKEYS
N_TILES = T_V + NKEYS
GROUP = 8
HALF = NKEYS // 2

SPLIT = ([T_GDN + n for n in range(N_GDN)] + [T_NSA + n for n in range(N_NSA)]
         + [T_MERGE + n for n in range(N_MERGE)] + [T_WQ + n for n in range(N_WQ)])
M_U = len(SPLIT)
SPLIT = SPLIT + list(range(T_U, N_TILES))

C_ID, C_TRI, C_SAME, C_ONES, C_IOTA, C_LEV = 0, 128, 256, 384, 512, 640
N_LEV = 6
C_CMASK = C_LEV + N_LEV * 128
C_FLIP = C_CMASK + 32
N_CONST = C_FLIP + 128
R_NM, R_NF, R_CW, R_PE, R_ALOG, R_DT, R_GN = 0, 8, 16, 64, 128, 136, 144
N_PAR = 208
N_E1, N_E2 = 384, 511

F32 = mybir.dt.float32
F32R = mybir.dt.float32r
U32 = mybir.dt.uint32
ALU = mybir.AluOpType
ACT = mybir.ActivationFunctionType
AX = mybir.AxisListType


def build(nc, x, stream, consts, params, onehot, relb, nfinal, bias_scratch, out, debug=None):
    ctx = ExitStack()
    with ctx:
        def sb(name, shape, dt=F32):
            return ctx.enter_context(nc.sbuf_tensor(name, shape, dt))

        semaphores = {}

        def sem(name):
            if name not in semaphores:
                semaphores[name] = ctx.enter_context(nc.semaphore(name))
            return semaphores[name]

        ring = sb("ring", [P, NSLOT, 1024])
        xr = sb("xr", [P, TT_, D])
        cst = sb("cst", [P, N_CONST])
        par = sb("par", [P, N_PAR])
        small = sb("small", [P, 640])
        arena = sb("arena", [P, 35200])
        wsplit = sb("wsplit", [P, 2, 2, 1024], F32R)
        hsplit = sb("hsplit", [P, 2, KT, T], F32R)
        asplit = sb("asplit", [P, 2, 2, T], F32R)
        ps = ctx.enter_context(nc.psum_tensor("ps", [P, 8, 512], F32))

        def at(off, n):
            return arena[:, off:off + n]

        ident = cst[:, C_ID:C_ID + P]
        tri = cst[:, C_TRI:C_TRI + P]
        same = cst[:, C_SAME:C_SAME + P]
        ones = cst[:, C_ONES:C_ONES + P]
        iota = cst[:, C_IOTA:C_IOTA + P]
        level = cst[:, C_LEV:C_LEV + N_LEV * P].rearrange("p (l j) -> p l j", l=N_LEV)
        flip = cst[:, C_FLIP:C_FLIP + P]
        cmask = cst[:, C_CMASK:C_CMASK + 32].rearrange("p (i n) -> p i n", i=TT_)

        hT = at(0, 2048).rearrange("p (k t) -> p k t", k=KT)
        Yb = at(0, 2048).rearrange("p (g h j) -> p g h j", g=4, h=HP)
        pad = at(2048, 12 * 259).rearrange("p (n t) -> p n t", n=12)
        conv = at(5160, 3072).rearrange("p (n t) -> p n t", n=12)
        kn, kb, qn, qd, kbg, vb = [
            at(2048 + 1024 * n, 1024).rearrange("p (i h d) -> p i h d", i=TT_, h=H) for n in range(6)]
        qkvt = at(8448, 3072).rearrange("p (i c) -> p i c", i=TT_)
        Tm = at(8448, 2048).rearrange("p (g h j) -> p g h j", g=4, h=HP)
        vn = at(8448, 512)
        S = at(8960, 512).rearrange("p (q e) -> p q e", q=HP)
        oaT = at(9472, 1024).rearrange("p (k t) -> p k t", k=HP)
        nsaf = at(11520, 2048).rearrange("p (n t) -> p n t", n=8)
        mg = at(13568, 4096).rearrange("p (n t) -> p n t", n=16)
        zs = at(17664, 1024).rearrange("p (i c) -> p i c", i=TT_)
        tk = at(18688, 592).rearrange("p (i c) -> p i c", i=TT_)
        BT = at(19328, 2048).rearrange("p (h j) -> p h j", h=H)
        BTrev = at(0, 2048).rearrange("p (h j) -> p h j", h=H)
        XT = at(21376, 4096).rearrange("p (x i q t) -> p x i q t", x=4, i=TT_, q=HP)
        onsa = at(21376, 1024).rearrange("p (i c) -> p i c", i=TT_)
        obT = at(22400, 1024).rearrange("p (k t) -> p k t", k=HP)
        oa = at(23424, 1024).rearrange("p (i c) -> p i c", i=TT_)
        qdT = XT[:, 3]
        DT = at(25472, 2048).rearrange("p (i h t) -> p i h t", i=TT_, h=H)
        nwT = at(25472, 1024).rearrange("p (i q t) -> p i q t", i=TT_, q=HP)
        AT = at(27520, 2048).rearrange("p (i h t) -> p i h t", i=TT_, h=H)
        mixT = at(27520, 2048).rearrange("p (k t) -> p k t", k=KT)
        attnT = at(29568, 2048).rearrange("p (i h t) -> p i h t", i=TT_, h=H)
        TT = at(31616, 2048).rearrange("p (g h j) -> p g h j", g=4, h=HP)
        AbT = at(4096, 2048).rearrange("p (g h j) -> p g h j", g=4, h=HP)
        grhs = at(27520, 2048).rearrange("p (i h t) -> p i h t", i=TT_, h=H)
        kd = at(33664, 1024).rearrange("p (i h d) -> p i h d", i=TT_, h=H)
        kd_f = at(33664, 1024).rearrange("p (i c) -> p i c", i=TT_)
        Sb = at(3072, 1024).rearrange("p (b j) -> p b j", b=2)
        PT = at(26496, 1024).rearrange("p (b j) -> p b j", b=2)
        vcbd = at(10496, 512)
        kcmpT = at(11008, 16)
        vcs = at(11024, 128)
        bcmp = at(34688, 256).rearrange("p (i h n) -> p i h n", i=TT_, h=H)
        pc = at(34944, 256).rearrange("p (i h n) -> p i h n", i=TT_, h=H)
        pc_f = at(34944, 256).rearrange("p (i c) -> p i c", i=TT_)
        pcT = at(11152, 256).rearrange("p (i t) -> p i t", i=TT_)
        rrs = at(32600, 384)
        E = at(25472, N_E1 + N_E2)
        kcpe = at(31616, 960).rearrange("p (s l n) -> p s l n", s=2, l=32)
        junk = at(27520, 2048).rearrange("p (i c) -> p i c", i=TT_)
        sq = at(29568, 2048).rearrange("p (i c) -> p i c", i=TT_)

        act_w = at(0, NKEYS * T).rearrange("p (e t) -> p e t", e=NKEYS)
        qT = at(16384, 4096).rearrange("p (n t) -> p n t", n=16)
        sc = at(20480, 4096).rearrange("p (i n k) -> p i n k", i=TT_, n=16)
        oh = at(24576, 2048).rearrange("p (m a) -> p m a", a=TOPK)
        tkv = at(26624, 512).rearrange("p (i n k) -> p i n k", i=TT_, n=16)
        tki = at(27136, 512).rearrange("p (i n k) -> p i n k", i=TT_, n=16)
        tki_u = at(27648, 512).bitcast(U32).rearrange("p (i n k) -> p i n k", i=TT_, n=16)
        rep = at(28160, 128)
        cand = at(28288, 256)
        cand2 = at(28544, 256)
        topv = at(28800, 256).rearrange("p (i h k) -> p i h k", i=TT_, h=H)
        topi_u = at(29056, 256).bitcast(U32).rearrange("p (i h k) -> p i h k", i=TT_, h=H)
        ab_u = at(29312, 512).bitcast(U32).rearrange("p (s i c) -> p s i c", s=2, i=TT_)
        ab_f = at(29824, 512).rearrange("p (s i c) -> p s i c", s=2, i=TT_)
        e_f = at(33536, 512).rearrange("p (s i c) -> p s i c", s=2, i=TT_)
        gate = at(34048, 256).rearrange("p (i h k) -> p i h k", i=TT_, h=H)
        gate_f = at(34048, 256).rearrange("p (i c) -> p i c", i=TT_)
        h2T = at(0, 2048).rearrange("p (k t) -> p k t", k=KT)
        egT = at(32768, 768).rearrange("p (s t) -> p s t", s=3)
        g2 = at(33536, 2 * T).rearrange("p (t x) -> p t x", x=2)
        nfin = at(34048, 1024)
        G_lo = cst[:, C_LEV:C_LEV + 512].rearrange("p (b t e) -> p b t e", b=2, t=4)
        peerT = at(0, 2048).rearrange("p (k t) -> p k t", k=KT)

        def sm(off, n):
            return small[:, off:off + n]

        rms = sm(0, 8)
        sg = sm(8, 64).rearrange("p (i c) -> p i c", i=TT_)
        ga_ = sm(72, 16).rearrange("p (i h) -> p i h", i=TT_)
        gm = sm(88, 16).rearrange("p (i h) -> p i h", i=TT_)
        ge = sm(104, 16).rearrange("p (i h) -> p i h", i=TT_)
        gz = sm(120, 16).rearrange("p (i h) -> p i h", i=TT_)
        gt = sm(136, 16).rearrange("p (i h) -> p i h", i=TT_)
        gp = sm(152, 16).rearrange("p (i h) -> p i h", i=TT_)
        gg = sm(168, 16).rearrange("p (i h) -> p i h", i=TT_)
        ea = sm(184, 8)
        gcl = sm(192, 32).rearrange("p (i c) -> p i c", i=TT_)
        ngc = sm(224, 16).rearrange("p (i h) -> p i h", i=TT_)
        eg = sm(240, 16).rearrange("p (i h) -> p i h", i=TT_)
        neg_eg = sm(256, 16).rearrange("p (i h) -> p i h", i=TT_)
        ekd = sm(272, 16).rearrange("p (i h) -> p i h", i=TT_)
        egl = sm(288, 16).rearrange("p (i q c) -> p i q c", i=TT_, q=HP)
        ssq = sm(304, 32).rearrange("p (i c) -> p i c", i=TT_)
        rq = sm(336, 32).rearrange("p (i c) -> p i c", i=TT_)
        mx = sm(368, 32).rearrange("p (n b) -> p n b", n=16)
        sums = sm(400, 48).rearrange("p (i h b) -> p i h b", i=TT_, h=H)
        coef = sm(448, 48).rearrange("p (i h b) -> p i h b", i=TT_, h=H)
        cmx = sm(496, 16).rearrange("p (i h) -> p i h", i=TT_)
        gs = sm(512, 16).rearrange("p (i h) -> p i h", i=TT_)
        gr = sm(528, 16).rearrange("p (i h) -> p i h", i=TT_)
        oss = sm(544, 16).rearrange("p (i h) -> p i h", i=TT_)
        osr = sm(560, 16).rearrange("p (i h) -> p i h", i=TT_)
        rel = sm(576, 8)

        def par_cols(off, n):
            return par[:, off:off + n]

        def bank(b, a=0, n=512):
            return ps[:, b, a:a + n]

        def slot(n):
            return ring[:, n % NSLOT, :]

        def each(ap, n):
            return ap.unsqueeze(2).broadcast_to([ap.shape[0], ap.shape[1], n])

        def over(ap, n):
            return ap.unsqueeze(1).broadcast_to([ap.shape[0], n, ap.shape[1]])

        ohA = [asplit[:, 0].rearrange("p a (t j) -> p (a t) j", j=P),
               hsplit[:, 0, 0:2].rearrange("p a (t j) -> p (a t) j", j=P)]
        ohB = [asplit[:, 1].rearrange("p a (t x j) -> p (a t) x j", x=2, j=HALF),
               hsplit[:, 1, 0:2].rearrange("p a (t x j) -> p (a t) x j", x=2, j=HALF)]

        block = ctx.enter_context(nc.Block())

        @block.sync
        def _(sp):
            sp.dma_start(xr[:, :, :], x.rearrange("(i p) d -> p i d", p=P)).then_inc(sem("x_in"), 16)
            sp.dma_start(cst[:, :], consts).then_inc(sem("consts_in"), 16)
            sp.dma_start(par[:, :], params).then_inc(sem("params_in"), 16)
            sp.dma_start(E[0:33, :], onehot).then_inc(sem("onehot_in"), 16)
            sp.dma_start(rel[0:33, :], relb).then_inc(sem("onehot_in"), 16)
            def load(n):
                sp.dma_start(slot(n), stream[n]).then_inc(sem(f"slot{n % NSLOT}_in"), 16)

            for n in range(T_U + NSLOT):
                if n >= NSLOT:
                    old = n - NSLOT
                    if old in SPLIT:
                        sp.wait_ge(sem("lo_ready"), 2 * SPLIT.index(old) + 2)
                    else:
                        sp.wait_ge(sem("tiles_used"), old + 1)
                load(n)
            with sp.Fori(0, (N_TILES - T_U) // NSLOT - 1, 1) as turn:
                for s in range(NSLOT):
                    n = T_U + NSLOT + s
                    sp.wait_ge(sem("lo_ready"), turn * (2 * NSLOT) + 2 * (M_U + s + 1))
                    sp.dma_start(slot(n), stream[turn * NSLOT + n]).then_inc(sem(f"slot{n % NSLOT}_in"), 16)
            sp.wait_ge(sem("out_ready"), TT_)
            sp.dma_start(out.rearrange("(i p) d -> p i d", p=P), xr[:, :, :]).then_inc(sem("stored"), 16)
            sp.wait_ge(sem("stored"), 16)

        @block.tensor
        def _(pe):
            def mm(o, lhsT, rhs, start=True, stop=True):
                return pe.matmul(o, lhsT, rhs, start=start, stop=stop, skip_group_check=True)

            def arrived(n):
                pe.wait_ge(sem(f"slot{n % NSLOT}_in"), 16 * (n // NSLOT + 1))

            pe.wait_ge(sem("consts_in"), 16)
            for i in range(TT_):
                pe.wait_ge(sem("xn_ready"), i + 1)
                for half in range(2):
                    for j in range(4):
                        k = half * 4 + j
                        m = pe.transpose(bank(4 + 2 * i + half, j * P, P), junk[:, i, k * P:(k + 1) * P], ident)
                    m.then_inc(sem("hT_done"), 1)

            def by_h(b, ms, past=0):
                for half in range(2):
                    pe.wait_ge(sem("lo_ready"), past * 2 + (2 * ms + half + 1))
                    ks = range(4 * half, 4 * half + 4)
                    for a, c in ((0, 0), (1, 0), (0, 1)):
                        for k in ks:
                            m = mm(bank(b, 0, T), wsplit[:, ms % 2, a, k * P:(k + 1) * P], hsplit[:, c, k, :],
                                   start=(half == 0 and a == 0 and c == 0 and k == 0), stop=(half == 1 and c == 1 and k == KT - 1))
                    m.then_inc(sem("tiles_used" if half else "half_used"), 1)

            def project(n, tile):
                if n >= 4:
                    pe.wait_ge(sem("proj_evac"), n - 3)
                by_h(n % 4, SPLIT.index(tile))

            pe.wait_ge(sem("hT_split"), 4)
            for n in range(N_GDN):
                project(n, T_GDN + n)
            for k in range(N_TOK):
                arrived(T_TOK + k)
                w = slot(T_TOK + k)
                for i in range(TT_):
                    h_t = hT[:, k, i * P:(i + 1) * P]
                    mm(bank(4 + 2 * i), h_t, w[:, 0:512], start=(k == 0), stop=(k == KT - 1))
                    m = mm(bank(5 + 2 * i, 0, 296), h_t, w[:, 512:808], start=(k == 0), stop=(k == KT - 1))
                m.then_inc(sem("tiles_used"), 1)
            for n in range(N_NSA):
                project(N_GDN + n, T_NSA + n)

            for f in range(6):
                part, i = f // 2, f % 2
                pe.wait_ge(sem("silu_done"), 4 * (part + 1))
                pe.wait_ge(*[(sem("z_evac"), 1), (sem("tok_evac"), 1), (sem("z_evac"), 2), (sem("tok_evac"), 2),
                             (sem("tt_evac"), 1), (sem("tt_evac"), 2)][f])
                for j in range(4):
                    m = pe.transpose(bank(4 + f % 4, j * P, P), conv[:, part * 4 + j, i * P:(i + 1) * P], ident)
                m.then_inc(sem("tt_done"), 1)

            project(N_GDN + N_NSA, T_MERGE)
            pe.wait_ge(sem("onehot_in"), 32)
            pe.wait_ge(sem("tt_evac"), 6)
            mm(bank(4, 0, N_E1)[0:H], rel[0:33, :], E[0:33, 0:N_E1]).then_inc(sem("bias_row_done"), 1)
            for i in range(TT_):
                for n in range(NCMP):
                    k = N_E1 + 224 - 16 * n + P * i
                    m = mm(bank(5, (i * NCMP + n) * H, H), E[0:33, k:k + P], rel[0:33, :],
                           start=(i == 0 and n == 0))
            m.then_inc(sem("bias_cmp_done"), 1)

            for n in range(1, N_MERGE):
                project(N_GDN + N_NSA + n, T_MERGE + n)

            pe.wait_ge(sem("g_ready"), 1)
            pe.wait_ge(sem("bias_read"), 3)
            for i in range(TT_):
                mm(bank(4, 16 * i, 8), tri, gg[:, i, :], start=(i == 0))
                m = mm(bank(4, 16 * i + 8, 8), same, gg[:, i, :], start=False)
            m.then_inc(sem("gcl_done"), 1)
            for i in range(TT_):
                pe.wait_ge(sem("grhs_ready"), i + 1)
                for half in range(2):
                    if i == 1 and half == 1:
                        pe.wait_ge(sem("gcl_evac"), 1)
                    m = mm(bank(4 + (1 + 2 * i + half) % 4), ones, grhs[:, i, 4 * half:4 * half + 4, :])
                m.then_inc(sem("gbc_done"), 1)

            pe.wait_ge(sem("proj_evac"), N_GDN + N_NSA + N_MERGE)
            for f in range(8):
                which, i = f // 2, f % 2
                pe.wait_ge(sem("gdn_rows_ready"), f + 1)
                if f >= 4:
                    pe.wait_ge(sem("fT_evac"), f - 3)
                src = at(2048 + 1024 * which, 1024).rearrange("p (i c) -> p i c", i=TT_)
                for q in range(HP):
                    m = pe.transpose(bank(f % 4, q * P, P), src[:, i, q * P:(q + 1) * P], ident)
                m.then_inc(sem("fT_done"), 1)

            pe.wait_ge(sem("gbc_read"), 2)
            pe.wait_ge(sem("DT_in"), 2)
            pe.wait_ge(sem("fT_evac"), 8)
            for r in range(8):
                which, i, p = r // 4, (r // 2) % 2, r % 2
                if r >= 4:
                    pe.wait_ge(sem("am_evac"), r - 3)
                rows = slice(DH * p, DH * p + DH)
                for q in range(HP):
                    m = mm(bank(4 + r % 4, q * P, P), XT[rows, 0, i, q, :], XT[rows, 1 + which, i, q, :],
                           start=(q == 0))
                m.then_inc(sem("am_done"), 1)

            pe.wait_ge(sem("kcpe_ready"), 4)
            for s in range(2):
                for half in range(2):
                    tile = T_CMP + 2 * s + half
                    arrived(tile)
                    w = slot(tile).rearrange("p (l e) -> p l e", l=16)
                    for g in range(2):
                        rows = slice(DH * g, DH * g + DH)
                        for l in range(16):
                            ll = half * 16 + l
                            if s == 0:
                                m = mm(ps[rows, g, 0:NCMP], w[rows, l, :], kcpe[rows, 0, ll, :],
                                       start=(ll == 0), stop=(ll == 31))
                            else:
                                m = mm(ps[0:NCMP, 2 + g, 0:DH], kcpe[rows, 1, ll, :], w[rows, l, :],
                                       start=(ll == 0), stop=(ll == 31))
                    m.then_inc(sem("tiles_used"), 1)

            pe.wait_ge(sem("kvcmp_evac"), 4)
            pe.wait_ge(sem("am_evac"), 8)
            for i in range(TT_):
                for g in range(2):
                    rows = slice(DH * g, DH * g + DH)
                    for q in range(4):
                        m = mm(bank(4 + 2 * i + g, q * 16, NCMP), nsaf[rows, q, i * P:(i + 1) * P],
                               kcmpT[rows, 0:NCMP], start=(q == 0))
                    m.then_inc(sem("sc_done"), 1)
            pe.wait_ge(sem("BTrev_in"), 16)
            for b in range(4):
                mm(bank(b), flip, BTrev[:, 2 * b:2 * b + 2, :]).then_inc(sem("BT_done"), 1)
            pe.wait_ge(sem("BT_in"), 4)
            pe.wait_ge(sem("vcbd_in"), 16 * H)
            for i in range(TT_):
                pe.wait_ge(sem("pc_ready"), i + 1)
                pe.transpose(bank(i, 0, P), pc_f[:, i, :], ident).then_inc(sem("pcT_done"), 1)
            for i in range(TT_):
                pe.wait_ge(sem("pcT_evac"), i + 1)
                mm(bank(2 + i), pcT[:, i, :], vcbd).then_inc(sem("oc_done"), 1)

            def nsa_scores(n):
                i, h = n // H, n % H
                nk = P * (i + 1)
                if n < 2:
                    pe.wait_ge(sem("pcT_evac"), n + 1)
                else:
                    pe.wait_ge(sem("s_evac"), n - 1)
                rows = slice(DH * (h // 4), DH * (h // 4) + DH)
                for b in range(2):
                    m = mm(bank(n % 2, b * nk, nk), nsaf[rows, h % 4, i * P:(i + 1) * P],
                           nsaf[rows, 5 + b, 0:nk], start=(b == 0))
                m.then_inc(sem("s_done"), 1)

            def nsa_transpose(n):
                i = n // H
                pe.wait_ge(sem("p_ready"), n + 1)
                if n < 2:
                    pe.wait_ge(sem("oc_evac"), n + 1)
                else:
                    pe.wait_ge(sem("pT_evac"), n - 1)
                for j in range(2 * (i + 1)):
                    m = pe.transpose(bank(2 + n % 2, j * P, P), Sb[:, n % 2, j * P:(j + 1) * P], ident)
                m.then_inc(sem("pT_done"), 1)

            def nsa_values(n):
                i, h = n // H, n % H
                g = h // 4
                pe.wait_ge(sem("pT_evac"), n + 1)
                for b in range(2):
                    for j in range(i + 1):
                        m = mm(bank(4 + 2 * i + b, h * DH, DH), PT[:, n % 2, (b * (i + 1) + j) * P:][:, 0:P],
                               tk[:, j, 40 + 128 * b + DH * g:][:, 0:DH], start=(h == 0 and j == 0), stop=(j == i))
                m.then_inc(sem("pv_done"), 1)

            for n in range(TT_ * H + 2):
                if n < TT_ * H:
                    nsa_scores(n)
                if 1 <= n <= TT_ * H:
                    nsa_transpose(n - 1)
                if n >= 2:
                    nsa_values(n - 2)

            for g in range(4):
                pe.wait_ge(sem("TT0_ready"), g + 1)
                if g == 0:
                    pe.wait_ge(sem("pT_evac"), TT_ * H)
                for q in range(HP):
                    m = pe.transpose(bank(g, q * P, P), TT[:, g, q, :], ident)
                m.then_inc(sem("T_done"), 1)
            pe.wait_ge(sem("onsa_ready"), TT_)

            def turn_back(lv, g):
                pe.wait_ge(sem("TT_ready"), (lv - 1) * 4 + g + 1)
                for q in range(HP):
                    m = pe.transpose(bank(g, q * P, P), TT[:, g, q, :], ident)
                m.then_inc(sem("T_done"), 1)

            for lv in range(1, N_LEV):
                for g in range(4):
                    pe.wait_ge(sem("AbT_ready"), (lv - 1) * 4 + g + 1)
                    pe.wait_ge(sem("T_ready"), (lv - 1) * 4 + g + 1)
                    for q in range(HP):
                        m = mm(bank(g, q * P, P), AbT[:, g, q, :], Tm[:, g, q, :], start=(q == 0))
                    m.then_inc(sem("Y_done"), 1)
                for g in range(4):
                    n = (lv - 1) * 4 + g
                    pe.wait_ge(sem("Y_evac"), n + 1)
                    for q in range(HP):
                        m = mm(bank(4 + g, q * P, P), Yb[:, g, q, :], TT[:, g, q, :], start=(q == 0))
                    m.then_inc(sem("YTT_done"), 1)
                    if lv < N_LEV - 1 and g >= 1:
                        turn_back(lv, g - 1)
                if lv < N_LEV - 1:
                    turn_back(lv, 3)

            for i in range(TT_):
                for p in range(2):
                    pe.wait_ge(sem("TT_ready"), 4 * (N_LEV - 2) + 2 * i + p + 1)
                    for q in range(HP):
                        m = mm(ps[DH * p:DH * p + DH, i, q * P:(q + 1) * P], kbg[:, i, 2 * q + p, :],
                               TT[:, 2 * i + p, q, :], start=(q == 0))
                m.then_inc(sem("nwT_done"), 1)

            pe.wait_ge(sem("TT_ready"), 4 * (N_LEV - 1))
            pe.wait_ge(sem("scan_zero"), 2)
            for c in range(T // CH):
                i, r0 = c // 2, CH * (c % 2)
                rows = slice(r0, r0 + CH)
                if c == 0:
                    pe.wait_ge(sem("nwT_evac"), TT_)
                for h in range(H):
                    m = mm(ps[rows, 2, h * DH:(h + 1) * DH], TT[:, 2 * i + h % 2, h // 2, rows],
                           vb[:, i, h, :], start=(h == 0), stop=(c == 0))
                if c >= 1:
                    pe.wait_ge(sem("S_ready"), c)
                    for q in range(HP):
                        m = mm(ps[rows, 2, q * P:(q + 1) * P], nwT[:, i, q, rows], S[:, q, :], start=False)
                m.then_inc(sem("vn_done"), 1)
                if c >= 1:
                    pe.wait_ge(sem("o_evac"), c)
                    for q in range(HP):
                        mm(ps[rows, 3, q * P:(q + 1) * P], qdT[:, i, q, rows], S[:, q, :], start=(q == 0), stop=False)
                pe.wait_ge(sem("vn_evac"), c + 1)
                if c < T // CH - 1:
                    for q in range(HP):
                        m = mm(bank(4, q * P, P), kd_f[rows, i, q * P:(q + 1) * P], vn[rows, q * P:(q + 1) * P],
                               start=(q == 0))
                    m.then_inc(sem("dS_done"), 1)
                for h in range(H):
                    m = mm(ps[rows, 3, h * DH:(h + 1) * DH], attnT[:, i, h, rows], vn[:, h * DH:(h + 1) * DH],
                           start=(c == 0 and h == 0))
                m.then_inc(sem("o_done"), 1)

            for i in range(TT_):
                pe.wait_ge(sem("onsa_ready"), TT_)
                for k in range(HP):
                    m = pe.transpose(bank(i, k * P, P), onsa[:, i, k * P:(k + 1) * P], ident)
                m.then_inc(sem("obT_done"), 1)
            for i in range(TT_):
                pe.wait_ge(sem("oa_ready"), TT_)
                for k in range(HP):
                    m = pe.transpose(bank(5 + i, k * P, P), oa[:, i, k * P:(k + 1) * P], ident)
                m.then_inc(sem("oaT_done"), 1)

            pe.wait_ge(sem("oaT_evac"), TT_)
            pe.wait_ge(sem("obT_evac"), TT_)
            for j in range(N_AB):
                arrived(T_AB + j)
                if j >= 4:
                    pe.wait_ge(sem("mix_ready"), j - 3)
                w = slot(T_AB + j).rearrange("p (k m) -> p k m", k=2 * HP)
                for s, src in ((0, oaT), (1, obT)):
                    for k in range(HP):
                        m = mm(bank(j % 4, s * T, T), w[:, s * HP + k, :], src[:, k, :],
                               start=(s == 0 and k == 0), stop=(k == HP - 1))
                m.then_inc(sem("tiles_used"), 1)
            for k in range(N_OUT):
                arrived(T_OUT + k)
                pe.wait_ge(sem("mix_ready"), k + 1)
                for i in range(TT_):
                    for half in range(2):
                        m = mm(bank(4 + 2 * i + half), mixT[:, k, i * P:(i + 1) * P],
                               slot(T_OUT + k)[:, half * 512:(half + 1) * 512], start=(k == 0), stop=(k == KT - 1))
                m.then_inc(sem("tiles_used"), 1)

            pe.wait_ge(sem("mix_ready"), N_AB)
            for i in range(TT_):
                pe.wait_ge(sem("xn2_ready"), i + 1)
                for half in range(2):
                    for j in range(4):
                        k = half * 4 + j
                        m = pe.transpose(bank(2 * i + half, j * P, P), junk[:, i, k * P:(k + 1) * P], ident)
                    m.then_inc(sem("h2T_done"), 1)

            pe.wait_ge(sem("hT_split"), 8)
            for n in range(N_WQ):
                if n >= 4:
                    pe.wait_ge(sem("q_evac"), n - 3)
                by_h(n % 4, SPLIT.index(T_WQ + n))
            for s in range(N_SK):
                arrived(T_SK + s)
                w = slot(T_SK + s).rearrange("p (n k) -> p n k", n=8)
                pe.wait_ge(sem("q_evac"), 8 * s + 8)
                for i in range(TT_):
                    for half in range(2):
                        f = s * 4 + i * 2 + half
                        if f >= 4:
                            pe.wait_ge(sem("key_sc_evac"), f - 3)
                        for j in range(4):
                            n = half * 4 + j
                            m = mm(bank(4 + f % 4, j * P, P), qT[:, s * 8 + n, i * P:(i + 1) * P], w[:, n, :],
                                   start=(j == 0))
                        m.then_inc(sem("tiles_used" if f % 4 == 3 else "key_sc_done"), 1)

            groups = HALF // GROUP

            def activations(first, group, s):
                pe.wait_ge(sem("u_evac"), group * GROUP + (first + s + 1))
                by_h(s % 4, M_U + first + s, group * GROUP)

            def gates(turn, group, s, b0):
                n = turn * HALF + s
                pe.wait_ge(sem("oh_ready"), group * GROUP + (n + 1))
                pe.wait_ge(sem("weighed"), group * GROUP + (n + 1))
                for j in range(4):
                    m = mm(bank(b0 + s % 2, j * 2 * HALF, 2 * HALF), ohA[turn][:, j, :], ohB[turn][:, j, :, :],
                           start=(j == 0))
                m.then_inc(sem("G_done"), 1)

            def outputs(turn, group, s, first=False):
                ms = M_U + NKEYS + turn * HALF + s
                pe.wait_ge(sem("a_lo_ready"), group * GROUP + (turn * HALF + s + 1))
                for half in range(2):
                    pe.wait_ge(sem("lo_ready"), group * (2 * GROUP) + (2 * ms + half + 1))
                    for c in range(4 * half, 4 * half + 4):
                        for a, b in ((0, 0), (1, 0), (0, 1)):
                            m = mm(bank(4 + c // 2, (c % 2) * T, T), wsplit[:, ms % 2, a, c * P:(c + 1) * P],
                                   asplit[:, s % 2, b, :],
                                   start=(first and s == 0 and c % 2 == 0 and a == 0 and b == 0), stop=False)
                    m.then_inc(sem("tiles_used" if half else "half_used"), 1)

            with pe.Fori(0, groups - 1, 1) as group:
                for s in range(GROUP):
                    activations(0, group, s)

            pe.wait_ge(sem("choice_ready"), 1)
            for s in range(3):
                for i in range(TT_):
                    src = gate_f[:, i, :] if s == 2 else e_f[:, s, i, :]
                    m = pe.transpose(bank(4 + s, i * P, P), src, ident)
            m.then_inc(sem("egT_done"), 1)
            for s in range(GROUP):
                activations(0, groups - 1, s)
            pe.wait_ge(sem("egT_read"), 1)
            with pe.Fori(0, groups, 1) as group:
                for s in range(GROUP):
                    gates(0, group, s, 4)
                    activations(HALF, group, s)

            pe.wait_ge(sem("u_evac"), NKEYS + 4)
            pe.wait_ge(sem("weighed"), HALF + 2)
            for s in range(GROUP):
                gates(1, 0, s, 0)
                outputs(0, 0, s, first=True)
            with pe.Fori(1, groups, 1) as group:
                for s in range(GROUP):
                    gates(1, group, s, 0)
                    outputs(0, group, s)
            with pe.Fori(0, groups, 1) as group:
                for s in range(GROUP):
                    outputs(1, group, s)

            pe.wait_ge(sem("peerT_ready"), 4)
            for i in range(TT_):
                for half in range(2):
                    for j in range(4):
                        k = half * 4 + j
                        m = pe.transpose(bank(2 * i + half, j * P, P), peerT[:, k, i * P:(i + 1) * P], ident)
                    m.then_inc(sem("peer_done"), 1)

        @block.scalar
        def _(act):
            def tile_done(n):
                act.wait_ge(sem("tiles_used"), n + 1)

            def split(ms, past=0):
                n = SPLIT[ms]
                for half in range(2):
                    cols = slice(512 * half, 512 * half + 512)
                    act.wait_ge(sem(f"slot{n % NSLOT}_in"), past * (16 // NSLOT) + 16 * (n // NSLOT + 1))
                    if ms >= 2:
                        if half == 0:
                            act.wait_ge(sem("half_used"), past + (ms - 1))
                        else:
                            act.wait_ge(sem("tiles_used"), past + (SPLIT[ms - 2] + 1))
                    act.activation(wsplit[:, ms % 2, 0, cols], slot(n)[:, cols], ACT.Copy)\
                       .then_inc(sem("hi_ready"), 1)

            def split_h(turn):
                for f in range(4):
                    i, half = f // 2, f % 2
                    act.wait_ge(sem("hT_ready"), 4 * turn + f + 1)
                    part = slice(4 * half, 4 * half + 4), slice(i * P, (i + 1) * P)
                    act.activation(hsplit[:, 0, part[0], part[1]], hT[:, part[0], part[1]], ACT.Copy)\
                       .then_inc(sem("hT_hi"), 1)

            split(0)
            act.wait_ge(sem("rms_mean"), 1)
            act.activation(rms[:, 4:6], rms[:, 2:4], ACT.Sqrt).then_inc(sem("rms_root"), 1)
            split(1)
            split_h(0)
            act.wait_ge(sem("pad_zero"), 1)
            for n in range(N_GDN + 2):
                if n < N_GDN:
                    tile_done(T_GDN + n)
                    act.activation(pad[:, n, 3:259], bank(n % 4, 0, T), ACT.Copy).then_inc(sem("proj_evac"), 1)
                    if n + 2 < N_GDN:
                        split(n + 2)
                if n >= 2:
                    act.wait_ge(sem("conv_done"), n - 1)
                    act.activation(conv[:, n - 2, :], conv[:, n - 2, :], ACT.Silu).then_inc(sem("silu_done"), 1)
            split(N_GDN)
            split(N_GDN + 1)
            tile_done(T_TOK + N_TOK - 1)
            for i in range(TT_):
                act.activation(zs[:, i, :], bank(4 + 2 * i), ACT.Silu).then_inc(sem("z_evac"), 1)
            for n in range(N_NSA):
                tile_done(T_NSA + n)
                act.activation(nsaf[:, n, :], bank((N_GDN + n) % 4, 0, T), ACT.Copy).then_inc(sem("proj_evac"), 1)
                split(N_GDN + n + 2)
            for f in range(6):
                act.wait_ge(sem("tt_done"), f + 1)
                act.activation(qkvt[:, f % 2, 512 * (f // 2):][:, 0:512], bank(4 + f % 4), ACT.Copy)\
                   .then_inc(sem("tt_evac"), 1)
            act.wait_ge(sem("tok_evac"), TT_)
            act.activation(sg, tk[:, :, 0:32], ACT.Sigmoid).then_inc(sem("sg_ready"), 1)
            for n in range(N_MERGE):
                tile_done(T_MERGE + n)
                act.activation(mg[:, n, :], bank((N_GDN + N_NSA + n) % 4, 0, T), ACT.Sigmoid)\
                   .then_inc(sem("proj_evac"), 1)
                if n + 2 < N_MERGE:
                    split(N_GDN + N_NSA + n + 2)
                if n == 3:
                    act.wait_ge(sem("ge_in"), 1)
                    act.activation(ge, ge, ACT.Exp).then_inc(sem("ge_out"), 1)
                    act.activation(ea, par_cols(R_ALOG, 8), ACT.Exp).then_inc(sem("ge_out"), 1)
                    act.wait_ge(sem("ssq_ready"), 1)
                    act.activation(rq, ssq, ACT.Sqrt).then_inc(sem("rq_root"), 1)
            act.wait_ge(sem("gcl_evac"), 1)
            act.activation(eg, gcl[:, :, 0:8], ACT.Exp).then_inc(sem("eg_ready"), 1)
            act.wait_ge(sem("ekd_in"), 1)
            act.activation(ekd, ekd, ACT.Exp).then_inc(sem("ekd_ready"), 1)
            for i in range(TT_):
                act.wait_ge(sem("DT_in"), i + 1)
                for p in range(2):
                    rows = slice(DH * p, DH * p + DH)
                    for half in range(2):
                        b = 4 + (1 + 2 * i + half) % 4
                        src = ps[rows, b, :].rearrange("p (q z c t) -> p q z c t", q=2, z=2, c=2)[:, :, p, :, CH - 1]
                        m = act.activation(egl[rows, i, 2 * half:2 * half + 2, :], src, ACT.Exp)
                m.then_inc(sem("gbc_read"), 1)
                act.activation(DT[:, i], DT[:, i], ACT.Exp).then_inc(sem("DT_exp"), 1)
            for f in range(8):
                act.wait_ge(sem("fT_done"), f + 1)
                act.activation(XT[:, f // 2, f % 2], bank(f % 4), ACT.Copy).then_inc(sem("fT_evac"), 1)
            for i in range(TT_):
                act.wait_ge(sem("pc_in"), i + 1)
                act.activation(pc[:, i], pc[:, i], ACT.Exp).then_inc(sem("pc_exp"), 1)
            for b in range(4):
                act.wait_ge(sem("BT_done"), b + 1)
                act.activation(BT[:, 2 * b:2 * b + 2, :], bank(b), ACT.Copy).then_inc(sem("BT_in"), 1)
            for i in range(TT_):
                act.wait_ge(sem("pcT_done"), i + 1)
                act.activation(pcT[:, i, :], bank(i, 0, P), ACT.Copy).then_inc(sem("pcT_evac"), 1)
            for n in range(TT_ * H + 1):
                if n < TT_ * H:
                    i, h = n // H, n % H
                    nk = P * (i + 1)
                    act.wait_ge(sem("s_ready"), n + 1)
                    for b in range(2):
                        m = act.activation(Sb[:, n % 2, b * nk:(b + 1) * nk], Sb[:, n % 2, b * nk:(b + 1) * nk], ACT.Exp,
                                           bias=mx[:, n, b:b + 1], accum_out=sums[:, i, h, 1 + b:2 + b])
                    m.then_inc(sem("p_ready"), 1)
                if n >= 1:
                    w = 2 * P * ((n - 1) // H + 1)
                    act.wait_ge(sem("pT_done"), n)
                    if n >= 3:
                        act.wait_ge(sem("pv_done"), n - 2)
                    act.activation(PT[:, (n - 1) % 2, 0:w], bank(2 + (n - 1) % 2, 0, w), ACT.Copy)\
                       .then_inc(sem("pT_evac"), 1)
            for lv in range(N_LEV):
                for g in range(4):
                    n = (lv - 1) * 4 + g
                    if lv > 0:
                        act.wait_ge(sem("Y_done"), n + 1)
                        act.activation(Yb[:, g], bank(g), ACT.Copy).then_inc(sem("Y_evac"), 1)
                if lv < N_LEV - 1:
                    for g in range(4):
                        act.wait_ge(sem("T_done"), lv * 4 + g + 1)
                        act.activation(Tm[:, g], bank(g), ACT.Copy).then_inc(sem("T_ready"), 1)
            for i in range(TT_):
                act.wait_ge(sem("nwT_done"), i + 1)
                act.activation(nwT[:, i], bank(i), ACT.Copy).then_inc(sem("nwT_evac"), 1)
            for c in range(T // CH):
                rows = slice(CH * (c % 2), CH * (c % 2) + CH)
                act.wait_ge(sem("o_done"), c + 1)
                act.activation(oa[rows, c // 2, :], ps[rows, 3, :], ACT.Copy).then_inc(sem("o_evac"), 1)
            act.wait_ge(sem("oss_ready"), 1)
            act.activation(osr, oss, ACT.Sqrt).then_inc(sem("osr_root"), 1)
            for i in range(TT_):
                act.wait_ge(sem("obT_done"), i + 1)
                act.activation(obT[:, :, i * P:(i + 1) * P], bank(i), ACT.Copy).then_inc(sem("obT_evac"), 1)
            for i in range(TT_):
                act.wait_ge(sem("oaT_done"), i + 1)
                act.activation(oaT[:, :, i * P:(i + 1) * P], bank(5 + i), ACT.Copy).then_inc(sem("oaT_evac"), 1)
            split(N_GDN + N_NSA + N_MERGE)
            split(N_GDN + N_NSA + N_MERGE + 1)
            act.wait_ge(sem("rms_mean"), 2)
            act.activation(rms[:, 4:6], rms[:, 2:4], ACT.Sqrt).then_inc(sem("rms_root"), 1)
            split_h(1)
            for n in range(N_WQ):
                tile_done(T_WQ + n)
                act.activation(qT[:, n, :], bank(n % 4, 0, T), ACT.Copy).then_inc(sem("q_evac"), 1)
                split(N_GDN + N_NSA + N_MERGE + n + 2)
            for f in range(8):
                s, i, half = f // 4, (f // 2) % 2, f % 2
                if f % 4 == 3:
                    tile_done(T_SK + s)
                else:
                    act.wait_ge(sem("key_sc_done"), 3 * s + f % 4 + 1)
                act.activation(sc[:, i, 8 * s + 4 * half:8 * s + 4 * half + 4, :], bank(4 + f % 4), ACT.Copy)\
                   .then_inc(sem("key_sc_evac"), 1)
            act.wait_ge(sem("q_evac"), N_WQ)
            act.sem_inc(sem("u_evac"), 4)
            act.preload_act_table(ACT.Gelu_apprx_tanh)

            groups = HALF // GROUP

            def gelu(group, s, first=0):
                act.wait_ge(sem("tiles_used"), group * GROUP + (T_U + first + s + 1))
                act.activation(act_w[:, group * GROUP + (first + s), :], bank(s % 4, 0, T), ACT.Gelu_apprx_tanh)\
                   .then_inc(sem("u_evac"), 1)
                split(M_U + first + s + 2, group * GROUP)

            with act.Fori(0, groups - 2, 1) as group:
                for s in range(GROUP):
                    gelu(group, s)
            act.wait_ge(sem("gate_in"), TT_)
            for i in range(TT_):
                act.activation(gate[:, i], gate[:, i], ACT.Exp).then_inc(sem("gate_exp"), 1)
            for s in range(GROUP):
                gelu(groups - 2, s)
            act.wait_ge(sem("egT_done"), 1)
            act.activation(egT[:, :, :], ps[:, 4:7, 0:T], ACT.Copy)
            act.activation(g2[:, :, 0].bitcast(F32R), bank(6, 0, T), ACT.Copy).then_inc(sem("egT_read"), 1)
            for s in range(GROUP):
                gelu(groups - 1, s)
            act.preload_act_table(ACT.Gelu_apprx_tanh)

            def lo_out(turn, group, s, b0):
                act.wait_ge(sem("G_done"), group * GROUP + (turn * HALF + s + 1))
                act.activation(G_lo[:, s % 2], bank(b0 + s % 2).rearrange("p (t x e) -> p x t e", t=4, x=2)[:, 1],
                               ACT.Copy).then_inc(sem("G_lo_read"), 1)

            with act.Fori(0, groups, 1) as group:
                for s in range(GROUP):
                    lo_out(0, group, s, 4)
                    gelu(group, s, HALF)

            def split_a(row, buf):
                act.activation(asplit[:, buf, 0, :], row, ACT.Copy).then_inc(sem("a_hi_ready"), 1)

            def out_step(group, s, ahead=True, gates=False):
                act.wait_ge(sem("tiles_used"), group * GROUP + (T_V + s))
                split_a(act_w[:, group * GROUP + (s + 1), :], (s + 1) % 2)
                if gates:
                    lo_out(1, group, s, 0)
                if ahead:
                    split(M_U + NKEYS + s + 2, group * GROUP)

            act.wait_ge(sem("weighed"), HALF + 2)
            split_a(act_w[:, 0, :], 0)
            with act.Fori(0, groups - 1, 1) as group:
                for s in range(GROUP):
                    out_step(group, s, gates=True)
            for s in range(GROUP - 1):
                out_step(groups - 1, s, gates=True)
            lo_out(1, groups - 1, GROUP - 1, 0)
            act.wait_ge(sem("weighed"), 2 * HALF + 2)
            out_step(groups - 1, GROUP - 1)
            with act.Fori(groups, 2 * groups - 1, 1) as group:
                for s in range(GROUP):
                    out_step(group, s)
            for s in range(GROUP - 1):
                out_step(2 * groups - 1, s, ahead=s < GROUP - 2)
            act.wait_ge(sem("tiles_used"), N_TILES)
            for b in range(4):
                act.activation(peerT[:, 2 * b:2 * b + 2, :], bank(4 + b), ACT.Copy).then_inc(sem("peerT_ready"), 1)
            act.wait_ge(sem("rms_mean"), 3)
            act.activation(rms[:, 4:6], rms[:, 2:4], ACT.Sqrt).then_inc(sem("rms_root"), 1)

        @block.vector
        def _(dve):
            chain = [0]

            def link(m):
                chain[0] += 1
                m.then_inc(sem("dve_chain"), 1)
                dve.wait_ge(sem("dve_chain"), chain[0])

            tt, ts, stt = dve.tensor_tensor, dve.tensor_scalar, dve.scalar_tensor_tensor

            def tile_done(n):
                dve.wait_ge(sem("tiles_used"), n + 1)

            def rms_scale(turn):
                for i in range(TT_):
                    link(dve.tensor_tensor_reduce(sq[:, i, :], xr[:, i, :], xr[:, i, :], 1.0, 0.0, ALU.mult,
                                                  ALU.add, rms[:, i:i + 1]))
                ts(rms[:, 2:4], rms[:, 0:2], 1.0 / D, EPS, ALU.mult, ALU.add).then_inc(sem("rms_mean"), 1)
                dve.wait_ge(sem("rms_root"), turn)
                link(dve.reciprocal(rms[:, 6:8], rms[:, 4:6]))

            dve.wait_ge(sem("x_in"), 16)
            rms_scale(1)
            for i in range(TT_):
                ts(junk[:, i, :], xr[:, i, :], rms[:, 6 + i:7 + i], None, ALU.mult).then_inc(sem("xn_ready"), 1)
            dve.wait_ge(sem("params_in"), 16)
            for f in range(4):
                i, half = f // 2, f % 2
                dve.wait_ge(sem("hT_done"), f + 1)
                tt(hT[:, 4 * half:4 * half + 4, i * P:(i + 1) * P], bank(4 + f).rearrange("p (k t) -> p k t", k=4),
                   each(par_cols(R_NM + 4 * half, 4), P), ALU.mult).then_inc(sem("hT_ready"), 1)

            def split_h(turn):
                for f in range(4):
                    i, half = f // 2, f % 2
                    dve.wait_ge(sem("hT_hi"), 4 * turn + f + 1)
                    part = slice(4 * half, 4 * half + 4), slice(i * P, (i + 1) * P)
                    tt(hsplit[:, 1, part[0], part[1]], hT[:, part[0], part[1]],
                       hsplit[:, 0, part[0], part[1]].bitcast(F32), ALU.subtract).then_inc(sem("hT_split"), 1)

            split_h(0)
            for n in range(N_GDN):
                dve.wait_ge(sem("proj_evac"), n + 1)
                c0 = R_CW + 4 * n
                link(ts(conv[:, n, :], pad[:, n, 0:T], par[:, c0:c0 + 1], None, ALU.mult))
                for j in range(1, 4):
                    m = stt(out=conv[:, n, :], in0=pad[:, n, j:j + T], scalar=par[:, c0 + j:c0 + j + 1],
                            in1=conv[:, n, :], op0=ALU.mult, op1=ALU.add)
                    if j < 3:
                        link(m)
                m.then_inc(sem("conv_done"), 1)

            tile_done(T_TOK + N_TOK - 1)
            for i in range(TT_):
                dve.tensor_copy(tk[:, i, :], bank(5 + 2 * i, 0, 296)).then_inc(sem("tok_evac"), 1)
            dve.wait_ge(sem("tok_evac"), TT_)
            link(tt(gs, tk[:, :, 32:40], over(par_cols(R_DT, 8), TT_), ALU.add))
            link(ts(gm, gs, 0.0, None, ALU.max))
            stt(out=ge, in0=gs, scalar=-1.0, in1=gs, op0=ALU.mult, op1=ALU.min).then_inc(sem("ge_in"), 1)

            for s in range(2):
                dve.wait_ge(sem("proj_evac"), N_GDN + (8 if s else 5))
                src = nsaf[:, 7 if s else 4, :].rearrange("p (m b) -> p b m", b=16)
                for a in range(2):
                    tt(kcpe[:, s, 16 * a:16 * a + 16, :], src[:, :, a:a + NCMP],
                       each(par_cols(R_PE + 32 * s + 16 * a, 16), NCMP), ALU.add).then_inc(sem("kcpe_ready"), 1)

            dve.wait_ge(sem("tt_evac"), 4)
            for i in range(TT_):
                link(tt(sq[:, i, :], qkvt[:, i, 0:1024], qkvt[:, i, 0:1024], ALU.mult))
                link(dve.tensor_reduce(ssq[:, i, :], sq[:, i, :].rearrange("p (h d) -> p h d", d=DH), AX.X, ALU.add))
            ts(ssq, ssq, EPS, None, ALU.add).then_inc(sem("ssq_ready"), 1)

            dve.wait_ge(sem("ge_out"), 2)
            link(ts(gz, ge, 2.0, None, ALU.add))
            link(dve.reciprocal(gr, gz))
            link(tt(gz, ge, gr, ALU.mult))
            link(tt(gt, gz, gz, ALU.mult))
            link(ts(gp, gt, 1.0 / 17, None, ALU.mult))
            for k in range(15, 1, -2):
                link(stt(out=gp, in0=gp, scalar=1.0 / k, in1=gt, op0=ALU.add, op1=ALU.mult))
            link(stt(out=gp, in0=gp, scalar=1.0, in1=gz, op0=ALU.add, op1=ALU.mult))
            link(stt(out=gp, in0=gp, scalar=2.0, in1=gm, op0=ALU.mult, op1=ALU.add))
            stt(out=gg, in0=gp, scalar=-1.0, in1=over(ea, TT_), op0=ALU.mult, op1=ALU.mult).then_inc(sem("g_ready"), 1)

            dve.wait_ge(sem("rq_root"), 1)
            link(dve.reciprocal(rq, rq))
            link(ts(rq[:, :, 0:8], rq[:, :, 0:8], DH ** -0.5, None, ALU.mult))
            dve.wait_ge(sem("tt_done"), 6)
            dve.wait_ge(sem("sg_ready"), 1)

            def heads(i, part):
                return qkvt[:, i, 512 * part:512 * part + 512].rearrange("p (h d) -> p h d", h=H)

            for i in range(TT_):
                tt(kn[:, i], heads(i, 1), each(rq[:, i, 8:16], DH), ALU.mult).then_inc(sem("gdn_rows_ready"), 1)
            dve.wait_ge(sem("gdn_rows_ready"), 2)
            for i in range(TT_):
                tt(kb[:, i], kn[:, i], each(sg[:, i, 0:8], DH), ALU.mult).then_inc(sem("gdn_rows_ready"), 1)
            for i in range(TT_):
                tt(qn[:, i], heads(i, 0), each(rq[:, i, 0:8], DH), ALU.mult).then_inc(sem("gdn_rows_ready"), 1)
            dve.wait_ge(sem("tt_evac"), 6)
            for i in range(TT_):
                link(tt(vb[:, i], heads(i, 2), each(sg[:, i, 0:8], DH), ALU.mult))
            for i in range(TT_):
                z = zs[:, i, :].rearrange("p (h d) -> p h d", h=H)
                dve.wait_ge(sem("z_evac"), i + 1)
                link(tt(z, z, over(par_cols(R_GN, DH), H), ALU.mult))

            dve.wait_ge(sem("bias_row_done"), 1)
            dve.tensor_copy(rrs[0:H, :], bank(4, 0, N_E1)[0:H]).then_inc(sem("bias_read"), 1)
            dve.wait_ge(sem("bias_cmp_done"), 1)
            for i in range(TT_):
                src = bank(5, i * NCMP * H, NCMP * H).rearrange("p (n h) -> p h n", h=H)
                dve.tensor_copy(bcmp[:, i, :, 0:NCMP], src).then_inc(sem("bias_read"), 1)

            dve.wait_ge(sem("gcl_done"), 1)
            dve.tensor_copy(gcl, bank(4, 0, 32).rearrange("p (i c) -> p i c", i=TT_)).then_inc(sem("gcl_evac"), 1)
            dve.wait_ge(sem("gcl_evac"), 1)
            tt(ekd, gcl[:, :, 8:16], gcl[:, :, 0:8], ALU.subtract).then_inc(sem("ekd_in"), 1)
            link(ts(ngc, gcl[:, :, 0:8], -1.0, None, ALU.mult))
            dve.wait_ge(sem("eg_ready"), 1)
            dve.wait_ge(sem("gdn_rows_ready"), 6)
            for i in range(TT_):
                tt(qd[:, i], qn[:, i], each(eg[:, i, :], DH), ALU.mult).then_inc(sem("gdn_rows_ready"), 1)
            for i in range(TT_):
                dve.wait_ge(sem("gbc_done"), i + 1)
                for h in range(H):
                    m = stt(out=DT[:, i, h, :], in0=bank(4 + (1 + 2 * i + h // 4) % 4, (h % 4) * P, P),
                            scalar=ngc[:, i, h:h + 1], in1=tri, op0=ALU.add, op1=ALU.mult)
                m.then_inc(sem("DT_in"), 1)
            link(ts(neg_eg, eg, -1.0, None, ALU.mult))
            dve.wait_ge(sem("ekd_ready"), 1)
            for i in range(TT_):
                tt(kbg[:, i], kb[:, i], each(neg_eg[:, i, :], DH), ALU.mult)
                link(tt(kd[:, i], kn[:, i], each(ekd[:, i, :], DH), ALU.mult))
            for i in range(TT_):
                dve.wait_ge(sem("DT_exp"), i + 1)
                link(tt(DT[:, i], DT[:, i], over(tri, H), ALU.mult))
            for r in range(8):
                which, i, p = r // 4, (r // 2) % 2, r % 2
                dve.wait_ge(sem("am_done"), r + 1)
                dst = attnT if which else AT
                tt(dst[:, i, p:H:2, :], bank(4 + r % 4).rearrange("p (q t) -> p q t", q=HP), DT[:, i, p:H:2, :],
                   ALU.mult).then_inc(sem("am_evac"), 1)

            for g in range(2):
                rows = slice(DH * g, DH * g + DH)
                tile_done(T_CMP + 1)
                dve.tensor_copy(kcmpT[rows, 0:NCMP], ps[rows, g, 0:NCMP]).then_inc(sem("kvcmp_evac"), 1)
            for g in range(2):
                tile_done(T_CMP + 3)
                dve.tensor_copy(vcs[0:NCMP, g * DH:(g + 1) * DH], ps[0:NCMP, 2 + g, 0:DH]).then_inc(sem("kvcmp_evac"), 1)
            dve.wait_ge(sem("nsa_zero"), 1)
            for i in range(TT_):
                for g in range(2):
                    dve.wait_ge(sem("sc_done"), 2 * i + g + 1)
                    link(stt(out=pc[:, i, 4 * g:4 * g + 4, 0:NCMP],
                             in0=bank(4 + 2 * i + g, 0, 64).rearrange("p (q n) -> p q n", q=4)[:, :, 0:NCMP],
                             scalar=DH ** -0.5, in1=bcmp[:, i, 4 * g:4 * g + 4, 0:NCMP], op0=ALU.mult, op1=ALU.add))
                link(dve.tensor_reduce(cmx[:, i, :], pc[:, i, :, 0:NCMP], AX.X, ALU.max))
                tt(pc[:, i, :, 0:NCMP], pc[:, i, :, 0:NCMP], each(cmx[:, i, :], NCMP), ALU.subtract)\
                    .then_inc(sem("pc_in"), 1)
            for i in range(TT_):
                dve.wait_ge(sem("pc_exp"), i + 1)
                link(dve.tensor_reduce(sums[:, i, :, 0], pc[:, i, :, 0:NCMP], AX.X, ALU.add))
                tt(pc[:, i], pc[:, i], over(cmask[:, i, :], H), ALU.mult).then_inc(sem("pc_ready"), 1)

            def branch_gates(i, b0, b1):
                gates = sg[:, i, 8:32].rearrange("p (h b) -> p h b", h=H)
                link(dve.reciprocal(coef[:, i, :, b0:b1], sums[:, i, :, b0:b1]))
                link(tt(coef[:, i, :, b0:b1], coef[:, i, :, b0:b1], gates[:, :, b0:b1], ALU.mult))

            for i in range(TT_):
                branch_gates(i, 0, 1)
                dve.wait_ge(sem("oc_done"), i + 1)
                tt(onsa[:, i, :].rearrange("p (h d) -> p h d", h=H), bank(2 + i).rearrange("p (h d) -> p h d", h=H),
                   each(coef[:, i, :, 0], DH), ALU.mult).then_inc(sem("oc_evac"), 1)

            dve.wait_ge(sem("BT_in"), 4)
            for n in range(TT_ * H):
                i, h = n // H, n % H
                nk = P * (i + 1)
                dve.wait_ge(sem("s_done"), n + 1)
                if n >= 2:
                    dve.wait_ge(sem("pT_done"), n - 1)
                s = Sb[:, n % 2, 0:2 * nk].rearrange("p (b j) -> p b j", b=2)
                stt(out=s, in0=bank(n % 2, 0, 2 * nk).rearrange("p (b j) -> p b j", b=2), scalar=DH ** -0.5,
                    in1=over(BT[:, h, T - nk:T], 2), op0=ALU.mult, op1=ALU.add).then_inc(sem("s_evac"), 1)
                dve.wait_ge(sem("s_evac"), n + 1)
                dve.tensor_reduce(mx[:, n, :], s, AX.X, ALU.max, negate=True).then_inc(sem("s_ready"), 1)
            dve.wait_ge(sem("pT_done"), TT_ * H)
            dve.wait_ge(sem("pv_done"), TT_ * H)
            for i in range(TT_):
                branch_gates(i, 1, 3)
                for b in range(2):
                    link(tt(Sb[:, b, :].rearrange("p (h d) -> p h d", h=H),
                            bank(4 + 2 * i + b).rearrange("p (h d) -> p h d", h=H),
                            each(coef[:, i, :, 1 + b], DH), ALU.mult))
                link(tt(onsa[:, i, :], onsa[:, i, :], Sb[:, 0, :], ALU.add))
                tt(onsa[:, i, :], onsa[:, i, :], Sb[:, 1, :], ALU.add).then_inc(sem("onsa_ready"), 1)

            for n in range(4 * (N_LEV - 1)):
                g = n % 4
                dve.wait_ge(sem("YTT_done"), n + 1)
                tt(TT[:, g], TT[:, g], bank(4 + g).rearrange("p (q j) -> p q j", q=HP), ALU.subtract)\
                    .then_inc(sem("TT_ready"), 1)

            dve.wait_ge(sem("scan_zero"), 2)
            for c in range(T // CH):
                rows = slice(CH * (c % 2), CH * (c % 2) + CH)
                dve.wait_ge(sem("vn_done"), c + 1)
                dve.tensor_copy(vn[rows, :], ps[rows, 2, :]).then_inc(sem("vn_evac"), 1)
                if c == T // CH - 1:
                    continue
                dve.wait_ge(sem("dS_done"), c + 1)
                for p in range(2):
                    hr = slice(DH * p, DH * p + DH)
                    dS = ps[hr, 4, :].rearrange("p (q e) -> p q e", q=HP)[:, :, DH * p:DH * p + DH]
                    Sp = S[hr, :, DH * p:DH * p + DH]
                    link(tt(Sp, Sp, each(egl[hr, c // 2, :, c % 2], DH), ALU.mult))
                    m = tt(Sp, Sp, dS, ALU.add)
                    if p == 0:
                        link(m)
                m.then_inc(sem("S_ready"), 1)

            dve.wait_ge(sem("o_evac"), T // CH)
            dve.wait_ge(sem("YTT_done"), 4 * (N_LEV - 1))
            osq = at(0, 1024).rearrange("p (i c) -> p i c", i=TT_)
            link(tt(osq, oa, oa, ALU.mult))
            for i in range(TT_):
                link(dve.tensor_reduce(oss[:, i, :], osq[:, i, :].rearrange("p (h d) -> p h d", h=H), AX.X, ALU.add))
            ts(oss, oss, 1.0 / DH, EPS, ALU.mult, ALU.add).then_inc(sem("oss_ready"), 1)
            dve.wait_ge(sem("osr_root"), 1)
            link(dve.reciprocal(osr, osr))
            for i in range(TT_):
                o3 = oa[:, i, :].rearrange("p (h d) -> p h d", h=H)
                link(tt(o3, o3, each(osr[:, i, :], DH), ALU.mult))
                tt(oa[:, i, :], oa[:, i, :], zs[:, i, :], ALU.mult).then_inc(sem("oa_ready"), 1)

            both = at(0, 512).rearrange("p (s t) -> p s t", s=2)
            for j in range(N_AB):
                tile_done(T_AB + j)
                link(tt(both, bank(j % 4).rearrange("p (s t) -> p s t", s=2), mg[:, j:16:8, :], ALU.mult))
                tt(mixT[:, j, :], both[:, 0, :], both[:, 1, :], ALU.add).then_inc(sem("mix_ready"), 1)
                dve.wait_ge(sem("mix_ready"), j + 1)
            tile_done(T_OUT + N_OUT - 1)
            for i in range(TT_):
                for half in range(2):
                    xh = xr[:, i, 512 * half:512 * half + 512]
                    link(tt(xh, xh, bank(4 + 2 * i + half), ALU.add))
            rms_scale(2)
            for i in range(TT_):
                ts(junk[:, i, :], xr[:, i, :], rms[:, 6 + i:7 + i], None, ALU.mult).then_inc(sem("xn2_ready"), 1)
            for f in range(4):
                i, half = f // 2, f % 2
                dve.wait_ge(sem("h2T_done"), f + 1)
                tt(h2T[:, 4 * half:4 * half + 4, i * P:(i + 1) * P], bank(f).rearrange("p (k t) -> p k t", k=4),
                   each(par_cols(R_NF + 4 * half, 4), P), ALU.mult).then_inc(sem("hT_ready"), 1)
            split_h(1)

            def best16(val, idx, src, left):
                link(dve.max(val[:, 0:8], src))
                dve.max_index(idx[:, 0:8], val[:, 0:8], src)
                link(dve.match_replace(left, val[:, 0:8], src, -3e38))
                link(dve.max(val[:, 8:16], left))
                link(dve.max_index(idx[:, 8:16], val[:, 8:16], left))

            dve.wait_ge(sem("key_sc_evac"), 8)
            for i in range(TT_):
                for n in range(2 * H):
                    best16(tkv[:, i, n, :], tki_u[:, i, n, :], sc[:, i, n, :], rep)
            link(dve.tensor_copy(tki, tki_u))
            for i in range(TT_):
                for h in range(H):
                    link(tt(cand.rearrange("p (a b) -> p a b", a=TOPK), each(tkv[:, i, 2 * h, :], TOPK),
                            over(tkv[:, i, 2 * h + 1, :], TOPK), ALU.add))
                    best16(topv[:, i, h, :], topi_u[:, i, h, :], cand, cand2)
            topi_c = topi_u.rearrange("p i h k -> p i (h k)")
            link(ts(ab_u[:, 0], topi_c, 4, None, ALU.logical_shift_right))
            link(ts(ab_u[:, 1], topi_c, 15, None, ALU.bitwise_and))
            link(dve.tensor_copy(ab_f, ab_u))
            for s in range(2):
                for i in range(TT_):
                    link(tt(oh, each(ab_f[:, s, i, :], TOPK), over(iota[:, 0:TOPK], P), ALU.is_equal))
                    oh4 = oh.rearrange("p (h k) a -> p h k a", h=H)
                    keys = tki[:, i, s:2 * H:2, :].unsqueeze(2).broadcast_to([P, H, TOPK, TOPK])
                    link(tt(oh4, oh4, keys, ALU.mult))
                    link(dve.tensor_reduce(e_f[:, s, i, :], oh, AX.X, ALU.add))
            for i in range(TT_):
                tt(gate[:, i], topv[:, i], each(topv[:, i, :, 0], TOPK), ALU.subtract).then_inc(sem("gate_in"), 1)
            dve.wait_ge(sem("gate_exp"), TT_)
            gsum = gs
            link(dve.tensor_reduce(gsum, gate, AX.X, ALU.add))
            link(dve.reciprocal(gr, gsum))
            link(tt(gate[:, 0], gate[:, 0], each(gr[:, 0, :], TOPK), ALU.mult))
            tt(gate[:, 1], gate[:, 1], each(gr[:, 1, :], TOPK), ALU.mult).then_inc(sem("choice_ready"), 1)

            groups = HALF // GROUP

            def one_hots(turn, group, s, first=False):
                n = turn * HALF + s
                b = (6, 2)[turn]
                row = bank(b, 0, P)
                hot = bank(b + s % 2, P, 4 * HALF).rearrange("p (t j) -> p t j", t=4)
                cols = bass.ds(group * (4 * GROUP) + 4 * s, 4)
                tt(hot, over(row[:, turn * HALF:(turn + 1) * HALF], 4), each(egT[:, 1, cols], HALF), ALU.is_equal)\
                    .then_inc(sem("hot_ready"), 1)
                if not first:
                    dve.wait_ge(sem("G_done"), group * GROUP + n)
                tt(ohA[turn], over(row, 4), each(egT[:, 0, cols], P), ALU.is_equal)
                dve.wait_ge(sem("hot_ready"), group * GROUP + (n + 1))
                tt(ohB[turn], hot.unsqueeze(2).broadcast_to([P, 4, 2, HALF]),
                   g2[:, cols, :].unsqueeze(3).broadcast_to([P, 4, 2, HALF]), ALU.mult).then_inc(sem("oh_ready"), 1)

            def weigh(turn, group, s, b0, between=None):
                n = turn * HALF + s
                dve.wait_ge(sem("G_done"), group * GROUP + (n + 1))
                G = bank(b0 + s % 2).rearrange("p (t x e) -> p x t e", t=4, x=2)
                dve.wait_ge(sem("G_lo_read"), group * GROUP + (n + 1))
                tt(G[:, 0], G[:, 0], G_lo[:, s % 2], ALU.add).then_inc(sem("G_sum"), 1)
                if between:
                    rest(group, between)
                dve.wait_ge(sem("G_sum"), group * GROUP + (n + 1))
                aw = act_w[:, turn * HALF:(turn + 1) * HALF, bass.ds(group * (4 * GROUP) + 4 * s, 4)]
                tt(aw.rearrange("p e t -> p t e"), aw.rearrange("p e t -> p t e"), G[:, 0], ALU.mult)\
                    .then_inc(sem("weighed"), 1)

            def rest(group, s):
                dve.wait_ge(sem("a_hi_ready"), group * GROUP + (s + 1))
                tt(asplit[:, s % 2, 1, :], act_w[:, group * GROUP + s, :], asplit[:, s % 2, 0, :].bitcast(F32),
                   ALU.subtract).then_inc(sem("a_lo_ready"), 1)

            dve.wait_ge(sem("egT_read"), 1)
            link(tt(g2[:, :, 1], egT[:, 2, :], g2[:, :, 0], ALU.subtract))
            dve.sem_inc(sem("weighed"), 2)
            dve.tensor_copy(bank(6, 0, P), iota).then_inc(sem("iota_in"), 1)
            dve.wait_ge(sem("iota_in"), 1)
            one_hots(0, 0, 0, first=True)
            dve.wait_ge(sem("u_evac"), HALF + 4)
            with dve.Fori(0, groups - 1, 1) as group:
                for s in range(GROUP):
                    one_hots(0, group, s + 1)
                    weigh(0, group, s, 4)
            for s in range(GROUP):
                if s < GROUP - 1:
                    one_hots(0, groups - 1, s + 1)
                weigh(0, groups - 1, s, 4)
            dve.wait_ge(sem("u_evac"), NKEYS + 4)
            dve.tensor_copy(bank(2, 0, P), iota).then_inc(sem("iota_in"), 1)
            dve.wait_ge(sem("iota_in"), 2)
            one_hots(1, 0, 0, first=True)
            rest(0, 0)

            def second_step(group, s, ahead=True):
                if ahead:
                    one_hots(1, group, s + 1)
                weigh(1, group, s, 0, between=s + 1 if ahead else None)

            with dve.Fori(0, groups - 1, 1) as group:
                for s in range(GROUP):
                    second_step(group, s)
            for s in range(GROUP):
                second_step(groups - 1, s, ahead=s < GROUP - 1)
            rest(groups - 1, GROUP)
            with dve.Fori(groups, 2 * groups - 1, 1) as group:
                for s in range(GROUP):
                    rest(group, s + 1)
            for s in range(GROUP - 1):
                rest(2 * groups - 1, s + 1)

            for i in range(TT_):
                for half in range(2):
                    dve.wait_ge(sem("peer_done"), 2 * i + half + 1)
                    xh = xr[:, i, 512 * half:512 * half + 512]
                    link(tt(xh, xh, bank(2 * i + half), ALU.add))
            rms_scale(3)
            dve.wait_ge(sem("nfinal_in"), 16)
            for i in range(TT_):
                stt(out=xr[:, i, :], in0=xr[:, i, :], scalar=rms[:, 6 + i:7 + i], in1=nfin, op0=ALU.mult,
                    op1=ALU.mult).then_inc(sem("out_ready"), 1)

        @block.gpsimd
        def _(pool):
            def rest(ms, past=0):
                for half in range(2):
                    cols = slice(512 * half, 512 * half + 512)
                    pool.wait_ge(sem("hi_ready"), past * 2 + (2 * ms + half + 1))
                    pool.tensor_tensor(wsplit[:, ms % 2, 1, cols], slot(SPLIT[ms])[:, cols],
                                       wsplit[:, ms % 2, 0, cols].bitcast(F32), ALU.subtract)\
                        .then_inc(sem("lo_ready"), 1)

            pool.memset(pad[:, :, 0:3], 0.0).then_inc(sem("pad_zero"), 1)
            pool.memset(pc, 0.0).then_inc(sem("nsa_zero"), 1)
            rest(0)
            rest(1)
            for ms in range(2, N_GDN + N_NSA + N_MERGE):
                rest(ms)
            pool.wait_ge(sem("consts_in"), 16)
            pool.wait_ge(sem("g_ready"), 1)
            for i in range(TT_):
                for h in range(H):
                    m = pool.tensor_scalar(grhs[:, i, h, :], tri, gg[:, i, h:h + 1], None, ALU.mult)
                m.then_inc(sem("grhs_ready"), 1)
            pool.wait_ge(sem("bias_read"), 1)
            pool.dma_start(bias_scratch, rrs[0:H, :]).then_inc(sem("bias_row_out"), 16)
            pool.wait_ge(sem("bias_row_out"), 16)
            pool.wait_ge(sem("tiles_used"), T_CMP)
            pool.dma_start(BTrev, bass.AP(bias_scratch.tensor, 0, [[1, P], [N_E1, H], [1, T]]))\
                .then_inc(sem("BTrev_in"), 16)
            pool.wait_ge(sem("gcl_evac"), 1)
            pool.memset(vcbd, 0.0).then_inc(sem("vcbd_zero"), 1)
            pool.wait_ge(sem("vcbd_zero"), 1)
            pool.wait_ge(sem("kvcmp_evac"), 4)
            for h in range(H):
                g = h // 4
                pool.dma_start(vcbd[16 * h:16 * h + NCMP, h * DH:(h + 1) * DH], vcs[0:NCMP, g * DH:(g + 1) * DH])\
                    .then_inc(sem("vcbd_in"), 16)
            pool.wait_ge(sem("am_evac"), 4)
            for g in range(4):
                i, p = g // 2, g % 2
                pool.tensor_tensor(TT[:, g], AT[:, i, p:H:2, :], over(level[:, 0, :], HP), ALU.mult)\
                    .then_inc(sem("TT0_part"), 1)
                pool.wait_ge(sem("TT0_part"), g + 1)
                pool.tensor_tensor(TT[:, g], over(ident, HP), TT[:, g], ALU.subtract).then_inc(sem("TT0_ready"), 1)
            pool.wait_ge(sem("gbc_done"), TT_)
            for lv in range(1, N_LEV):
                for g in range(4):
                    i, p = g // 2, g % 2
                    if lv >= 2:
                        pool.wait_ge(sem("Y_done"), (lv - 2) * 4 + g + 1)
                    pool.tensor_tensor(AbT[:, g], AT[:, i, p:H:2, :], over(level[:, lv, :], HP), ALU.mult)\
                        .then_inc(sem("AbT_ready"), 1)
            pool.wait_ge(sem("Y_done"), 4 * (N_LEV - 1))
            pool.memset(vn, 0.0).then_inc(sem("scan_zero"), 1)
            pool.memset(S, 0.0).then_inc(sem("scan_zero"), 1)
            for ms in range(N_GDN + N_NSA + N_MERGE, M_U + 2):
                rest(ms)
            with pool.Fori(0, 2 * NKEYS // GROUP - 1, 1) as group:
                for s in range(GROUP):
                    rest(M_U + s + 2, group * GROUP)
            for s in range(GROUP - 2):
                rest(M_U + 2 * NKEYS - GROUP + s + 2)
            pool.wait_ge(sem("weighed"), 2 * HALF + 2)
            pool.dma_start(nfin, nfinal.partition_broadcast(P)).then_inc(sem("nfinal_in"), 16)


def _constants():
    import math
    import numpy as np
    k = np.arange(P)[:, None]
    i = np.arange(P)[None, :]
    chunk = (k // CH) == (i // CH)
    c = np.zeros((P, N_CONST), np.float32)
    c[:, C_ID:C_ID + P] = np.eye(P)
    c[:, C_TRI:C_TRI + P] = chunk & (k <= i)
    c[:, C_SAME:C_SAME + P] = chunk
    c[:, C_ONES:C_ONES + P] = 1.0
    c[:, C_IOTA:C_IOTA + P] = i
    c[:, C_FLIP:C_FLIP + P] = (k + i) == P - 1
    for lv in range(N_LEV):
        b = 1 << lv
        c[:, C_LEV + lv * P:C_LEV + (lv + 1) * P] = (k // (2 * b) == i // (2 * b)) & ((i // b) % 2 == 1) & ((k // b) % 2 == 0)
    for t in range(TT_):
        for n in range(NCMP):
            c[:, C_CMASK + 16 * t + n] = (16 * n + 31) <= (np.arange(P) + P * t)

    def bucket(d):
        far = 16 + int(np.float32(np.log(np.float32(max(d, 1) / 16))) / np.float32(math.log(8.0)) * np.float32(16))
        return d if d < 16 else min(far, 31)

    e = np.zeros((33, N_E1 + N_E2), np.float32)
    for m in range(N_E1):
        d = T - 1 - m
        e[bucket(d) if d >= 0 else 32, m] = 1.0
    for m in range(N_E2):
        d = m - (T - 1)
        e[bucket(d) if d >= 0 else 32, N_E1 + m] = 1.0
    return c, e


def _layout(a):
    import numpy as np
    w_in = a["w_in"][0]
    stream = np.zeros((N_TILES, P, 1024), np.float32)

    def by_columns(w, cols, first):
        n = len(cols) // P
        t = w[:, cols].reshape(KT, P, n, P)
        stream[first:first + n] = t.transpose(2, 1, 0, 3).reshape(n, P, 1024)

    z0, b0, d0, q0, kv0, g0, m0 = 1536, 2048, 2056, 2064, 2576, 3344, 3368
    ar = np.arange
    by_columns(w_in, ar(0, 1536), T_GDN)
    v_cols = [ar(kv0 + ((b * 2 + 1) * 2) * DH, kv0 + ((b * 2 + 1) * 2) * DH + P) for b in (1, 2)]
    tok = np.concatenate([ar(z0, z0 + 512), ar(b0, b0 + 8), ar(g0, g0 + 24), ar(d0, d0 + 8)] + v_cols)
    stream[T_TOK:T_TOK + KT, :, 0:len(tok)] = w_in[:, tok].reshape(KT, P, len(tok))
    q_cols = [ar(q0 + h * DH, q0 + (h + 1) * DH) for m in range(4) for h in (m, m + 4)]
    k_cols = [ar(kv0 + (b * 2 * 2) * DH, kv0 + (b * 2 * 2) * DH + P) for b in range(3)]
    by_columns(w_in, np.concatenate(q_cols + k_cols + [ar(kv0 + 2 * DH, kv0 + 4 * DH)]), T_NSA)
    by_columns(w_in, ar(m0, m0 + 2048), T_MERGE)
    for s, name in enumerate(("cmp_w_k", "cmp_w_v")):
        w = a[name][0].transpose(1, 0, 2).reshape(DH, 2, 1024).transpose(1, 0, 2)
        stream[T_CMP + 2 * s:T_CMP + 2 * s + 2] = np.concatenate([w, w], axis=1)
    for s, name in enumerate(("w_branch_a", "w_branch_b")):
        w = a[name][0].reshape(HP, P, N_AB, P).transpose(2, 1, 0, 3).reshape(N_AB, P, 512)
        stream[T_AB:T_AB + N_AB, :, 512 * s:512 * s + 512] = w
    stream[T_OUT:T_OUT + N_OUT] = a["w_out"][0].reshape(N_OUT, P, D)
    by_columns(a["w_query"][0], ar(2048), T_WQ)
    sk = a["sub_keys"][0].reshape(N_SK, 8, P, P).transpose(0, 3, 1, 2).reshape(N_SK, P, 1024)
    stream[T_SK:T_SK + N_SK] = sk
    u = a["expert_u"][0].reshape(NKEYS, NKEYS, KT, P)
    stream[T_U:T_U + NKEYS] = u.transpose(1, 3, 2, 0).reshape(NKEYS, P, 1024)
    stream[T_V:T_V + NKEYS] = a["expert_v"][0].reshape(NKEYS, NKEYS, D).transpose(1, 0, 2)

    par = np.zeros((P, N_PAR), np.float32)
    par[:, R_NM:R_NM + 8] = a["norm_mix"][0].reshape(8, P).T
    par[:, R_NF:R_NF + 8] = a["norm_ffn"][0].reshape(8, P).T
    par[:, R_CW:R_CW + 48] = a["conv_w"][0].reshape(4, 12, P).transpose(2, 1, 0).reshape(P, 48)
    for s, name in enumerate(("cmp_pe_k", "cmp_pe_v")):
        pe = a[name][0].T
        par[:, R_PE + 32 * s:R_PE + 32 * s + 32] = np.concatenate([pe, pe], axis=0)
    par[:, R_ALOG:R_ALOG + 8] = a["a_log"][0][None, :]
    par[:, R_DT:R_DT + 8] = a["dt_bias"][0][None, :]
    par[:, R_GN:R_GN + DH] = a["gdn_norm"][0][None, :]
    relb = np.concatenate([a["rel_bias"], np.full((1, H), NEG, np.float32)], axis=0)
    consts, onehot = _constants()
    return {"x": a["x"][0], "stream": stream, "consts": consts, "params": par, "onehot": onehot,
            "relb": relb, "nfinal": a["norm_final"]}


def kernel(**inputs):
    import numpy as np
    import concourse.bacc as bacc
    from concourse.bass_utils import run_bass_kernel_spmd
    arrays = _layout({k: np.asarray(v) for k, v in inputs.items()})
    nc = bacc.Bacc("TRN2", target_bir_lowering=False, num_devices=1)
    aps = {k: nc.dram_tensor("in_" + k, v.shape, F32, kind="ExternalInput").ap() for k, v in arrays.items()}
    out = nc.dram_tensor("out", (T, D), F32, kind="ExternalOutput").ap()
    scratch = nc.dram_tensor("bias_scratch", (H, N_E1), F32, kind="Internal").ap()
    build(nc, bias_scratch=scratch, out=out, **aps)
    r = run_bass_kernel_spmd(nc, [{"in_" + k: np.ascontiguousarray(v) for k, v in arrays.items()}], core_ids=[0])
    return r.results[0]["out"].reshape(1, T, D)
```

```python
from contextlib import ExitStack

import concourse.bass as bass
from concourse import mybir

P = 128
T = 256
TT_ = T // P
D = 1024
KT = D // P
H = 8
HP = H // 2
DH = 64
CH = 64
NSLOT = 4
NKEYS = 128
TOPK = 16
NCMP = (T - 32) // 16 + 1
EPS = 1e-6
NEG = -1e30

N_GDN, N_TOK, N_NSA, N_MERGE, N_CMP, N_AB, N_OUT, N_WQ, N_SK = 12, 8, 8, 16, 4, 8, 8, 16, 2
T_GDN = 0
T_TOK = T_GDN + N_GDN
T_NSA = T_TOK + N_TOK
T_MERGE = T_NSA + N_NSA
T_CMP = T_MERGE + N_MERGE
T_AB = T_CMP + N_CMP
T_OUT = T_AB + N_AB
T_WQ = T_OUT + N_OUT
T_SK = T_WQ + N_WQ
T_U = T_SK + N_SK
T_V = T_U + NKEYS
N_TILES = T_V + NKEYS
GROUP = 8
HALF = NKEYS // 2

SPLIT = list(range(T_GDN, T_CMP)) + list(range(T_AB, T_SK))
M_TOK, M_NSA, M_MERGE = T_TOK, T_NSA, T_MERGE
M_AB, M_WQ = SPLIT.index(T_AB), SPLIT.index(T_WQ)
M_U = len(SPLIT)
SPLIT = SPLIT + list(range(T_U, N_TILES))

TOK_COLS = 808

C_ID, C_TRI, C_SAME, C_ONES, C_IOTA, C_LEV = 0, 128, 256, 384, 512, 640
N_LEV = 6
C_CMASK = C_LEV + N_LEV * 128
C_FLIP = C_CMASK + 32
C_HEAD = C_FLIP + 128
C_GROUP = C_HEAD + H
N_CONST = C_GROUP + P
R_NM, R_NF, R_CW, R_PE, R_ALOG, R_DT, R_GN = 0, 8, 16, 64, 128, 136, 144
N_PAR = 208
N_E1 = 384

F32 = mybir.dt.float32
F32R = mybir.dt.float32r
U32 = mybir.dt.uint32
ALU = mybir.AluOpType
ACT = mybir.ActivationFunctionType
AX = mybir.AxisListType


def build(nc, x, stream, consts, params, onehot, relb, nfinal, bias_scratch, out, debug=None):
    ctx = ExitStack()
    with ctx:
        def sb(name, shape, dt=F32):
            return ctx.enter_context(nc.sbuf_tensor(name, shape, dt))

        semaphores = {}

        def sem(name):
            if name not in semaphores:
                semaphores[name] = ctx.enter_context(nc.semaphore(name))
            return semaphores[name]

        ring = sb("ring", [P, NSLOT, 1024])
        xr = sb("xr", [P, TT_, D])
        cst = sb("cst", [P, N_CONST])
        par = sb("par", [P, N_PAR])
        small = sb("small", [P, 640])
        arena = sb("arena", [P, 35200])
        wsplit = sb("wsplit", [P, 2, 2, 1024], F32R)
        hsplit = sb("hsplit", [P, 2, KT, T], F32R)
        asplit = sb("asplit", [P, 2, 2, T], F32R)
        ps = ctx.enter_context(nc.psum_tensor("ps", [P, 8, 512], F32))

        def at(off, n):
            return arena[:, off:off + n]

        ident = cst[:, C_ID:C_ID + P]
        tri = cst[:, C_TRI:C_TRI + P]
        same = cst[:, C_SAME:C_SAME + P]
        ones = cst[:, C_ONES:C_ONES + P]
        iota = cst[:, C_IOTA:C_IOTA + P]
        level = cst[:, C_LEV:C_LEV + N_LEV * P].rearrange("p (l j) -> p l j", l=N_LEV)
        flip = cst[:, C_FLIP:C_FLIP + P]
        head_of = cst[:, C_HEAD:C_HEAD + H]
        group_rows = cst[:, C_GROUP:C_GROUP + P]
        cmask = cst[:, C_CMASK:C_CMASK + 32].rearrange("p (i n) -> p i n", i=TT_)

        hT = at(0, 2048).rearrange("p (k t) -> p k t", k=KT)
        Yb = at(0, 2048).rearrange("p (g h j) -> p g h j", g=4, h=HP)
        pad = at(2048, 12 * 259).rearrange("p (n t) -> p n t", n=12)
        conv = at(5160, 3072).rearrange("p (n t) -> p n t", n=12)
        kn, kb, qn, qd, kbg, vb = [
            at(2048 + 1024 * n, 1024).rearrange("p (i h d) -> p i h d", i=TT_, h=H) for n in range(6)]
        qkvt = at(8448, 3072).rearrange("p (i c) -> p i c", i=TT_)
        Tm = at(8448, 2048).rearrange("p (g h j) -> p g h j", g=4, h=HP)
        vn = at(8448, 512)
        S = at(8960, 512).rearrange("p (q e) -> p q e", q=HP)
        nsaf = at(11520, 2048).rearrange("p (n t) -> p n t", n=8)
        mg = at(13568, 4096).rearrange("p (n t) -> p n t", n=16)
        zs = at(17664, 1024).rearrange("p (i c) -> p i c", i=TT_)
        tk = at(18688, 592).rearrange("p (i c) -> p i c", i=TT_)
        BT = at(19328, 2048).rearrange("p (h j) -> p h j", h=H)
        BTrev = at(0, 2048).rearrange("p (h j) -> p h j", h=H)
        XT = at(21376, 4096).rearrange("p (x i q t) -> p x i q t", x=4, i=TT_, q=HP)
        onsa = at(21376, 1024).rearrange("p (i c) -> p i c", i=TT_)
        oa = at(23424, 1024).rearrange("p (i c) -> p i c", i=TT_)
        qdT = XT[:, 3]
        DT = at(25472, 2048).rearrange("p (i h t) -> p i h t", i=TT_, h=H)
        nwT = at(25472, 1024).rearrange("p (i q t) -> p i q t", i=TT_, q=HP)
        AT = at(27520, 2048).rearrange("p (i h t) -> p i h t", i=TT_, h=H)
        mixT = at(27520, 2048).rearrange("p (k t) -> p k t", k=KT)
        attnT = at(29568, 2048).rearrange("p (i h t) -> p i h t", i=TT_, h=H)
        TT = at(31616, 2048).rearrange("p (g h j) -> p g h j", g=4, h=HP)
        AbT = at(4096, 2048).rearrange("p (g h j) -> p g h j", g=4, h=HP)
        grhs = at(27520, 2048).rearrange("p (i h t) -> p i h t", i=TT_, h=H)
        kd = at(33664, 1024).rearrange("p (i h d) -> p i h d", i=TT_, h=H)
        kd_f = at(33664, 1024).rearrange("p (i c) -> p i c", i=TT_)
        Sb = at(2560, 1536).rearrange("p (b j) -> p b j", b=3)
        PT = at(26496, 1024).rearrange("p (b j) -> p b j", b=2)
        vcbd = at(10496, 512)
        kcmpT = at(11008, 32)
        vcs = at(11040, DH)
        kc2 = at(8448, P)
        pc = at(34944, 256).rearrange("p (i h n) -> p i h n", i=TT_, h=H)
        pc_f = at(34944, 256).rearrange("p (i c) -> p i c", i=TT_)
        pcT = at(11152, 256).rearrange("p (i t) -> p i t", i=TT_)
        rrs = at(26400, 384)
        E = at(25472, N_E1)
        kcbd = at(31616, 2048).rearrange("p (s l g n) -> p s l g n", s=2, l=32, g=2)
        junk = at(27520, 2048).rearrange("p (i c) -> p i c", i=TT_)
        sq = at(29568, 2048).rearrange("p (i c) -> p i c", i=TT_)

        act_w = at(0, NKEYS * T).rearrange("p (e t) -> p e t", e=NKEYS)
        qT = at(16384, 4096).rearrange("p (n t) -> p n t", n=16)
        sc = at(20480, 4096).rearrange("p (i n k) -> p i n k", i=TT_, n=16)
        oh = at(24576, 2048).rearrange("p (m a) -> p m a", a=TOPK)
        tkv = at(26624, 512).rearrange("p (i n k) -> p i n k", i=TT_, n=16)
        tki = at(27136, 512).rearrange("p (i n k) -> p i n k", i=TT_, n=16)
        tki_u = at(27648, 512).bitcast(U32).rearrange("p (i n k) -> p i n k", i=TT_, n=16)
        rep = at(28160, 128)
        cand = at(28288, 256)
        cand2 = at(28544, 256)
        topv = at(28800, 256).rearrange("p (i h k) -> p i h k", i=TT_, h=H)
        topi_u = at(29056, 256).bitcast(U32).rearrange("p (i h k) -> p i h k", i=TT_, h=H)
        ab_u = at(29312, 512).bitcast(U32).rearrange("p (s i c) -> p s i c", s=2, i=TT_)
        ab_f = at(29824, 512).rearrange("p (s i c) -> p s i c", s=2, i=TT_)
        e_f = at(33536, 512).rearrange("p (s i c) -> p s i c", s=2, i=TT_)
        gate = at(34048, 256).rearrange("p (i h k) -> p i h k", i=TT_, h=H)
        gate_f = at(34048, 256).rearrange("p (i c) -> p i c", i=TT_)
        egT = at(32768, 768).rearrange("p (s t) -> p s t", s=3)
        g2 = at(33536, 2 * T).rearrange("p (t x) -> p t x", x=2)
        nfin = at(34048, 1024)
        G_lo = cst[:, C_LEV:C_LEV + 512].rearrange("p (b t e) -> p b t e", b=2, t=4)
        peerT = at(0, 2048).rearrange("p (k t) -> p k t", k=KT)

        def sm(off, n):
            return small[:, off:off + n]

        rms = sm(0, 8)
        sg = sm(8, 64).rearrange("p (i c) -> p i c", i=TT_)
        gm = sm(88, 16).rearrange("p (i h) -> p i h", i=TT_)
        ge = sm(104, 16).rearrange("p (i h) -> p i h", i=TT_)
        gz = sm(120, 16).rearrange("p (i h) -> p i h", i=TT_)
        gt = sm(136, 16).rearrange("p (i h) -> p i h", i=TT_)
        gp = sm(152, 16).rearrange("p (i h) -> p i h", i=TT_)
        gg = sm(168, 16).rearrange("p (i h) -> p i h", i=TT_)
        ea = sm(184, 8)
        gcl = sm(192, 32).rearrange("p (i c) -> p i c", i=TT_)
        ngc = sm(224, 16).rearrange("p (i h) -> p i h", i=TT_)
        eg = sm(240, 16).rearrange("p (i h) -> p i h", i=TT_)
        neg_eg = sm(256, 16).rearrange("p (i h) -> p i h", i=TT_)
        ekd = sm(272, 16).rearrange("p (i h) -> p i h", i=TT_)
        egl = sm(288, 16).rearrange("p (i q c) -> p i q c", i=TT_, q=HP)
        ssq = sm(304, 32).rearrange("p (i c) -> p i c", i=TT_)
        rq = sm(336, 32).rearrange("p (i c) -> p i c", i=TT_)
        mx = sm(368, 32).rearrange("p (n b) -> p n b", n=16)
        sums = sm(400, 48).rearrange("p (i h b) -> p i h b", i=TT_, h=H)
        coef = sm(448, 48).rearrange("p (i h b) -> p i h b", i=TT_, h=H)
        cmx = sm(496, 16).rearrange("p (i h) -> p i h", i=TT_)
        gs = sm(512, 16).rearrange("p (i h) -> p i h", i=TT_)
        gr = sm(528, 16).rearrange("p (i h) -> p i h", i=TT_)
        oss = sm(544, 16).rearrange("p (i h) -> p i h", i=TT_)
        osr = sm(560, 16).rearrange("p (i h) -> p i h", i=TT_)
        rel = sm(576, 8)

        def par_cols(off, n):
            return par[:, off:off + n]

        def bank(b, a=0, n=512):
            return ps[:, b, a:a + n]

        def slot(n):
            return ring[:, n % NSLOT, :]

        def each(ap, n):
            return ap.unsqueeze(2).broadcast_to([ap.shape[0], ap.shape[1], n])

        def over(ap, n):
            return ap.unsqueeze(1).broadcast_to([ap.shape[0], n, ap.shape[1]])

        ohA = [asplit[:, 0].rearrange("p a (t j) -> p (a t) j", j=P),
               hsplit[:, 0, 0:2].rearrange("p a (t j) -> p (a t) j", j=P)]
        ohB = [asplit[:, 1].rearrange("p a (t x j) -> p (a t) x j", x=2, j=HALF),
               hsplit[:, 1, 0:2].rearrange("p a (t x j) -> p (a t) x j", x=2, j=HALF)]

        def halves(n, half):
            wide = TOK_COLS if T_TOK <= n < T_NSA else 1024
            return slice(512 * half, min(512 * half + 512, wide))

        block = ctx.enter_context(nc.Block())

        @block.sync
        def _(sp):
            for i in range(TT_):
                sp.dma_start(xr[:, i, :], x[i * P:(i + 1) * P, :]).then_inc(sem(f"x{i}_in"), 16)
            sp.dma_start(cst[:, :], consts).then_inc(sem("consts_in"), 16)
            sp.dma_start(par[:, :], params).then_inc(sem("params_in"), 16)
            sp.dma_start(E[0:33, :], onehot).then_inc(sem("onehot_in"), 16)
            sp.dma_start(rel[0:33, :], relb).then_inc(sem("onehot_in"), 16)
            def load(n):
                sp.dma_start(slot(n), stream[n]).then_inc(sem(f"slot{n % NSLOT}_in"), 16)

            for n in range(T_U + NSLOT):
                if n >= NSLOT:
                    old = n - NSLOT
                    if old in SPLIT:
                        sp.wait_ge(sem("lo_ready"), 2 * SPLIT.index(old) + 2)
                    else:
                        sp.wait_ge(sem("tiles_used"), old + 1)
                load(n)
                if n == T_MERGE + 4:
                    sp.wait_ge(sem("bias_read"), 1)
                    sp.dma_start(bias_scratch, rrs[0:H, :]).then_inc(sem("bias_row_out"), 16)
                if n == T_CMP + 3:
                    sp.wait_ge(sem("bias_row_out"), 16)
                    sp.wait_ge(sem("tiles_used"), T_CMP)
                    sp.dma_start(BTrev, bass.AP(bias_scratch.tensor, 0, [[1, P], [N_E1, H], [1, T]]))\
                        .then_inc(sem("BTrev_in"), 16)
            with sp.Fori(0, (N_TILES - T_U) // NSLOT - 1, 1) as turn:
                for s in range(NSLOT):
                    n = T_U + NSLOT + s
                    sp.wait_ge(sem("lo_ready"), turn * (2 * NSLOT) + 2 * (M_U + s + 1))
                    sp.dma_start(slot(n), stream[turn * NSLOT + n]).then_inc(sem(f"slot{n % NSLOT}_in"), 16)
            for i in range(TT_):
                sp.wait_ge(sem("out_ready"), i + 1)
                sp.dma_start(out[i * P:(i + 1) * P, :], xr[:, i, :]).then_inc(sem("stored"), 16)
            sp.wait_ge(sem("stored"), 16 * TT_)

        @block.tensor
        def _(pe):
            def mm(o, lhsT, rhs, start=True, stop=True):
                return pe.matmul(o, lhsT, rhs, start=start, stop=stop, skip_group_check=True)

            def arrived(n):
                pe.wait_ge(sem(f"slot{n % NSLOT}_in"), 16 * (n // NSLOT + 1))

            pe.wait_ge(sem("consts_in"), 16)
            def turn_normed(turn, b0):
                for f in range(4):
                    half, i = f // 2, f % 2
                    pe.wait_ge(sem("xn1_ready" if i else "xn0_ready"), turn + 1)
                    for j in range(4):
                        k = half * 4 + j
                        m = pe.transpose(bank(b0 + f, j * P, P), junk[:, i, k * P:(k + 1) * P], ident)
                    m.then_inc(sem("hT_done"), 1)

            turn_normed(0, 4)

            def by_h(b, ms, past=0, turn=None):
                for half in range(2):
                    if turn is not None:
                        pe.wait_ge(sem("hT_split"), 4 * turn + 2 * half + 2)
                    pe.wait_ge(sem("lo_ready"), past * 2 + (2 * ms + half + 1))
                    ks = range(4 * half, 4 * half + 4)
                    for a, c in ((0, 0), (1, 0), (0, 1)):
                        for k in ks:
                            m = mm(bank(b, 0, T), wsplit[:, ms % 2, a, k * P:(k + 1) * P], hsplit[:, c, k, :],
                                   start=(half == 0 and a == 0 and c == 0 and k == 0), stop=(half == 1 and c == 1 and k == KT - 1))
                    m.then_inc(sem("tiles_used" if half else "half_used"), 1)

            def project(n, tile):
                if n >= 4:
                    pe.wait_ge(sem("proj_evac"), n - 3)
                by_h(n % 4, SPLIT.index(tile), turn=0 if n == 0 else None)

            for n in range(N_GDN):
                project(n, T_GDN + n)
            for k in range(N_TOK):
                ms = M_TOK + k
                for half in range(2):
                    n = TOK_COLS - 512 if half else 512
                    pe.wait_ge(sem("lo_ready"), 2 * ms + half + 1)
                    for i in range(TT_):
                        for a, c in ((0, 0), (1, 0), (0, 1)):
                            m = mm(bank(4 + 2 * i + half, 0, n), hsplit[:, c, k, i * P:(i + 1) * P],
                                   wsplit[:, ms % 2, a, 512 * half:512 * half + n],
                                   start=(k == 0 and a == 0 and c == 0), stop=(k == KT - 1 and c == 1))
                    m.then_inc(sem("tiles_used" if half else "half_used"), 1)
            for n in range(N_NSA):
                project(N_GDN + n, T_NSA + n)

            for f in range(6):
                part, i = f // 2, f % 2
                pe.wait_ge(sem("silu_done"), 4 * (part + 1))
                pe.wait_ge(*[(sem("z_evac"), 1), (sem("tok_evac"), 1), (sem("z_evac"), 2), (sem("tok_evac"), 2),
                             (sem("tt_evac"), 1), (sem("tt_evac"), 2)][f])
                for j in range(4):
                    m = pe.transpose(bank(4 + f % 4, j * P, P), conv[:, part * 4 + j, i * P:(i + 1) * P], ident)
                m.then_inc(sem("tt_done"), 1)

            def bias_row():
                pe.wait_ge(sem("onehot_in"), 32)
                pe.wait_ge(sem("tt_evac"), 6)
                mm(bank(7, 0, N_E1)[0:H], rel[0:33, :], E[0:33, 0:N_E1]).then_inc(sem("bias_row_done"), 1)

            def decay_sums():
                pe.wait_ge(sem("g_ready"), 1)
                for i in range(TT_):
                    mm(bank(4, 16 * i, 8), tri, gg[:, i, :], start=(i == 0))
                    m = mm(bank(4, 16 * i + 8, 8), same, gg[:, i, :], start=False)
                m.then_inc(sem("gcl_done"), 1)

            def decay_rows(i):
                pe.wait_ge(sem("grhs_ready"), i + 1)
                for half in range(2):
                    if i == 1:
                        pe.wait_ge(*((sem("gcl_evac"), 1) if half else (sem("bias_read"), 1)))
                    m = mm(bank(4 + (1 + 2 * i + half) % 4), ones, grhs[:, i, 4 * half:4 * half + 4, :])
                m.then_inc(sem("gbc_done"), 1)

            def rows_back(first):
                for f in range(first, first + 4):
                    which, i = f // 2, f % 2
                    pe.wait_ge(sem("gdn_rows_ready"), f + 1)
                    if f >= 4:
                        pe.wait_ge(sem("fT_evac"), f - 3)
                    else:
                        pe.wait_ge(sem("gbc_read"), 2)
                    src = at(2048 + 1024 * which, 1024).rearrange("p (i c) -> p i c", i=TT_)
                    for q in range(HP):
                        m = pe.transpose(bank(4 + f % 4, q * P, P), src[:, i, q * P:(q + 1) * P], ident)
                    m.then_inc(sem("fT_done"), 1)

            def chunk_products(which):
                pe.wait_ge(sem("fT_evac"), 8)
                for r in range(4 * which, 4 * which + 4):
                    i, p = (r // 2) % 2, r % 2
                    if r >= 4:
                        pe.wait_ge(sem("am_evac"), r - 3)
                    rows = slice(DH * p, DH * p + DH)
                    for q in range(HP):
                        m = mm(bank(4 + r % 4, q * P, P), XT[rows, 0, i, q, :], XT[rows, 1 + which, i, q, :],
                               start=(q == 0))
                    m.then_inc(sem("am_done"), 1)

            for n in range(N_MERGE):
                project(N_GDN + N_NSA + n, T_MERGE + n)
                if n == 0:
                    bias_row()
                elif n == 1:
                    decay_sums()
                elif n == 2:
                    decay_rows(0)
                elif n == 3:
                    decay_rows(1)
                elif n == 8:
                    rows_back(0)
                elif n == 10:
                    rows_back(4)
                elif n == 12:
                    chunk_products(0)
            chunk_products(1)

            pe.wait_ge(sem("proj_evac"), N_GDN + N_NSA + N_MERGE)
            pe.wait_ge(sem("kcbd_ready"), 8)
            for s in range(2):
                if s == 1:
                    pe.wait_ge(sem("BTrev_in"), 16)
                    pe.wait_ge(sem("am_evac"), 8)
                    for b in range(4):
                        mm(bank(4 + b), flip, BTrev[:, 2 * b:2 * b + 2, :]).then_inc(sem("BT_done"), 1)
                for half in range(2):
                    if s == 1 and half == 1:
                        pe.wait_ge(sem("kc_ready"), 1)
                        pe.transpose(bank(2, 0, 32), kc2[0:32, :], ident[0:32, 0:32]).then_inc(sem("kcT_done"), 1)
                    tile = T_CMP + 2 * s + half
                    arrived(tile)
                    w = slot(tile).rearrange("p (l e) -> p l e", l=16)
                    for l in range(16):
                        ll = half * 16 + l
                        m = mm(bank(s, 0, DH)[0:32], kcbd[:, s, ll, :, :], w[:, l, :], start=(ll == 0), stop=(ll == 31))
                    m.then_inc(sem("tiles_used"), 1)
            pe.wait_ge(sem("kcmpT_ready"), 1)
            pe.wait_ge(sem("BT_in"), 4)
            for i in range(TT_):
                for g in range(2):
                    rows = slice(DH * g, DH * g + DH)
                    for q in range(4):
                        m = mm(bank(4 + 2 * i + g, q * 16, NCMP), nsaf[rows, q, i * P:(i + 1) * P],
                               kcmpT[rows, 16 * g:16 * g + NCMP], start=(q == 0))
                    m.then_inc(sem("sc_done"), 1)
            pe.wait_ge(sem("vc_ready"), 1)
            mm(bank(3, 0, DH), group_rows[0:32, :], vcs[0:32, :]).then_inc(sem("vc_copied"), 1)

            def nsa_scores(n):
                i, h = n // H, n % H
                nk = P * (i + 1)
                if n >= 2:
                    pe.wait_ge(sem("s_evac"), n - 1)
                rows = slice(DH * (h // 4), DH * (h // 4) + DH)
                for b in range(2):
                    m = mm(bank(n % 2, b * nk, nk), nsaf[rows, h % 4, i * P:(i + 1) * P],
                           nsaf[rows, 5 + b, 0:nk], start=(b == 0))
                m.then_inc(sem("s_done"), 1)

            def nsa_transpose(n):
                i = n // H
                pe.wait_ge(sem("p_ready"), n + 1)
                if n >= 2:
                    pe.wait_ge(sem("pT_evac"), n - 1)
                for j in range(2 * (i + 1)):
                    m = pe.transpose(bank(2 + n % 2, j * P, P), Sb[:, n % 3, j * P:(j + 1) * P], ident)
                m.then_inc(sem("pT_done"), 1)

            def nsa_values(n):
                i, h = n // H, n % H
                g = h // 4
                pe.wait_ge(sem("pT_evac"), n + 1)
                if n == H:
                    pe.wait_ge(sem("oc_evac"), TT_)
                for b in range(2):
                    for j in range(i + 1):
                        m = mm(bank(4 + 2 * i + b, h * DH, DH), PT[:, n % 2, (b * (i + 1) + j) * P:][:, 0:P],
                               tk[:, j, 40 + 128 * b + DH * g:][:, 0:DH], start=(h == 0 and j == 0), stop=(j == i))
                m.then_inc(sem("pv_done"), 1)

            nsa_scores(0)
            for i in range(TT_):
                pe.wait_ge(sem("pc_ready"), TT_)
                pe.transpose(bank(4 + i, 0, P), pc_f[:, i, :], ident).then_inc(sem("pcT_done"), 1)
            nsa_scores(1)
            pe.wait_ge(sem("vcbd_ready"), 1)
            for i in range(TT_):
                pe.wait_ge(sem("pcT_evac"), i + 1)
                mm(bank(6 + i), pcT[:, i, :], vcbd).then_inc(sem("oc_done"), 1)
            for n in range(2, TT_ * H + 3):
                if n < TT_ * H:
                    nsa_scores(n)
                if n < TT_ * H + 2:
                    nsa_transpose(n - 2)
                if n >= 3:
                    nsa_values(n - 3)

            for g in range(4):
                pe.wait_ge(sem("TT0_ready"), g + 1)
                if g == 0:
                    pe.wait_ge(sem("pT_evac"), TT_ * H)
                for q in range(HP):
                    m = pe.transpose(bank(g, q * P, P), TT[:, g, q, :], ident)
                m.then_inc(sem("T_done"), 1)
            def turn_back(lv, g):
                pe.wait_ge(sem("TT_ready"), (lv - 1) * 4 + g + 1)
                for q in range(HP):
                    m = pe.transpose(bank(g, q * P, P), TT[:, g, q, :], ident)
                m.then_inc(sem("T_done"), 1)

            for lv in range(1, N_LEV):
                for g in range(4):
                    pe.wait_ge(sem("AbT_ready"), (lv - 1) * 4 + g + 1)
                    pe.wait_ge(sem("T_ready"), (lv - 1) * 4 + g + 1)
                    for q in range(HP):
                        m = mm(bank(g, q * P, P), AbT[:, g, q, :], Tm[:, g, q, :], start=(q == 0))
                    m.then_inc(sem("Y_done"), 1)
                if lv == 1:
                    for i in range(TT_):
                        pe.wait_ge(sem("onsa_ready"), TT_)
                        for k in range(HP):
                            m = pe.transpose(bank(4 + i, k * P, P), onsa[:, i, k * P:(k + 1) * P], ident)
                        m.then_inc(sem("obT_done"), 1)
                for g in range(4):
                    n = (lv - 1) * 4 + g
                    pe.wait_ge(sem("Y_evac"), n + 1)
                    if n == 0:
                        pe.wait_ge(sem("obT_split"), TT_)
                    for q in range(HP):
                        m = mm(bank(4 + g, q * P, P), Yb[:, g, q, :], TT[:, g, q, :], start=(q == 0))
                    m.then_inc(sem("YTT_done"), 1)
                    if lv < N_LEV - 1 and g >= 1:
                        turn_back(lv, g - 1)
                if lv < N_LEV - 1:
                    turn_back(lv, 3)

            for i in range(TT_):
                for p in range(2):
                    pe.wait_ge(sem("TT_ready"), 4 * (N_LEV - 2) + 2 * i + p + 1)
                    for q in range(HP):
                        m = mm(ps[DH * p:DH * p + DH, i, q * P:(q + 1) * P], kbg[:, i, 2 * q + p, :],
                               TT[:, 2 * i + p, q, :], start=(q == 0))
                m.then_inc(sem("nwT_done"), 1)

            def branch(s, j):
                n = N_AB * (1 - s) + j
                ms, half = M_AB + n // 2, n % 2
                pe.wait_ge(sem("lo_ready"), 2 * ms + half + 1)
                if n >= 4:
                    pe.wait_ge(sem("branch_evac"), n - 3)
                for a, c in ((0, 0), (1, 0), (0, 1)):
                    for k in range(HP):
                        m = mm(bank((5, 6, 7, 0)[j % 4], 0, T), wsplit[:, ms % 2, a, (half * HP + k) * P:][:, 0:P],
                               hsplit[:, c, HP * (1 - s) + k, :], start=(a == 0 and c == 0 and k == 0),
                               stop=(c == 1 and k == HP - 1))
                m.then_inc(sem("tiles_used" if half else "half_used"), 1)

            pe.wait_ge(sem("TT_ready"), 4 * (N_LEV - 1))
            pe.wait_ge(sem("scan_zero"), 1)
            pe.wait_ge(sem("nwT_evac"), TT_)
            for c in range(T // CH):
                i, r0 = c // 2, CH * (c % 2)
                rows = slice(r0, r0 + CH)
                if c % 2 == 0:
                    for h in range(H):
                        m = mm(bank(2 - i, h * DH, DH), TT[:, 2 * i + h % 2, h // 2, :], vb[:, i, h, :],
                               start=(h == 0), stop=False)
                if c >= 1:
                    pe.wait_ge(sem("S_ready"), c)
                    for q in range(HP):
                        m = mm(ps[rows, 2 - i, q * P:(q + 1) * P], nwT[:, i, q, rows], S[:, q, :], start=False)
                m.then_inc(sem("vn_done"), 1)
                if c == 2:
                    pe.wait_ge(sem("o_evac"), 1)
                for q in range(HP):
                    m = mm(ps[rows, 3, q * P:(q + 1) * P], qdT[:, i, q, rows], S[:, q, :], start=(q == 0), stop=False)
                m.then_inc(sem("S_read"), 1)
                pe.wait_ge(sem("vn_evac"), c + 1)
                if c < T // CH - 1:
                    for q in range(HP):
                        m = mm(bank(4, q * P, P), kd_f[rows, i, q * P:(q + 1) * P], vn[rows, q * P:(q + 1) * P],
                               start=(q == 0))
                    m.then_inc(sem("dS_done"), 1)
                    branch(1, c)
                if c % 2 == 1:
                    for h in range(H):
                        m = mm(bank(3, h * DH, DH), attnT[:, i, h, :], vn[:, h * DH:(h + 1) * DH], start=False)
                    m.then_inc(sem("o_done"), 1)
            for j in range(T // CH - 1, N_AB - 1):
                branch(1, j)

            for i in range(TT_):
                pe.wait_ge(sem("oa_ready"), i + 1)
                for k in range(HP):
                    m = pe.transpose(bank(1 + i, k * P, P), oa[:, i, k * P:(k + 1) * P], ident)
                m.then_inc(sem("oaT_done"), 1)
            branch(1, N_AB - 1)
            pe.wait_ge(sem("oaT_split"), TT_)
            for j in range(N_AB):
                branch(0, j)
            for k in range(N_OUT):
                ms = M_AB + N_AB + k
                pe.wait_ge(sem("mix_split"), k + 1)
                for half in range(2):
                    pe.wait_ge(sem("lo_ready"), 2 * ms + half + 1)
                    for i in range(TT_):
                        for a, c in ((0, 0), (1, 0), (0, 1)):
                            m = mm(bank(1 + 2 * i + half), hsplit[:, c, k, i * P:(i + 1) * P],
                                   wsplit[:, ms % 2, a, half * 512:(half + 1) * 512],
                                   start=(k == 0 and a == 0 and c == 0), stop=(k == KT - 1 and c == 1))
                    m.then_inc(sem("tiles_used" if half else "half_used"), 1)

            turn_normed(1, 0)

            for n in range(N_WQ):
                if n >= 4:
                    pe.wait_ge(sem("q_evac"), n - 3)
                by_h(n % 4, M_WQ + n, turn=1 if n == 0 else None)
            for s in range(N_SK):
                arrived(T_SK + s)
                w = slot(T_SK + s).rearrange("p (n k) -> p n k", n=8)
                pe.wait_ge(sem("q_evac"), 8 * s + 8)
                for i in range(TT_):
                    for half in range(2):
                        f = s * 4 + i * 2 + half
                        if f >= 4:
                            pe.wait_ge(sem("key_sc_evac"), f - 3)
                        for j in range(4):
                            n = half * 4 + j
                            m = mm(bank(4 + f % 4, j * P, P), qT[:, s * 8 + n, i * P:(i + 1) * P], w[:, n, :],
                                   start=(j == 0))
                        m.then_inc(sem("tiles_used" if f % 4 == 3 else "key_sc_done"), 1)

            groups = HALF // GROUP

            def activations(first, group, s):
                pe.wait_ge(sem("u_evac"), group * GROUP + (first + s + 1))
                by_h(s % 4, M_U + first + s, group * GROUP)

            def gates(turn, group, s, b0):
                n = turn * HALF + s
                pe.wait_ge(sem("oh_ready"), group * GROUP + (n + 1))
                pe.wait_ge(sem("weighed"), group * GROUP + (n + 1))
                for j in range(4):
                    m = mm(bank(b0 + s % 2, j * 2 * HALF, 2 * HALF), ohA[turn][:, j, :], ohB[turn][:, j, :, :],
                           start=(j == 0))
                m.then_inc(sem("G_done"), 1)

            def outputs(turn, group, s, first=False):
                ms = M_U + NKEYS + turn * HALF + s
                pe.wait_ge(sem("a_lo_ready"), group * GROUP + (turn * HALF + s + 1))
                for half in range(2):
                    pe.wait_ge(sem("lo_ready"), group * (2 * GROUP) + (2 * ms + half + 1))
                    for c in range(4 * half, 4 * half + 4):
                        for a, b in ((0, 0), (1, 0), (0, 1)):
                            m = mm(bank(4 + c // 2, (c % 2) * T, T), wsplit[:, ms % 2, a, c * P:(c + 1) * P],
                                   asplit[:, s % 2, b, :],
                                   start=(first and s == 0 and c % 2 == 0 and a == 0 and b == 0), stop=False)
                    m.then_inc(sem("tiles_used" if half else "half_used"), 1)

            with pe.Fori(0, groups - 1, 1) as group:
                for s in range(GROUP):
                    activations(0, group, s)

            pe.wait_ge(sem("choice_ready"), 1)
            for s in range(3):
                for i in range(TT_):
                    src = gate_f[:, i, :] if s == 2 else e_f[:, s, i, :]
                    m = pe.transpose(bank(4 + s, i * P, P), src, ident)
            m.then_inc(sem("egT_done"), 1)
            for s in range(GROUP):
                activations(0, groups - 1, s)
            pe.wait_ge(sem("egT_read"), 1)
            with pe.Fori(0, groups, 1) as group:
                for s in range(GROUP):
                    gates(0, group, s, 4)
                    activations(HALF, group, s)

            pe.wait_ge(sem("u_evac"), NKEYS + 4)
            pe.wait_ge(sem("weighed"), HALF + 2)
            for s in range(GROUP):
                gates(1, 0, s, 0)
                outputs(0, 0, s, first=True)
            with pe.Fori(1, groups, 1) as group:
                for s in range(GROUP):
                    gates(1, group, s, 0)
                    outputs(0, group, s)
            with pe.Fori(0, groups, 1) as group:
                for s in range(GROUP):
                    outputs(1, group, s)

            for i in range(TT_):
                for half in range(2):
                    pe.wait_ge(sem(f"peerT{half}_ready"), 2)
                    for j in range(4):
                        k = half * 4 + j
                        m = pe.transpose(bank(2 * i + half, j * P, P), peerT[:, k, i * P:(i + 1) * P], ident)
                    m.then_inc(sem("peer_done"), 1)

        @block.scalar
        def _(act):
            def tile_done(n):
                act.wait_ge(sem("tiles_used"), n + 1)

            def split(ms, past=0):
                n = SPLIT[ms]
                for half in range(2):
                    cols = halves(n, half)
                    act.wait_ge(sem(f"slot{n % NSLOT}_in"), past * (16 // NSLOT) + 16 * (n // NSLOT + 1))
                    if ms >= 2:
                        if half == 0:
                            act.wait_ge(sem("half_used"), past + (ms - 1))
                        else:
                            act.wait_ge(sem("tiles_used"), past + (SPLIT[ms - 2] + 1))
                    act.activation(wsplit[:, ms % 2, 0, cols], slot(n)[:, cols], ACT.Copy)\
                       .then_inc(sem("hi_ready"), 1)

            def norm(turn):
                if turn == 0:
                    act.wait_ge(sem("x0_in"), 16)
                else:
                    act.wait_ge(sem("x0_sum"), turn)
                act.activation(sq[:, 0, :], xr[:, 0, :], ACT.Square, accum_out=rms[:, 0:1]).then_inc(sem("x0_sq"), 1)
                act.wait_ge(sem("rms_mean"), turn + 1)
                act.activation(rms[:, 4:6], rms[:, 2:4], ACT.Sqrt).then_inc(sem("rms_root"), 1)
                if turn < 2:
                    act.wait_ge(sem("rms_ready"), turn + 1)
                    act.activation(junk[:, 0, :], xr[:, 0, :], ACT.Copy, scale=rms[:, 6:7]).then_inc(sem("xn0_ready"), 1)

            def split_h(turn):
                for f in range(4):
                    half, i = f // 2, f % 2
                    act.wait_ge(sem("hT_ready"), 4 * turn + f + 1)
                    part = slice(4 * half, 4 * half + 4), slice(i * P, (i + 1) * P)
                    act.activation(hsplit[:, 0, part[0], part[1]], hT[:, part[0], part[1]], ACT.Copy)\
                       .then_inc(sem("hT_hi"), 1)

            norm(0)
            split(0)
            split(1)
            split_h(0)
            act.wait_ge(sem("pad_zero"), 1)
            for n in range(N_GDN + 2):
                if n < N_GDN:
                    tile_done(T_GDN + n)
                    act.activation(pad[:, n, 3:259], bank(n % 4, 0, T), ACT.Copy).then_inc(sem("proj_evac"), 1)
                    split(n + 2)
                if n >= 2:
                    act.wait_ge(sem("conv_done"), n - 1)
                    act.activation(conv[:, n - 2, :], conv[:, n - 2, :], ACT.Silu).then_inc(sem("silu_done"), 1)
            for k in range(N_TOK):
                split(M_TOK + k + 2)
            tile_done(T_TOK + N_TOK - 1)
            for i in range(TT_):
                act.activation(zs[:, i, :], bank(4 + 2 * i), ACT.Silu).then_inc(sem("z_evac"), 1)
            for n in range(N_NSA):
                tile_done(T_NSA + n)
                act.activation(nsaf[:, n, :], bank((N_GDN + n) % 4, 0, T), ACT.Copy).then_inc(sem("proj_evac"), 1)
                split(M_NSA + n + 2)
                if n == 1:
                    act.wait_ge(sem("ge_in"), 1)
                    act.activation(ge, ge, ACT.Exp).then_inc(sem("ge_out"), 1)
                    act.activation(ea, par_cols(R_ALOG, 8), ACT.Exp).then_inc(sem("ge_out"), 1)
            for f in range(6):
                act.wait_ge(sem("tt_done"), f + 1)
                act.activation(qkvt[:, f % 2, 512 * (f // 2):][:, 0:512], bank(4 + f % 4), ACT.Copy)\
                   .then_inc(sem("tt_evac"), 1)
            split(M_MERGE + 2)
            act.wait_ge(sem("ssq_ready"), 1)
            act.activation(rq, ssq, ACT.Sqrt).then_inc(sem("rq_root"), 1)
            act.wait_ge(sem("tok_evac"), TT_)
            act.activation(sg, tk[:, :, 0:32], ACT.Sigmoid).then_inc(sem("sg_ready"), 1)
            for n in range(N_MERGE):
                if 1 <= n < N_MERGE - 2:
                    split(M_MERGE + n + 2)
                tile_done(T_MERGE + n)
                act.activation(mg[:, n, :], bank((N_GDN + N_NSA + n) % 4, 0, T), ACT.Sigmoid)\
                   .then_inc(sem("proj_evac"), 1)
                if n == 5:
                    act.wait_ge(sem("gcl_evac"), 1)
                    act.activation(eg, gcl[:, :, 0:8], ACT.Exp).then_inc(sem("eg_ready"), 1)
                    act.wait_ge(sem("ekd_in"), 1)
                    act.activation(ekd, ekd, ACT.Exp).then_inc(sem("ekd_ready"), 1)
                    for i in range(TT_):
                        act.wait_ge(sem("DT_in"), i + 1)
                        for p in range(2):
                            rows = slice(DH * p, DH * p + DH)
                            for half in range(2):
                                b = 4 + (1 + 2 * i + half) % 4
                                src = ps[rows, b, :].rearrange("p (q z c t) -> p q z c t", q=2, z=2, c=2)
                                m = act.activation(egl[rows, i, 2 * half:2 * half + 2, :], src[:, :, p, :, CH - 1],
                                                   ACT.Exp)
                        m.then_inc(sem("gbc_read"), 1)
                        act.activation(DT[:, i], DT[:, i], ACT.Exp).then_inc(sem("DT_exp"), 1)
                if n in (9, 11):
                    for f in range(2 * (n - 9), 2 * (n - 9) + 4):
                        act.wait_ge(sem("fT_done"), f + 1)
                        act.activation(XT[:, f // 2, f % 2], bank(4 + f % 4), ACT.Copy).then_inc(sem("fT_evac"), 1)
            for b in range(4):
                act.wait_ge(sem("BT_done"), b + 1)
                act.activation(BT[:, 2 * b:2 * b + 2, :], bank(4 + b), ACT.Copy).then_inc(sem("BT_in"), 1)
            for i in range(TT_):
                act.wait_ge(sem("pc_in"), i + 1)
                act.activation(pc[:, i], pc[:, i], ACT.Exp).then_inc(sem("pc_exp"), 1)
            for i in range(TT_):
                act.wait_ge(sem("pcT_done"), i + 1)
                act.activation(pcT[:, i, :], bank(4 + i, 0, P), ACT.Copy).then_inc(sem("pcT_evac"), 1)
            for n in range(TT_ * H + 1):
                if n < TT_ * H:
                    i, h = n // H, n % H
                    nk = P * (i + 1)
                    act.wait_ge(sem("s_ready"), n + 1)
                    for b in range(2):
                        m = act.activation(Sb[:, n % 3, b * nk:(b + 1) * nk], Sb[:, n % 3, b * nk:(b + 1) * nk], ACT.Exp,
                                           bias=mx[:, n, b:b + 1], accum_out=sums[:, i, h, 1 + b:2 + b])
                    m.then_inc(sem("p_ready"), 1)
                if n >= 1:
                    w = 2 * P * ((n - 1) // H + 1)
                    act.wait_ge(sem("pT_done"), n)
                    if n >= 3:
                        act.wait_ge(sem("pv_done"), n - 2)
                    act.activation(PT[:, (n - 1) % 2, 0:w], bank(2 + (n - 1) % 2, 0, w), ACT.Copy)\
                       .then_inc(sem("pT_evac"), 1)
            for lv in range(N_LEV):
                for g in range(4):
                    n = (lv - 1) * 4 + g
                    if lv > 0:
                        act.wait_ge(sem("Y_done"), n + 1)
                        act.activation(Yb[:, g], bank(g), ACT.Copy).then_inc(sem("Y_evac"), 1)
                if lv == 1:
                    for i in range(TT_):
                        act.wait_ge(sem("obT_done"), i + 1)
                        act.activation(hsplit[:, 0, 0:HP, i * P:(i + 1) * P],
                                       bank(4 + i).rearrange("p (k t) -> p k t", k=HP), ACT.Copy)\
                           .then_inc(sem("obT_hi"), 1)
                if lv < N_LEV - 1:
                    for g in range(4):
                        act.wait_ge(sem("T_done"), lv * 4 + g + 1)
                        act.activation(Tm[:, g], bank(g), ACT.Copy).then_inc(sem("T_ready"), 1)
            split(M_AB)
            split(M_AB + 1)
            for i in range(TT_):
                act.wait_ge(sem("nwT_done"), i + 1)
                act.activation(nwT[:, i], bank(i), ACT.Copy).then_inc(sem("nwT_evac"), 1)
            for i in range(TT_):
                act.wait_ge(sem("o_done"), i + 1)
                act.activation(oa[:, i, :], bank(3), ACT.Copy).then_inc(sem("o_evac"), 1)
                if i == 0:
                    split(M_AB + 2)
            act.wait_ge(sem("oss_ready"), 1)
            act.activation(osr, oss, ACT.Sqrt).then_inc(sem("osr_root"), 1)
            split(M_AB + 3)
            split(M_AB + 4)
            for i in range(TT_):
                act.wait_ge(sem("oaT_done"), i + 1)
                act.activation(hsplit[:, 0, HP:KT, i * P:(i + 1) * P], bank(1 + i).rearrange("p (k t) -> p k t", k=HP),
                               ACT.Copy).then_inc(sem("oaT_hi"), 1)
            split(M_AB + 5)

            def mix_hi(k):
                act.wait_ge(sem("mix_ready"), k + 1)
                if k == HP:
                    tile_done(T_AB + N_AB - 1)
                act.activation(hsplit[:, 0, k, :], mixT[:, k, :], ACT.Copy).then_inc(sem("mix_hi"), 1)

            split(M_AB + 6)
            split(M_AB + 7)
            for k in range(2):
                mix_hi(2 * k)
                mix_hi(2 * k + 1)
                split(M_AB + N_AB + k)
            for k in range(HP, KT):
                mix_hi(k)
            for k in range(2, N_OUT + 2):
                split(M_AB + N_AB + k)
            norm(1)
            split_h(1)
            for n in range(N_WQ):
                tile_done(T_WQ + n)
                act.activation(qT[:, n, :], bank(n % 4, 0, T), ACT.Copy).then_inc(sem("q_evac"), 1)
                split(M_WQ + n + 2)
            for f in range(8):
                s, i, half = f // 4, (f // 2) % 2, f % 2
                if f % 4 == 3:
                    tile_done(T_SK + s)
                else:
                    act.wait_ge(sem("key_sc_done"), 3 * s + f % 4 + 1)
                act.activation(sc[:, i, 8 * s + 4 * half:8 * s + 4 * half + 4, :], bank(4 + f % 4), ACT.Copy)\
                   .then_inc(sem("key_sc_evac"), 1)
            act.wait_ge(sem("q_evac"), N_WQ)
            act.sem_inc(sem("u_evac"), 4)
            act.preload_act_table(ACT.Gelu_apprx_tanh)

            groups = HALF // GROUP

            def gelu(group, s, first=0):
                act.wait_ge(sem("tiles_used"), group * GROUP + (T_U + first + s + 1))
                act.activation(act_w[:, group * GROUP + (first + s), :], bank(s % 4, 0, T), ACT.Gelu_apprx_tanh)\
                   .then_inc(sem("u_evac"), 1)
                split(M_U + first + s + 2, group * GROUP)

            with act.Fori(0, groups - 2, 1) as group:
                for s in range(GROUP):
                    gelu(group, s)
            act.wait_ge(sem("gate_in"), TT_)
            for i in range(TT_):
                act.activation(gate[:, i], gate[:, i], ACT.Exp).then_inc(sem("gate_exp"), 1)
            for s in range(GROUP):
                gelu(groups - 2, s)
            act.wait_ge(sem("egT_done"), 1)
            act.activation(egT[:, :, :], ps[:, 4:7, 0:T], ACT.Copy)
            act.activation(g2[:, :, 0].bitcast(F32R), bank(6, 0, T), ACT.Copy).then_inc(sem("egT_read"), 1)
            for s in range(GROUP):
                gelu(groups - 1, s)
            act.preload_act_table(ACT.Gelu_apprx_tanh)

            def lo_out(turn, group, s, b0):
                act.wait_ge(sem("G_done"), group * GROUP + (turn * HALF + s + 1))
                act.activation(G_lo[:, s % 2], bank(b0 + s % 2).rearrange("p (t x e) -> p x t e", t=4, x=2)[:, 1],
                               ACT.Copy).then_inc(sem("G_lo_read"), 1)

            with act.Fori(0, groups, 1) as group:
                for s in range(GROUP):
                    lo_out(0, group, s, 4)
                    gelu(group, s, HALF)

            def split_a(row, buf):
                act.activation(asplit[:, buf, 0, :], row, ACT.Copy).then_inc(sem("a_hi_ready"), 1)

            def out_step(group, s, ahead=True, gates=False):
                act.wait_ge(sem("tiles_used"), group * GROUP + (T_V + s))
                split_a(act_w[:, group * GROUP + (s + 1), :], (s + 1) % 2)
                if gates:
                    lo_out(1, group, s, 0)
                if ahead:
                    split(M_U + NKEYS + s + 2, group * GROUP)

            act.wait_ge(sem("weighed"), HALF + 2)
            split_a(act_w[:, 0, :], 0)
            with act.Fori(0, groups - 1, 1) as group:
                for s in range(GROUP):
                    out_step(group, s, gates=True)
            for s in range(GROUP - 1):
                out_step(groups - 1, s, gates=True)
            lo_out(1, groups - 1, GROUP - 1, 0)
            act.wait_ge(sem("weighed"), 2 * HALF + 2)
            out_step(groups - 1, GROUP - 1)
            with act.Fori(groups, 2 * groups - 1, 1) as group:
                for s in range(GROUP):
                    out_step(group, s)
            for s in range(GROUP - 1):
                out_step(2 * groups - 1, s, ahead=s < GROUP - 2)
            act.wait_ge(sem("tiles_used"), N_TILES)
            for b in range(2):
                act.activation(peerT[:, 2 * b:2 * b + 2, :], bank(4 + b), ACT.Copy).then_inc(sem("peerT0_ready"), 1)
            norm(2)

        @block.vector
        def _(dve):
            chain = [0]

            def link(m):
                chain[0] += 1
                m.then_inc(sem("dve_chain"), 1)
                dve.wait_ge(sem("dve_chain"), chain[0])

            tt, ts, stt = dve.tensor_tensor, dve.tensor_scalar, dve.scalar_tensor_tensor

            def tile_done(n):
                dve.wait_ge(sem("tiles_used"), n + 1)

            def norm(turn):
                link(dve.tensor_tensor_reduce(sq[:, 1, :], xr[:, 1, :], xr[:, 1, :], 1.0, 0.0, ALU.mult,
                                              ALU.add, rms[:, 1:2]))
                dve.wait_ge(sem("x0_sq"), turn + 1)
                ts(rms[:, 2:4], rms[:, 0:2], 1.0 / D, EPS, ALU.mult, ALU.add).then_inc(sem("rms_mean"), 1)
                dve.wait_ge(sem("rms_root"), turn + 1)
                dve.reciprocal(rms[:, 6:8], rms[:, 4:6]).then_inc(sem("rms_ready"), 1)
                dve.wait_ge(sem("rms_ready"), turn + 1)
                if turn < 2:
                    ts(junk[:, 1, :], xr[:, 1, :], rms[:, 7:8], None, ALU.mult).then_inc(sem("xn1_ready"), 1)

            def take_h(turn, b0, gain):
                for half in range(2):
                    for i in range(TT_):
                        f = 2 * half + i
                        dve.wait_ge(sem("hT_done"), 4 * turn + f + 1)
                        tt(hT[:, 4 * half:4 * half + 4, i * P:(i + 1) * P],
                           bank(b0 + f).rearrange("p (k t) -> p k t", k=4), each(par_cols(gain + 4 * half, 4), P),
                           ALU.mult).then_inc(sem("hT_ready"), 1)
                    for i in range(TT_):
                        f = 2 * half + i
                        dve.wait_ge(sem("hT_hi"), 4 * turn + f + 1)
                        part = slice(4 * half, 4 * half + 4), slice(i * P, (i + 1) * P)
                        tt(hsplit[:, 1, part[0], part[1]], hT[:, part[0], part[1]],
                           hsplit[:, 0, part[0], part[1]].bitcast(F32), ALU.subtract).then_inc(sem("hT_split"), 1)

            dve.wait_ge(sem("x1_in"), 16)
            norm(0)
            dve.wait_ge(sem("params_in"), 16)
            take_h(0, 4, R_NM)
            for n in range(N_GDN):
                dve.wait_ge(sem("proj_evac"), n + 1)
                c0 = R_CW + 4 * n
                link(ts(conv[:, n, :], pad[:, n, 0:T], par[:, c0:c0 + 1], None, ALU.mult))
                for j in range(1, 4):
                    m = stt(out=conv[:, n, :], in0=pad[:, n, j:j + T], scalar=par[:, c0 + j:c0 + j + 1],
                            in1=conv[:, n, :], op0=ALU.mult, op1=ALU.add)
                    if j < 3:
                        link(m)
                m.then_inc(sem("conv_done"), 1)

            tile_done(T_TOK + N_TOK - 1)
            for i in range(TT_):
                dve.tensor_copy(tk[:, i, :], bank(5 + 2 * i, 0, 296)).then_inc(sem("tok_evac"), 1)
            dve.wait_ge(sem("tok_evac"), TT_)
            link(tt(gs, tk[:, :, 32:40], over(par_cols(R_DT, 8), TT_), ALU.add))
            link(ts(gm, gs, 0.0, None, ALU.max))
            stt(out=ge, in0=gs, scalar=-1.0, in1=gs, op0=ALU.mult, op1=ALU.min).then_inc(sem("ge_in"), 1)

            dve.wait_ge(sem("ge_out"), 2)
            link(ts(gz, ge, 2.0, None, ALU.add))
            link(dve.reciprocal(gr, gz))
            link(tt(gz, ge, gr, ALU.mult))
            link(tt(gt, gz, gz, ALU.mult))
            link(ts(gp, gt, 1.0 / 17, None, ALU.mult))
            for k in range(15, 1, -2):
                link(stt(out=gp, in0=gp, scalar=1.0 / k, in1=gt, op0=ALU.add, op1=ALU.mult))
            link(stt(out=gp, in0=gp, scalar=1.0, in1=gz, op0=ALU.add, op1=ALU.mult))
            link(stt(out=gp, in0=gp, scalar=2.0, in1=gm, op0=ALU.mult, op1=ALU.add))
            stt(out=gg, in0=gp, scalar=-1.0, in1=over(ea, TT_), op0=ALU.mult, op1=ALU.mult).then_inc(sem("g_ready"), 1)
            dve.wait_ge(sem("g_ready"), 1)
            dve.wait_ge(sem("consts_in"), 16)
            for i in range(TT_):
                tt(grhs[:, i], over(tri, H), each(gg[:, i, :], P), ALU.mult).then_inc(sem("grhs_ready"), 1)

            dve.wait_ge(sem("nsa_zero"), 2)
            for s in range(2):
                dve.wait_ge(sem("proj_evac"), N_GDN + (8 if s else 5))
                for g in range(2):
                    rows = slice(DH * g, DH * g + DH)
                    src = nsaf[rows, 7 if s else 4, :].rearrange("p (m b) -> p b m", b=16)
                    for a in range(2):
                        pe_cols = par[rows, R_PE + 32 * s + 16 * a:R_PE + 32 * s + 16 * a + 16]
                        tt(kcbd[rows, s, 16 * a:16 * a + 16, g, 0:NCMP], src[:, :, a:a + NCMP],
                           each(pe_cols, NCMP), ALU.add).then_inc(sem("kcbd_ready"), 1)

            dve.wait_ge(sem("tt_evac"), 4)
            for i in range(TT_):
                link(tt(sq[:, i, :], qkvt[:, i, 0:1024], qkvt[:, i, 0:1024], ALU.mult))
                link(dve.tensor_reduce(ssq[:, i, :], sq[:, i, :].rearrange("p (h d) -> p h d", d=DH), AX.X, ALU.add))
            ts(ssq, ssq, EPS, None, ALU.add).then_inc(sem("ssq_ready"), 1)

            dve.wait_ge(sem("bias_row_done"), 1)
            dve.tensor_copy(rrs[0:H, :], bank(7, 0, N_E1)[0:H]).then_inc(sem("bias_read"), 1)
            dve.wait_ge(sem("gcl_done"), 1)
            dve.tensor_copy(gcl, bank(4, 0, 32).rearrange("p (i c) -> p i c", i=TT_)).then_inc(sem("gcl_evac"), 1)
            dve.wait_ge(sem("gcl_evac"), 1)
            tt(ekd, gcl[:, :, 8:16], gcl[:, :, 0:8], ALU.subtract).then_inc(sem("ekd_in"), 1)
            link(ts(ngc, gcl[:, :, 0:8], -1.0, None, ALU.mult))
            dve.wait_ge(sem("rq_root"), 1)
            link(dve.reciprocal(rq, rq))
            link(ts(rq[:, :, 0:8], rq[:, :, 0:8], DH ** -0.5, None, ALU.mult))
            dve.wait_ge(sem("tt_done"), 6)
            dve.wait_ge(sem("sg_ready"), 1)

            def heads(i, part):
                return qkvt[:, i, 512 * part:512 * part + 512].rearrange("p (h d) -> p h d", h=H)

            for i in range(TT_):
                tt(kn[:, i], heads(i, 1), each(rq[:, i, 8:16], DH), ALU.mult).then_inc(sem("gdn_rows_ready"), 1)
            dve.wait_ge(sem("gdn_rows_ready"), 2)
            dve.wait_ge(sem("bias_row_out"), 16)
            for i in range(TT_):
                dve.wait_ge(sem("gbc_done"), i + 1)
                for h in range(H):
                    m = stt(out=DT[:, i, h, :], in0=bank(4 + (1 + 2 * i + h // 4) % 4, (h % 4) * P, P),
                            scalar=ngc[:, i, h:h + 1], in1=tri, op0=ALU.add, op1=ALU.mult)
                m.then_inc(sem("DT_in"), 1)
            for i in range(TT_):
                tt(kb[:, i], kn[:, i], each(sg[:, i, 0:8], DH), ALU.mult).then_inc(sem("gdn_rows_ready"), 1)
            for i in range(TT_):
                tt(qn[:, i], heads(i, 0), each(rq[:, i, 0:8], DH), ALU.mult).then_inc(sem("gdn_rows_ready"), 1)
            dve.wait_ge(sem("tt_evac"), 6)
            for i in range(TT_):
                link(tt(vb[:, i], heads(i, 2), each(sg[:, i, 0:8], DH), ALU.mult))
            for i in range(TT_):
                z = zs[:, i, :].rearrange("p (h d) -> p h d", h=H)
                dve.wait_ge(sem("z_evac"), i + 1)
                link(tt(z, z, over(par_cols(R_GN, DH), H), ALU.mult))

            dve.wait_ge(sem("eg_ready"), 1)
            dve.wait_ge(sem("gdn_rows_ready"), 6)
            for i in range(TT_):
                tt(qd[:, i], qn[:, i], each(eg[:, i, :], DH), ALU.mult).then_inc(sem("gdn_rows_ready"), 1)
            link(ts(neg_eg, eg, -1.0, None, ALU.mult))
            dve.wait_ge(sem("ekd_ready"), 1)
            for i in range(TT_):
                tt(kbg[:, i], kb[:, i], each(neg_eg[:, i, :], DH), ALU.mult)
                link(tt(kd[:, i], kn[:, i], each(ekd[:, i, :], DH), ALU.mult))
            for i in range(TT_):
                dve.wait_ge(sem("DT_exp"), i + 1)
                link(tt(DT[:, i], DT[:, i], over(tri, H), ALU.mult))
            for r in range(8):
                which, i, p = r // 4, (r // 2) % 2, r % 2
                dve.wait_ge(sem("am_done"), r + 1)
                dst = attnT if which else AT
                tt(dst[:, i, p:H:2, :], bank(4 + r % 4).rearrange("p (q t) -> p q t", q=HP), DT[:, i, p:H:2, :],
                   ALU.mult).then_inc(sem("am_evac"), 1)

            tile_done(T_CMP + 1)
            tt(kc2[0:32, :].rearrange("p (g d) -> p g d", g=2), over(bank(0, 0, DH)[0:32], 2),
               each(head_of[0:32, 0:2], DH), ALU.mult).then_inc(sem("kc_ready"), 1)
            dve.wait_ge(sem("kcT_done"), 1)
            dve.tensor_copy(kcmpT, bank(2, 0, 32)).then_inc(sem("kcmpT_ready"), 1)
            tile_done(T_CMP + 3)
            dve.tensor_copy(vcs[0:32, :], bank(1, 0, DH)[0:32]).then_inc(sem("vc_ready"), 1)
            seen = [(P - 32) // 16 + 1, NCMP]
            link(dve.memset(pc[:, 0, :, seen[0]:NCMP], NEG))
            dve.wait_ge(sem("BT_in"), 4)
            for i in range(TT_):
                for g in range(2):
                    dve.wait_ge(sem("sc_done"), 2 * i + g + 1)
                    j0 = (TT_ - 1 - i) * P + 31
                    link(stt(out=pc[:, i, 4 * g:4 * g + 4, 0:seen[i]],
                             in0=bank(4 + 2 * i + g, 0, 64).rearrange("p (q n) -> p q n", q=4)[:, :, 0:seen[i]],
                             scalar=DH ** -0.5, in1=BT[:, 4 * g:4 * g + 4, j0:j0 + 16 * seen[i] - 15:16],
                             op0=ALU.mult, op1=ALU.add))
                link(dve.tensor_reduce(cmx[:, i, :], pc[:, i, :, 0:NCMP], AX.X, ALU.max))
                tt(pc[:, i, :, 0:NCMP], pc[:, i, :, 0:NCMP], each(cmx[:, i, :], NCMP), ALU.subtract)\
                    .then_inc(sem("pc_in"), 1)
            for i in range(TT_):
                dve.wait_ge(sem("pc_exp"), i + 1)
                link(dve.tensor_reduce(sums[:, i, :, 0], pc[:, i, :, 0:NCMP], AX.X, ALU.add))
                tt(pc[:, i], pc[:, i], over(cmask[:, i, :], H), ALU.mult).then_inc(sem("pc_ready"), 1)

            def branch_gates(i, b0, b1):
                gates = sg[:, i, 8:32].rearrange("p (h b) -> p h b", h=H)
                link(dve.reciprocal(coef[:, i, :, b0:b1], sums[:, i, :, b0:b1]))
                link(tt(coef[:, i, :, b0:b1], coef[:, i, :, b0:b1], gates[:, :, b0:b1], ALU.mult))

            dve.wait_ge(sem("vc_copied"), 1)
            tt(vcbd.rearrange("p (h d) -> p h d", h=H), over(bank(3, 0, DH), H), each(head_of, DH), ALU.mult)\
                .then_inc(sem("vcbd_ready"), 1)

            def add_branches(i, tmp):
                dve.wait_ge(sem("pv_done"), H * (i + 1))
                branch_gates(i, 1, 3)
                for b in range(2):
                    link(tt(tmp[:, b, :].rearrange("p (h d) -> p h d", h=H),
                            bank(4 + 2 * i + b).rearrange("p (h d) -> p h d", h=H),
                            each(coef[:, i, :, 1 + b], DH), ALU.mult))
                link(tt(onsa[:, i, :], onsa[:, i, :], tmp[:, 0, :], ALU.add))
                tt(onsa[:, i, :], onsa[:, i, :], tmp[:, 1, :], ALU.add).then_inc(sem("onsa_ready"), 1)

            for n in range(TT_ * H):
                i, h = n // H, n % H
                nk = P * (i + 1)
                dve.wait_ge(sem("s_done"), n + 1)
                if n >= 3:
                    dve.wait_ge(sem("pT_done"), n - 2)
                s = Sb[:, n % 3, 0:2 * nk].rearrange("p (b j) -> p b j", b=2)
                stt(out=s, in0=bank(n % 2, 0, 2 * nk).rearrange("p (b j) -> p b j", b=2), scalar=DH ** -0.5,
                    in1=over(BT[:, h, T - nk:T], 2), op0=ALU.mult, op1=ALU.add).then_inc(sem("s_evac"), 1)
                dve.wait_ge(sem("s_evac"), n + 1)
                dve.tensor_reduce(mx[:, n, :], s, AX.X, ALU.max, negate=True).then_inc(sem("s_ready"), 1)
                if n == H + 3:
                    add_branches(0, at(0, 1024).rearrange("p (b j) -> p b j", b=2))
                if n == 1:
                    for i in range(TT_):
                        branch_gates(i, 0, 1)
                        dve.wait_ge(sem("oc_done"), i + 1)
                        tt(onsa[:, i, :].rearrange("p (h d) -> p h d", h=H), bank(6 + i).rearrange("p (h d) -> p h d", h=H),
                           each(coef[:, i, :, 0], DH), ALU.mult).then_inc(sem("oc_evac"), 1)
            dve.wait_ge(sem("pT_done"), TT_ * H)
            add_branches(1, Sb)

            for i in range(TT_):
                dve.wait_ge(sem("obT_hi"), i + 1)
                part = slice(0, HP), slice(i * P, (i + 1) * P)
                tt(hsplit[:, 1, part[0], part[1]], bank(4 + i).rearrange("p (k t) -> p k t", k=HP),
                   hsplit[:, 0, part[0], part[1]].bitcast(F32), ALU.subtract).then_inc(sem("obT_split"), 1)

            def branch_done(n):
                ms, half = M_AB + n // 2, n % 2
                dve.wait_ge(*((sem("tiles_used"), SPLIT[ms] + 1) if half else (sem("half_used"), ms + 1)))

            def weigh_b(j):
                branch_done(j)
                tt(mg[:, N_AB + j, :], mg[:, N_AB + j, :], bank((5, 6, 7, 0)[j % 4], 0, T), ALU.mult)\
                    .then_inc(sem("branch_evac"), 1)

            for n in range(4 * (N_LEV - 1)):
                g = n % 4
                dve.wait_ge(sem("YTT_done"), n + 1)
                tt(TT[:, g], TT[:, g], bank(4 + g).rearrange("p (q j) -> p q j", q=HP), ALU.subtract)\
                    .then_inc(sem("TT_ready"), 1)

            osq = at(0, 1024).rearrange("p (i c) -> p i c", i=TT_)

            def square_sums(i):
                dve.wait_ge(sem("o_evac"), i + 1)
                link(tt(osq[:, i], oa[:, i, :], oa[:, i, :], ALU.mult))
                link(dve.tensor_reduce(oss[:, i, :], osq[:, i].rearrange("p (h d) -> p h d", h=H), AX.X, ALU.add))

            dve.wait_ge(sem("scan_zero"), 1)
            for c in range(T // CH):
                rows = slice(CH * (c % 2), CH * (c % 2) + CH)
                dve.wait_ge(sem("vn_done"), c + 1)
                dve.tensor_copy(vn[rows, :], ps[rows, 2 - c // 2, :]).then_inc(sem("vn_evac"), 1)
                if c >= 1:
                    weigh_b(c - 1)
                if c == T // CH - 1:
                    continue
                dve.wait_ge(sem("S_read"), c + 1)
                for add in range(2):
                    if add:
                        dve.wait_ge(sem("dS_done"), c + 1)
                    for p in range(2):
                        hr = slice(DH * p, DH * p + DH)
                        Sp = S[hr, :, DH * p:DH * p + DH]
                        if add:
                            dS = ps[hr, 4, :].rearrange("p (q e) -> p q e", q=HP)[:, :, DH * p:DH * p + DH]
                            m = tt(Sp, Sp, dS, ALU.add)
                        else:
                            m = tt(Sp, Sp, each(egl[hr, c // 2, :, c % 2], DH), ALU.mult)
                    if not add:
                        link(m)
                m.then_inc(sem("S_ready"), 1)
                if c == 2:
                    square_sums(0)

            square_sums(1)
            ts(oss, oss, 1.0 / DH, EPS, ALU.mult, ALU.add).then_inc(sem("oss_ready"), 1)
            weigh_b(3)
            dve.wait_ge(sem("osr_root"), 1)
            link(dve.reciprocal(osr, osr))
            for i in range(TT_):
                o3 = oa[:, i, :].rearrange("p (h d) -> p h d", h=H)
                link(tt(o3, o3, each(osr[:, i, :], DH), ALU.mult))
                tt(oa[:, i, :], oa[:, i, :], zs[:, i, :], ALU.mult).then_inc(sem("oa_ready"), 1)

            for j in range(4, N_AB - 1):
                weigh_b(j)
            for i in range(TT_):
                dve.wait_ge(sem("oaT_hi"), i + 1)
                part = slice(HP, KT), slice(i * P, (i + 1) * P)
                tt(hsplit[:, 1, part[0], part[1]], bank(1 + i).rearrange("p (k t) -> p k t", k=HP),
                   hsplit[:, 0, part[0], part[1]].bitcast(F32), ALU.subtract).then_inc(sem("oaT_split"), 1)
            weigh_b(N_AB - 1)

            def mix_lo(k):
                dve.wait_ge(sem("mix_hi"), k + 1)
                tt(hsplit[:, 1, k, :], mixT[:, k, :], hsplit[:, 0, k, :].bitcast(F32), ALU.subtract)\
                    .then_inc(sem("mix_split"), 1)

            for j in range(N_AB):
                branch_done(N_AB + j)
                tt(mg[:, j, :], mg[:, j, :], bank((5, 6, 7, 0)[j % 4], 0, T), ALU.mult).then_inc(sem("branch_evac"), 1)
                dve.wait_ge(sem("branch_evac"), N_AB + j + 1)
                tt(mixT[:, j, :], mg[:, j, :], mg[:, N_AB + j, :], ALU.add).then_inc(sem("mix_ready"), 1)
                if 1 <= j <= HP:
                    mix_lo(j - 1)
            for k in range(HP, KT):
                mix_lo(k)
            tile_done(T_OUT + N_OUT - 1)
            for i in range(TT_):
                for half in range(2):
                    xh = xr[:, i, 512 * half:512 * half + 512]
                    m = tt(xh, xh, bank(1 + 2 * i + half), ALU.add)
                    if i:
                        link(m)
                if i == 0:
                    m.then_inc(sem("x0_sum"), 1)
            norm(1)
            take_h(1, 0, R_NF)

            def best16(val, idx, src, left):
                link(dve.max(val[:, 0:8], src))
                dve.max_index(idx[:, 0:8], val[:, 0:8], src)
                link(dve.match_replace(left, val[:, 0:8], src, -3e38))
                link(dve.max(val[:, 8:16], left))
                link(dve.max_index(idx[:, 8:16], val[:, 8:16], left))

            dve.wait_ge(sem("key_sc_evac"), 8)
            for i in range(TT_):
                for n in range(2 * H):
                    best16(tkv[:, i, n, :], tki_u[:, i, n, :], sc[:, i, n, :], rep)
            link(dve.tensor_copy(tki, tki_u))
            for i in range(TT_):
                for h in range(H):
                    link(tt(cand.rearrange("p (a b) -> p a b", a=TOPK), each(tkv[:, i, 2 * h, :], TOPK),
                            over(tkv[:, i, 2 * h + 1, :], TOPK), ALU.add))
                    best16(topv[:, i, h, :], topi_u[:, i, h, :], cand, cand2)
            topi_c = topi_u.rearrange("p i h k -> p i (h k)")
            link(ts(ab_u[:, 0], topi_c, 4, None, ALU.logical_shift_right))
            link(ts(ab_u[:, 1], topi_c, 15, None, ALU.bitwise_and))
            link(dve.tensor_copy(ab_f, ab_u))
            for s in range(2):
                for i in range(TT_):
                    link(tt(oh, each(ab_f[:, s, i, :], TOPK), over(iota[:, 0:TOPK], P), ALU.is_equal))
                    oh4 = oh.rearrange("p (h k) a -> p h k a", h=H)
                    keys = tki[:, i, s:2 * H:2, :].unsqueeze(2).broadcast_to([P, H, TOPK, TOPK])
                    link(tt(oh4, oh4, keys, ALU.mult))
                    link(dve.tensor_reduce(e_f[:, s, i, :], oh, AX.X, ALU.add))
            for i in range(TT_):
                tt(gate[:, i], topv[:, i], each(topv[:, i, :, 0], TOPK), ALU.subtract).then_inc(sem("gate_in"), 1)
            dve.wait_ge(sem("gate_exp"), TT_)
            gsum = gs
            link(dve.tensor_reduce(gsum, gate, AX.X, ALU.add))
            link(dve.reciprocal(gr, gsum))
            link(tt(gate[:, 0], gate[:, 0], each(gr[:, 0, :], TOPK), ALU.mult))
            tt(gate[:, 1], gate[:, 1], each(gr[:, 1, :], TOPK), ALU.mult).then_inc(sem("choice_ready"), 1)

            groups = HALF // GROUP

            def one_hots(turn, group, s, first=False):
                n = turn * HALF + s
                b = (6, 2)[turn]
                row = bank(b, 0, P)
                hot = bank(b + s % 2, P, 4 * HALF).rearrange("p (t j) -> p t j", t=4)
                cols = bass.ds(group * (4 * GROUP) + 4 * s, 4)
                tt(hot, over(row[:, turn * HALF:(turn + 1) * HALF], 4), each(egT[:, 1, cols], HALF), ALU.is_equal)\
                    .then_inc(sem("hot_ready"), 1)
                if not first:
                    dve.wait_ge(sem("G_done"), group * GROUP + n)
                tt(ohA[turn], over(row, 4), each(egT[:, 0, cols], P), ALU.is_equal)
                dve.wait_ge(sem("hot_ready"), group * GROUP + (n + 1))
                tt(ohB[turn], hot.unsqueeze(2).broadcast_to([P, 4, 2, HALF]),
                   g2[:, cols, :].unsqueeze(3).broadcast_to([P, 4, 2, HALF]), ALU.mult).then_inc(sem("oh_ready"), 1)

            def weigh(turn, group, s, b0, between=None):
                n = turn * HALF + s
                dve.wait_ge(sem("G_done"), group * GROUP + (n + 1))
                G = bank(b0 + s % 2).rearrange("p (t x e) -> p x t e", t=4, x=2)
                dve.wait_ge(sem("G_lo_read"), group * GROUP + (n + 1))
                tt(G[:, 0], G[:, 0], G_lo[:, s % 2], ALU.add).then_inc(sem("G_sum"), 1)
                if between:
                    rest(group, between)
                dve.wait_ge(sem("G_sum"), group * GROUP + (n + 1))
                aw = act_w[:, turn * HALF:(turn + 1) * HALF, bass.ds(group * (4 * GROUP) + 4 * s, 4)]
                tt(aw.rearrange("p e t -> p t e"), aw.rearrange("p e t -> p t e"), G[:, 0], ALU.mult)\
                    .then_inc(sem("weighed"), 1)

            def rest(group, s):
                dve.wait_ge(sem("a_hi_ready"), group * GROUP + (s + 1))
                tt(asplit[:, s % 2, 1, :], act_w[:, group * GROUP + s, :], asplit[:, s % 2, 0, :].bitcast(F32),
                   ALU.subtract).then_inc(sem("a_lo_ready"), 1)

            dve.wait_ge(sem("egT_read"), 1)
            link(tt(g2[:, :, 1], egT[:, 2, :], g2[:, :, 0], ALU.subtract))
            dve.sem_inc(sem("weighed"), 2)
            dve.tensor_copy(bank(6, 0, P), iota).then_inc(sem("iota_in"), 1)
            dve.wait_ge(sem("iota_in"), 1)
            one_hots(0, 0, 0, first=True)
            dve.wait_ge(sem("u_evac"), HALF + 4)
            with dve.Fori(0, groups - 1, 1) as group:
                for s in range(GROUP):
                    one_hots(0, group, s + 1)
                    weigh(0, group, s, 4)
            for s in range(GROUP):
                if s < GROUP - 1:
                    one_hots(0, groups - 1, s + 1)
                weigh(0, groups - 1, s, 4)
            dve.wait_ge(sem("u_evac"), NKEYS + 4)
            dve.tensor_copy(bank(2, 0, P), iota).then_inc(sem("iota_in"), 1)
            dve.wait_ge(sem("iota_in"), 2)
            one_hots(1, 0, 0, first=True)
            rest(0, 0)

            def second_step(group, s, ahead=True):
                if ahead:
                    one_hots(1, group, s + 1)
                weigh(1, group, s, 0, between=s + 1 if ahead else None)

            with dve.Fori(0, groups - 1, 1) as group:
                for s in range(GROUP):
                    second_step(group, s)
            for s in range(GROUP):
                second_step(groups - 1, s, ahead=s < GROUP - 1)
            rest(groups - 1, GROUP)
            with dve.Fori(groups, 2 * groups - 1, 1) as group:
                for s in range(GROUP):
                    rest(group, s + 1)
            for s in range(GROUP - 1):
                rest(2 * groups - 1, s + 1)

            tile_done(N_TILES - 1)
            for b in range(2, 4):
                dve.tensor_copy(peerT[:, 2 * b:2 * b + 2, :], bank(4 + b)).then_inc(sem("peerT1_ready"), 1)
            for i in range(TT_):
                for half in range(2):
                    dve.wait_ge(sem("peer_done"), 2 * i + half + 1)
                    xh = xr[:, i, 512 * half:512 * half + 512]
                    m = tt(xh, xh, bank(2 * i + half), ALU.add)
                    if i:
                        link(m)
                if i == 0:
                    m.then_inc(sem("x0_sum"), 1)
            norm(2)
            dve.wait_ge(sem("nfinal_in"), 16)
            for i in range(TT_):
                stt(out=xr[:, i, :], in0=xr[:, i, :], scalar=rms[:, 6 + i:7 + i], in1=nfin, op0=ALU.mult,
                    op1=ALU.mult).then_inc(sem("out_ready"), 1)

        @block.gpsimd
        def _(pool):
            def rest(ms, past=0):
                for half in range(2):
                    cols = halves(SPLIT[ms], half)
                    pool.wait_ge(sem("hi_ready"), past * 2 + (2 * ms + half + 1))
                    pool.tensor_tensor(wsplit[:, ms % 2, 1, cols], slot(SPLIT[ms])[:, cols],
                                       wsplit[:, ms % 2, 0, cols].bitcast(F32), ALU.subtract)\
                        .then_inc(sem("lo_ready"), 1)

            pool.memset(pad[:, :, 0:3], 0.0).then_inc(sem("pad_zero"), 1)
            pool.memset(pc, 0.0).then_inc(sem("nsa_zero"), 1)
            pool.memset(kcbd, 0.0).then_inc(sem("nsa_zero"), 1)
            rest(0)
            rest(1)
            for ms in range(2, M_AB):
                rest(ms)
            pool.wait_ge(sem("am_evac"), 4)
            pool.wait_ge(sem("tiles_used"), T_AB)
            for g in range(4):
                i, p = g // 2, g % 2
                pool.tensor_tensor(TT[:, g], AT[:, i, p:H:2, :], over(level[:, 0, :], HP), ALU.mult)\
                    .then_inc(sem("TT0_part"), 1)
                pool.wait_ge(sem("TT0_part"), g + 1)
                pool.tensor_tensor(TT[:, g], over(ident, HP), TT[:, g], ALU.subtract).then_inc(sem("TT0_ready"), 1)
            pool.wait_ge(sem("gbc_done"), TT_)
            for lv in range(1, N_LEV):
                for g in range(4):
                    i, p = g // 2, g % 2
                    if lv >= 2:
                        pool.wait_ge(sem("Y_done"), (lv - 2) * 4 + g + 1)
                    pool.tensor_tensor(AbT[:, g], AT[:, i, p:H:2, :], over(level[:, lv, :], HP), ALU.mult)\
                        .then_inc(sem("AbT_ready"), 1)
            pool.wait_ge(sem("Y_done"), 4 * (N_LEV - 1))
            pool.memset(S, 0.0).then_inc(sem("scan_zero"), 1)
            for ms in range(M_AB, M_U + 2):
                rest(ms)
            with pool.Fori(0, 2 * NKEYS // GROUP - 1, 1) as group:
                for s in range(GROUP):
                    rest(M_U + s + 2, group * GROUP)
            for s in range(GROUP - 2):
                rest(M_U + 2 * NKEYS - GROUP + s + 2)
            pool.wait_ge(sem("weighed"), 2 * HALF + 2)
            pool.dma_start(nfin, nfinal.partition_broadcast(P)).then_inc(sem("nfinal_in"), 16)


def _constants():
    import math
    import numpy as np
    k = np.arange(P)[:, None]
    i = np.arange(P)[None, :]
    chunk = (k // CH) == (i // CH)
    c = np.zeros((P, N_CONST), np.float32)
    c[:, C_ID:C_ID + P] = np.eye(P)
    c[:, C_TRI:C_TRI + P] = chunk & (k <= i)
    c[:, C_SAME:C_SAME + P] = chunk
    c[:, C_ONES:C_ONES + P] = 1.0
    c[:, C_IOTA:C_IOTA + P] = i
    c[:, C_FLIP:C_FLIP + P] = (k + i) == P - 1
    for lv in range(N_LEV):
        b = 1 << lv
        c[:, C_LEV + lv * P:C_LEV + (lv + 1) * P] = (k // (2 * b) == i // (2 * b)) & ((i // b) % 2 == 1) & ((k // b) % 2 == 0)
    c[:, C_HEAD:C_HEAD + H] = (k // 16) == np.arange(H)[None, :]
    c[:, C_GROUP:C_GROUP + P] = (k // 16 == i // 64) & (k % 16 == i % 16)
    for t in range(TT_):
        for n in range(NCMP):
            c[:, C_CMASK + 16 * t + n] = (16 * n + 31) <= (np.arange(P) + P * t)

    def bucket(d):
        far = 16 + int(np.float32(np.log(np.float32(max(d, 1) / 16))) / np.float32(math.log(8.0)) * np.float32(16))
        return d if d < 16 else min(far, 31)

    e = np.zeros((33, N_E1), np.float32)
    for m in range(N_E1):
        d = T - 1 - m
        e[bucket(d) if d >= 0 else 32, m] = 1.0
    return c, e


def _layout(a):
    import numpy as np
    w_in = a["w_in"][0]
    stream = np.zeros((N_TILES, P, 1024), np.float32)

    def by_columns(w, cols, first):
        n = len(cols) // P
        t = w[:, cols].reshape(KT, P, n, P)
        stream[first:first + n] = t.transpose(2, 1, 0, 3).reshape(n, P, 1024)

    z0, b0, d0, q0, kv0, g0, m0 = 1536, 2048, 2056, 2064, 2576, 3344, 3368
    ar = np.arange
    by_columns(w_in, ar(0, 1536), T_GDN)
    v_cols = [ar(kv0 + ((b * 2 + 1) * 2) * DH, kv0 + ((b * 2 + 1) * 2) * DH + P) for b in (1, 2)]
    tok = np.concatenate([ar(z0, z0 + 512), ar(b0, b0 + 8), ar(g0, g0 + 24), ar(d0, d0 + 8)] + v_cols)
    stream[T_TOK:T_TOK + KT, :, 0:len(tok)] = w_in[:, tok].reshape(KT, P, len(tok))
    q_cols = [ar(q0 + h * DH, q0 + (h + 1) * DH) for m in range(4) for h in (m, m + 4)]
    k_cols = [ar(kv0 + (b * 2 * 2) * DH, kv0 + (b * 2 * 2) * DH + P) for b in range(3)]
    by_columns(w_in, np.concatenate(q_cols + k_cols + [ar(kv0 + 2 * DH, kv0 + 4 * DH)]), T_NSA)
    by_columns(w_in, ar(m0, m0 + 2048), T_MERGE)
    for s, name in enumerate(("cmp_w_k", "cmp_w_v")):
        w = a[name][0].transpose(1, 0, 2).reshape(DH, 2, 1024).transpose(1, 0, 2)
        stream[T_CMP + 2 * s:T_CMP + 2 * s + 2] = np.concatenate([w, w], axis=1)
    for s, name in enumerate(("w_branch_b", "w_branch_a")):
        w = a[name][0].reshape(HP, P, N_AB // 2, 2, P).transpose(2, 1, 3, 0, 4).reshape(N_AB // 2, P, 1024)
        stream[T_AB + N_AB // 2 * s:T_AB + N_AB // 2 * (s + 1)] = w
    stream[T_OUT:T_OUT + N_OUT] = a["w_out"][0].reshape(N_OUT, P, D)
    by_columns(a["w_query"][0], ar(2048), T_WQ)
    sk = a["sub_keys"][0].reshape(N_SK, 8, P, P).transpose(0, 3, 1, 2).reshape(N_SK, P, 1024)
    stream[T_SK:T_SK + N_SK] = sk
    u = a["expert_u"][0].reshape(NKEYS, NKEYS, KT, P)
    stream[T_U:T_U + NKEYS] = u.transpose(1, 3, 2, 0).reshape(NKEYS, P, 1024)
    stream[T_V:T_V + NKEYS] = a["expert_v"][0].reshape(NKEYS, NKEYS, D).transpose(1, 0, 2)

    par = np.zeros((P, N_PAR), np.float32)
    par[:, R_NM:R_NM + 8] = a["norm_mix"][0].reshape(8, P).T
    par[:, R_NF:R_NF + 8] = a["norm_ffn"][0].reshape(8, P).T
    par[:, R_CW:R_CW + 48] = a["conv_w"][0].reshape(4, 12, P).transpose(2, 1, 0).reshape(P, 48)
    for s, name in enumerate(("cmp_pe_k", "cmp_pe_v")):
        pe = a[name][0].T
        par[:, R_PE + 32 * s:R_PE + 32 * s + 32] = np.concatenate([pe, pe], axis=0)
    par[:, R_ALOG:R_ALOG + 8] = a["a_log"][0][None, :]
    par[:, R_DT:R_DT + 8] = a["dt_bias"][0][None, :]
    par[:, R_GN:R_GN + DH] = a["gdn_norm"][0][None, :]
    relb = np.concatenate([a["rel_bias"], np.full((1, H), NEG, np.float32)], axis=0)
    consts, onehot = _constants()
    return {"x": a["x"][0], "stream": stream, "consts": consts, "params": par, "onehot": onehot,
            "relb": relb, "nfinal": a["norm_final"]}


def kernel(**inputs):
    import numpy as np
    import concourse.bacc as bacc
    from concourse.bass_utils import run_bass_kernel_spmd
    arrays = _layout({k: np.asarray(v) for k, v in inputs.items()})
    nc = bacc.Bacc("TRN2", target_bir_lowering=False, num_devices=1)
    aps = {k: nc.dram_tensor("in_" + k, v.shape, F32, kind="ExternalInput").ap() for k, v in arrays.items()}
    out = nc.dram_tensor("out", (T, D), F32, kind="ExternalOutput").ap()
    scratch = nc.dram_tensor("bias_scratch", (H, N_E1), F32, kind="Internal").ap()
    build(nc, bias_scratch=scratch, out=out, **aps)
    r = run_bass_kernel_spmd(nc, [{"in_" + k: np.ascontiguousarray(v) for k, v in arrays.items()}], core_ids=[0])
    return r.results[0]["out"].reshape(1, T, D)
```
